# Optimizing a Trainium2 kernel written in Bass

```python
import jax, jax.numpy as jnp
from jax import lax
import numpy as np

D_MODEL = 1024
BATCH = 1
SEQ = 2048
DEPTH = 1
DEC_BATCH = 1
DEC_SEQ = 32
PAST_LEN = 1024

CHUNK = 64
D_MIX = D_MODEL
C_CONV = D_MIX // 2
N_HEADS = 8
HEAD_DIM = (D_MIX - C_CONV) // N_HEADS
D_ATTN = N_HEADS * HEAD_DIM
D_IN = 2 * C_CONV + 3 * D_ATTN
CONV_W = 31
Q_BLOCK = 128
N_GROUPS = 4
EXPERTS_PER_GROUP = 8
N_EXPERTS = N_GROUPS * EXPERTS_PER_GROUP
TOP_K = 2
D_EXPERT = D_MODEL // 2
ROW_BLOCK = 128
EPS = 1e-6

kernel_name = "hymba_conformer_stickbreak_hmoe_stream"

def rms_norm(x, g):
    xf = x.astype(jnp.float32)
    y = xf * lax.rsqrt(jnp.mean(xf * xf, axis=-1, keepdims=True) + EPS)
    return (y * g.astype(jnp.float32)).astype(x.dtype)

def layer_norm(x, g, b):
    xf = x.astype(jnp.float32)
    mu = jnp.mean(xf, axis=-1, keepdims=True)
    xc = xf - mu
    y = xc * lax.rsqrt(jnp.mean(xc * xc, axis=-1, keepdims=True) + EPS)
    return (y * g.astype(jnp.float32) + b.astype(jnp.float32)).astype(x.dtype)

def stick_breaking_block(q, k, v, q_pos, k_pos):
    z = jnp.einsum('bqhd,bkhd->bhqk', q, k).astype(jnp.float32) * (HEAD_DIM ** -0.5)
    valid = k_pos[None, :] < q_pos[:, None]
    log_keep = jnp.where(valid, jax.nn.log_sigmoid(-z), 0.0)
    later = lax.cumsum(log_keep, axis=3, reverse=True) - log_keep
    a = jnp.where(valid, jnp.exp(jax.nn.log_sigmoid(z) + later), 0.0)
    return jnp.einsum('bhqk,bkhd->bqhd', a.astype(v.dtype), v)

def stick_breaking_attention(q, k_all, v_all, past_len):
    S = q.shape[1]
    outs = []
    for blk in range(-(-S // Q_BLOCK)):
        lo = blk * Q_BLOCK
        hi = min(lo + Q_BLOCK, S)
        kend = past_len + hi
        outs.append(stick_breaking_block(q[:, lo:hi], k_all[:, :kend], v_all[:, :kend],
                                         past_len + jnp.arange(lo, hi), jnp.arange(kend)))
    return jnp.concatenate(outs, axis=1)

def hierarchical_moe(h, w_rg, w_re, w_g, w_u, w_d):
    T = h.shape[0]
    lg = (h @ w_rg).astype(jnp.float32)
    p_group = jax.nn.softmax(lg, axis=-1)
    g_idx = jnp.argmax(lg, axis=-1)
    p_sel = jnp.take_along_axis(p_group, g_idx[:, None], axis=1)[:, 0]
    le = (h @ w_re).astype(jnp.float32).reshape(T, N_GROUPS, EXPERTS_PER_GROUP)
    le = jnp.take_along_axis(le, g_idx[:, None, None], axis=1)[:, 0]
    top_v, top_i = lax.top_k(le, TOP_K)
    combine = p_sel[:, None] * jax.nn.softmax(top_v, axis=-1)
    expert_id = g_idx[:, None] * EXPERTS_PER_GROUP + top_i

    A = T * TOP_K
    flat_e = expert_id.reshape(A).astype(jnp.int32)
    flat_tok = jnp.repeat(jnp.arange(T, dtype=jnp.int32), TOP_K)
    flat_w = combine.reshape(A)
    order = jnp.argsort(flat_e)
    sorted_e = flat_e[order]
    counts = jnp.bincount(flat_e, length=N_EXPERTS)
    start = jnp.cumsum(counts) - counts
    padded = (counts + ROW_BLOCK - 1) // ROW_BLOCK * ROW_BLOCK
    padded_end = jnp.cumsum(padded)
    padded_start = padded_end - padded
    dest = padded_start[sorted_e] + jnp.arange(A, dtype=jnp.int32) - start[sorted_e]
    n_blocks = -(-(A + N_EXPERTS * (ROW_BLOCK - 1)) // ROW_BLOCK)
    P = n_blocks * ROW_BLOCK
    row_tok = jnp.full((P,), T, jnp.int32).at[dest].set(flat_tok[order])
    row_w = jnp.zeros((P,), jnp.float32).at[dest].set(flat_w[order])
    block_e = jnp.minimum(
        jnp.sum(jnp.arange(n_blocks)[:, None] * ROW_BLOCK >= padded_end[None, :], axis=1),
        N_EXPERTS - 1)
    h_pad = jnp.concatenate([h, jnp.zeros((1, h.shape[1]), h.dtype)], axis=0)
    xb = h_pad[row_tok].reshape(n_blocks, ROW_BLOCK, h.shape[1])

    def expert_block(args):
        xe, e = args
        return (jax.nn.silu(xe @ w_g[e]) * (xe @ w_u[e])) @ w_d[e]

    yb = lax.map(expert_block, (xb, block_e))
    out = jnp.zeros((T + 1, h.shape[1]), jnp.float32).at[row_tok].add(
        yb.reshape(P, h.shape[1]).astype(jnp.float32) * row_w[:, None])
    return out[:T].astype(h.dtype)

def trunk_layer(x, conv_hist, k_past, v_past, norm_mix_g, w_in, conv_w, conv_b, conv_ln_g,
                conv_ln_b, q_norm_g, k_norm_g, attn_out_g, w_out, norm_ffn_g,
                w_router_group, w_router_expert, w_exp_gate, w_exp_up, w_exp_down):
    B, S, _ = x.shape
    past_len = k_past.shape[1]
    h = rms_norm(x, norm_mix_g)
    proj = h @ w_in
    a, gate, q, k, v = jnp.split(
        proj, [C_CONV, 2 * C_CONV, 2 * C_CONV + D_ATTN, 2 * C_CONV + 2 * D_ATTN], axis=-1)

    u = a * jax.nn.sigmoid(gate)
    u_full = jnp.concatenate([conv_hist, u], axis=1)
    c = lax.conv_general_dilated(u_full, conv_w[:, None, :], (1,), 'VALID',
                                 dimension_numbers=('NWC', 'WIO', 'NWC'),
                                 feature_group_count=C_CONV) + conv_b
    c = jax.nn.silu(layer_norm(c, conv_ln_g, conv_ln_b))
    conv_state = u_full[:, -(CONV_W - 1):]

    q = rms_norm(q.reshape(B, S, N_HEADS, HEAD_DIM), q_norm_g)
    k = rms_norm(k.reshape(B, S, N_HEADS, HEAD_DIM), k_norm_g)
    v = v.reshape(B, S, N_HEADS, HEAD_DIM)
    k_all = jnp.concatenate([k_past, k], axis=1)
    v_all = jnp.concatenate([v_past, v], axis=1)
    o = stick_breaking_attention(q, k_all, v_all, past_len)
    o = rms_norm(o, attn_out_g).reshape(B, S, D_ATTN)

    x = x + jnp.concatenate([c, o], axis=-1) @ w_out
    h2 = rms_norm(x, norm_ffn_g).reshape(B * S, D_MODEL)
    x = x + hierarchical_moe(h2, w_router_group, w_router_expert,
                             w_exp_gate, w_exp_up, w_exp_down).reshape(B, S, D_MODEL)
    return x, k, v, conv_state

def setup_inputs(seed: int = 0) -> dict:
    key = jax.random.key(seed)
    ks = jax.random.split(key, 24)
    f32 = jnp.float32
    nrm = lambda k, shape, s: jax.random.normal(k, shape, f32) * s
    L = DEPTH
    return {
        "x_prompt": nrm(ks[0], (BATCH, SEQ, D_MODEL), 1.0),
        "x_sample": nrm(ks[1], (DEC_BATCH, DEC_SEQ, D_MODEL), 1.0),
        "cache_k": nrm(ks[2], (L, DEC_BATCH, PAST_LEN, N_HEADS, HEAD_DIM), 1.0),
        "cache_v": nrm(ks[3], (L, DEC_BATCH, PAST_LEN, N_HEADS, HEAD_DIM), 1.0),
        "cache_conv": nrm(ks[4], (L, DEC_BATCH, CONV_W - 1, C_CONV), 0.5),
        "norm_mix_g": 1.0 + nrm(ks[5], (L, D_MODEL), 0.02),
        "w_in": nrm(ks[6], (L, D_MODEL, D_IN), D_MODEL ** -0.5),
        "conv_w": nrm(ks[7], (L, CONV_W, C_CONV), CONV_W ** -0.5),
        "conv_b": nrm(ks[8], (L, C_CONV), 0.02),
        "conv_ln_g": 1.0 + nrm(ks[9], (L, C_CONV), 0.02),
        "conv_ln_b": nrm(ks[10], (L, C_CONV), 0.02),
        "q_norm_g": 1.0 + nrm(ks[11], (L, HEAD_DIM), 0.02),
        "k_norm_g": 1.0 + nrm(ks[12], (L, HEAD_DIM), 0.02),
        "attn_out_g": 1.0 + nrm(ks[13], (L, N_HEADS, HEAD_DIM), 0.02),
        "w_out": nrm(ks[14], (L, D_MIX, D_MODEL), D_MIX ** -0.5),
        "norm_ffn_g": 1.0 + nrm(ks[15], (L, D_MODEL), 0.02),
        "w_router_group": nrm(ks[16], (L, D_MODEL, N_GROUPS), D_MODEL ** -0.5),
        "w_router_expert": nrm(ks[17], (L, D_MODEL, N_EXPERTS), D_MODEL ** -0.5),
        "w_exp_gate": nrm(ks[18], (L, N_EXPERTS, D_MODEL, D_EXPERT), D_MODEL ** -0.5),
        "w_exp_up": nrm(ks[19], (L, N_EXPERTS, D_MODEL, D_EXPERT), D_MODEL ** -0.5),
        "w_exp_down": nrm(ks[20], (L, N_EXPERTS, D_EXPERT, D_MODEL), D_EXPERT ** -0.5),
    }

def reference(x_prompt, x_sample, cache_k, cache_v, cache_conv, norm_mix_g, w_in, conv_w,
              conv_b, conv_ln_g, conv_ln_b, q_norm_g, k_norm_g, attn_out_g, w_out, norm_ffn_g,
              w_router_group, w_router_expert, w_exp_gate, w_exp_up, w_exp_down):
    yp, ys = x_prompt, x_sample
    bp = x_prompt.shape[0]
    kp, vp, cp, ksl, vsl, csl = [], [], [], [], [], []
    for l in range(DEPTH):
        w = (norm_mix_g[l], w_in[l], conv_w[l], conv_b[l], conv_ln_g[l], conv_ln_b[l],
             q_norm_g[l], k_norm_g[l], attn_out_g[l], w_out[l], norm_ffn_g[l],
             w_router_group[l], w_router_expert[l], w_exp_gate[l], w_exp_up[l], w_exp_down[l])
        yp, k1, v1, c1 = trunk_layer(
            yp, jnp.zeros((bp, CONV_W - 1, C_CONV), x_prompt.dtype),
            jnp.zeros((bp, 0, N_HEADS, HEAD_DIM), x_prompt.dtype),
            jnp.zeros((bp, 0, N_HEADS, HEAD_DIM), x_prompt.dtype), *w)
        ys, k2, v2, c2 = trunk_layer(ys, cache_conv[l], cache_k[l], cache_v[l], *w)
        kp.append(k1); vp.append(v1); cp.append(c1)
        ksl.append(k2); vsl.append(v2); csl.append(c2)
    return (yp, ys, jnp.stack(kp), jnp.stack(vp), jnp.stack(cp),
            jnp.stack(ksl), jnp.stack(vsl), jnp.stack(csl))


_drawn_inputs = setup_inputs


def setup_inputs(seed=0):
    import zlib

    import numpy as np

    out = dict(_drawn_inputs(seed))
    spreads = {}
    factors = {'conv_ln_g': 3.51,
     'q_norm_g': 12.837,
     'k_norm_g': 9.733,
     'conv_ln_b': 5.888,
     'attn_out_g': 4.981,
     'norm_ffn_g': 3.393}
    for name, (base, spread) in spreads.items():
        noise = np.random.default_rng([zlib.crc32(name.encode()), seed]).standard_normal(out[name].shape)
        drawn = base * np.exp(spread * noise) if base else spread * noise
        out[name] = __import__('jax').numpy.asarray(drawn.astype(out[name].dtype))
    for name, factor in factors.items():
        out[name] = (out[name] * factor).astype(out[name].dtype)
    return out
```

```python
from contextlib import ExitStack

import concourse.bass as bass
from concourse import mybir

F32 = mybir.dt.float32
F32R = mybir.dt.float32r
I32 = mybir.dt.int32
ALU = mybir.AluOpType
ACT = mybir.ActivationFunctionType
AX = mybir.AxisListType

P = 128
D = 1024
KT = D // P
C = 512
CT = C // P
NH, HD = 8, 64
W = 31
HIST = W - 1
SEQ, DEC, PAST = 2048, 32, 1024
PT = SEQ // P
NT = PT + 1
TOK = SEQ + DEC
ROWS = (NT + 1) * P
NR = 36
NCH = 5
EPS = 1e-6
SCRATCH = "Internal"
CHUNKS = [1, 0, 2, 3, 4]


def tiles(eng, body):
    body(0, 0)
    body(1, 1)
    with eng.Fori(1, PT // 2) as i:
        body(i * 2, 0)
        body(i * 2 + 1, 1)
    body(PT, 0)


def first(t, n):
    return isinstance(t, int) and t < n


def hold(eng, signal, value, passed):
    eng.wait_ge(signal, value)
    if not isinstance(value, int):
        eng.sem_inc(passed, 1)


def phase_project(nc, io, scr):
    with ExitStack() as ctx:
        def sb(name, shape, dt=F32):
            return ctx.enter_context(nc.sbuf_tensor("p1_" + name, shape, dt))

        def ps(name, shape):
            return ctx.enter_context(nc.psum_tensor("p1_" + name, shape, F32))

        sems = []

        def sem(name):
            sems.append(nc.alloc_semaphore("p1_" + name))
            return sems[-1]

        w_hi = sb("w_hi", [P, KT, NCH * C], F32R)
        w_lo = sb("w_lo", [P, KT, NCH * C], F32R)
        RAW = 4
        w_raw = sb("w_raw", [P, RAW, C])
        conv = w_raw[:, 0, :].rearrange("p (a t) -> p a t", a=CT)
        normed, sig, swish = w_raw[:, 1, :], w_raw[:, 2, :], w_raw[:, 3, :]
        x_sb = sb("x", [P, 2, D])
        xt_hi = sb("xt_hi", [P, 2, KT, P], F32R)
        xt_lo = sb("xt_lo", [P, 2, KT, P], F32R)
        u = sb("u", [P, C])
        tmp = sb("tmp", [P, C])
        q_sb, k_sb, v_sb = sb("q", [P, C]), sb("k", [P, C]), sb("v", [P, C])
        ut = sb("ut", [P, CT, HIST + P])
        ident = sb("ident", [P, P])
        gcol = sb("gcol", [P, KT])
        gk = sb("gk", [P, HD])
        cw = sb("cw", [P, CT, W])
        cb, lng, lnb = sb("cb", [P, CT]), sb("lng", [P, CT]), sb("lnb", [P, CT])
        prod = sb("prod", [P, 2, P])
        st = sb("st", [P, 64])
        ss, rstd, rs2 = st[:, 0:2], st[:, 2:4], st[:, 4:6]
        rtmp = st[:, 6:7]
        msq, msk = st[:, 8:16], st[:, 16:24]
        rq, rk = st[:, 24:32], st[:, 32:40]
        bnst, mv, lnr, lnm = st[:, 40:46], st[:, 46:48], st[:, 48:49], st[:, 49:50]
        rqt = st[:, 50:58]
        mhalf = sb("mhalf", [P, NH])
        cached = x_sb[:, 1, 0:C]

        pj = ps("pj", [P, NCH, C])
        pxt = ps("pxt", [P, KT, P])
        pm = ps("pm", [P, C])

        ident_done, const_dma = sem("ident_done"), sem("const_dma")
        x_in = [sem("x_in0"), sem("x_in1")]
        piece_in = [sem(f"piece_in{i}") for i in range(RAW)]
        w_hi_done, w_lo_done = sem("w_hi_done"), sem("w_lo_done")
        xt_ps, xt_hi_done, xt_lo_done = sem("xt_ps"), sem("xt_hi_done"), sem("xt_lo_done")
        sq_done, rstd_step, rstd_done = sem("sq_done"), sem("rstd_step"), sem("rstd_done")
        pj_done = sem("pj_done")
        sg_done, tmp_read = sem("sg_done"), sem("tmp_read")
        u_done, ut_ps, ut_done, hist_done = sem("u_done"), sem("ut_ps"), sem("ut_done"), sem("hist_done")
        ms_done, r_step, r_done = sem("ms_done"), sem("r_step"), sem("r_done")
        qk_done, kg_done, v_done = sem("qk_done"), sem("kg_done"), sem("v_done")
        tap_dve, tap_pool = sem("tap_dve"), sem("tap_pool")
        ln1_ps, ln_stat, ln_step, ln_rs = sem("ln1_ps"), sem("ln_stat"), sem("ln_step"), sem("ln_rs")
        normed_done, ln2_ps, act_ln, swish_done = sem("normed_done"), sem("ln2_ps"), sem("act_ln"), sem("swish_done")
        st_q, st_k, st_v, st_c, st_u = sem("st_q"), sem("st_k"), sem("st_v"), sem("st_c"), sem("st_u")
        passed, passed_dve = sem("passed"), sem("passed_dve")
        cached_in, cached_ps = sem("cached_in"), sem("cached_ps")

        DVE_CT = [0, 1, 2]
        POOL_CT = 3
        ND = W * len(DVE_CT)
        NP = 2 * W - 1
        NPIECE = NCH * KT
        NCONST = 6
        pieces = [(c, k) for c in CHUNKS for k in range(KT)]

        block = ctx.enter_context(nc.Block())

        @block.sync
        def _(sp):
            sp.dma_start(gcol[:, :], io["norm_mix_g"]).then_inc(const_dma, 16)
            sp.dma_start(x_sb[:, 0, :], io["x"][0:P, :]).then_inc(x_in[0], 16)
            sp.dma_start(gk[:, :], io["k_norm_g"].partition_broadcast(P)).then_inc(const_dma, 16)
            sp.dma_start(cw[:, :, :], io["conv_w"]).then_inc(const_dma, 16)
            sp.dma_start(cb[:, :], io["conv_b"]).then_inc(const_dma, 16)
            sp.dma_start(lng[:, :], io["conv_ln_g"]).then_inc(const_dma, 16)
            sp.dma_start(lnb[:, :], io["conv_ln_b"]).then_inc(const_dma, 16)
            for n, (c, k) in enumerate(pieces):
                if n >= RAW:
                    sp.wait_ge(w_lo_done, n - RAW + 1)
                sp.dma_start(w_raw[:, n % RAW, :],
                             io["w_in"][k * P:(k + 1) * P, c * C:(c + 1) * C]).then_inc(piece_in[n % RAW], 16)
                if n == KT:
                    sp.dma_start(x_sb[:, 1, :], io["x"][P:2 * P, :]).then_inc(x_in[1], 16)

            def store_swish(t):
                sp.wait_ge(swish_done, t + 1)
                sp.dma_start(scr["c"][:, :, bass.ts(t, P)],
                             swish.rearrange("p (a t) -> p a t", a=CT)).then_inc(st_c, 16)

            def body(t, b):
                if isinstance(t, int) and t == PT:
                    sp.wait_ge(x_in[1], 8 * PT + 16)
                    sp.dma_start(cached[0:HIST, :], io["cache_conv"]).then_inc(cached_in, 16)
                else:
                    sp.wait_ge(sq_done, t + 1)
                    sp.dma_start(x_sb[:, b, :], io["x"][bass.ts(t + 2, P), :]).then_inc(x_in[b], 16)
                if not first(t, 2):
                    store_swish(t - 2)
                sp.wait_ge(u_done, t + 1)
                sp.dma_start(io["u_out"][bass.ts(t, P), :], u[:, :]).then_inc(st_u, 16)
                sp.wait_ge(qk_done, 2 * t + 1)
                sp.dma_start(scr["q"][bass.ts(t, P), :], q_sb[:, :]).then_inc(st_q, 16)
                sp.wait_ge(kg_done, t + 1)
                sp.dma_start(io["k_out"][bass.ts(t, P), :], k_sb[:, :]).then_inc(st_k, 16)
                sp.wait_ge(v_done, t + 1)
                sp.dma_start(io["v_out"][bass.ts(t, P), :], v_sb[:, :]).then_inc(st_v, 16)

            tiles(sp, body)
            store_swish(PT - 1)
            store_swish(PT)
            for s in (st_q, st_k, st_v, st_c, st_u):
                sp.wait_ge(s, 16 * NT)

        @block.tensor
        def _(pe):
            def transpose_x(t, b):
                pe.wait_ge(x_in[b], (t - b) * 8 + 16)
                if not first(t, 1):
                    pe.wait_ge(xt_lo_done, t)
                for k in range(KT):
                    last = pe.transpose(pxt[:, k, :], x_sb[:, b, k * P:(k + 1) * P], ident[:, :])
                last.then_inc(xt_ps, 1)

            def project(t, b, i):
                c = CHUNKS[i]
                if i == 0:
                    pe.wait_ge(xt_lo_done, t + 1)
                    pe.wait_ge(xt_hi_done, t + 1)
                if first(t, 1):
                    pe.wait_ge(w_lo_done, KT * (i + 1))
                    pe.wait_ge(w_hi_done, KT * (i + 1))
                elif c < 2:
                    pe.wait_ge(u_done, t)
                elif c < 4:
                    pe.wait_ge(qk_done, 2 * t - 3 + c)
                else:
                    pe.wait_ge(v_done, t)
                n = 0
                for k in range(KT):
                    for xa, wa in ((xt_hi, w_hi), (xt_hi, w_lo), (xt_lo, w_hi)):
                        last = pe.matmul(pj[:, c, :], xa[:, b, k, :], wa[:, k, c * C:(c + 1) * C],
                                         start=(n == 0), stop=(n == 3 * KT - 1))
                        n += 1
                last.then_inc(pj_done, 1)

            def four(src, done):
                for a in range(CT):
                    last = pe.transpose(pm[:, a * P:(a + 1) * P], src(a), ident[:, :])
                last.then_inc(done, 1)

            def ln1(t):
                pe.wait_ge(tap_dve, (t + 1) * ND)
                pe.wait_ge(tap_pool, (t + 1) * NP)
                if isinstance(t, int) and t == PT:
                    pe.wait_ge(act_ln, PT)
                else:
                    pe.wait_ge(ut_done, t + 2)
                four(lambda a: conv[:, a, :], ln1_ps)

            def ln2(t):
                pe.wait_ge(normed_done, t + 1)
                four(lambda a: normed[:, a * P:(a + 1) * P], ln2_ps)

            def ut_transpose(t):
                pe.wait_ge(u_done, t + 1)
                if not first(t, 2):
                    pe.wait_ge(act_ln, t - 1)
                if not first(t, 1):
                    pe.wait_ge(hist_done, t + 1)
                four(lambda a: u[:, a * P:(a + 1) * P], ut_ps)

            pe.wait_ge(ident_done, 3)
            transpose_x(0, 0)

            def body(t, b):
                sample = isinstance(t, int) and t == PT
                project(t, b, 0)
                if not first(t, 2):
                    ln2(t - 2)
                project(t, b, 1)
                if sample:
                    pe.wait_ge(cached_in, 16)
                    pe.wait_ge(act_ln, t - 1)
                    for a in range(CT):
                        last = pe.transpose(pm[:, a * P:a * P + HIST], cached[0:HIST, a * P:(a + 1) * P],
                                            ident[0:HIST, 0:HIST])
                    last.then_inc(cached_ps, 1)
                else:
                    transpose_x(t + 1, 1 - b)
                project(t, b, 2)
                project(t, b, 3)
                ut_transpose(t)
                project(t, b, 4)
                if not first(t, 1):
                    ln1(t - 1)

            tiles(pe, body)
            ln2(PT - 1)
            ln1(PT)
            ln2(PT)

        @block.scalar
        def _(act):
            act.wait_ge(const_dma, 16 * NCONST)

            def x_parts(t, b):
                act.wait_ge(xt_ps, t + 1)
                if not first(t, 2):
                    act.wait_ge(pj_done, 5 * t - 5)
                    act.wait_ge(rstd_done, t - 1)
                act.activation(xt_hi[:, b, :, :], pxt[:, :, :], ACT.Copy).then_inc(xt_hi_done, 1)
                act.activation(x_sb[:, b, :], x_sb[:, b, :], ACT.Square,
                               accum_out=ss[:, b:b + 1]).then_inc(sq_done, 1)

            for n, (c, k) in enumerate(pieces):
                act.wait_ge(piece_in[n % RAW], 16 * (n // RAW + 1))
                act.activation(w_hi[:, k, c * C:(c + 1) * C], w_raw[:, n % RAW, :], ACT.Copy,
                               scale=gcol[:, k:k + 1]).then_inc(w_hi_done, 1)
                if n == 1:
                    x_parts(0, 0)

            def ln_norm(t):
                act.wait_ge(ln_rs, t + 1)
                if not first(t, 1):
                    act.wait_ge(ln2_ps, t)
                act.activation(normed, pm[:, :], ACT.Identity, scale=lnr, bias=lnm).then_inc(normed_done, 1)

            def ln_out(t):
                act.wait_ge(ln2_ps, t + 1)
                if not first(t, 1):
                    act.wait_ge(st_c, 16 * t)
                for a in range(CT):
                    act.activation(sig[:, a * P:(a + 1) * P], pm[:, a * P:(a + 1) * P], ACT.Sigmoid,
                                   scale=lng[:, a:a + 1], bias=lnb[:, a:a + 1])
                    last = act.activation(swish[:, a * P:(a + 1) * P], pm[:, a * P:(a + 1) * P], ACT.Identity,
                                          scale=lng[:, a:a + 1], bias=lnb[:, a:a + 1])
                last.then_inc(act_ln, 1)

            def body(t, b):
                sample = isinstance(t, int) and t == PT
                act.wait_ge(pj_done, 5 * t + 1)
                act.wait_ge(rstd_done, t + 1)
                if not first(t, 1):
                    act.wait_ge(tmp_read, 3 * t)
                act.activation(tmp[:, :], pj[:, 1, :], ACT.Sigmoid, scale=rstd[:, b:b + 1]).then_inc(sg_done, 1)
                if not first(t, 2):
                    ln_out(t - 2)
                if not sample:
                    x_parts(t + 1, 1 - b)
                act.wait_ge(pj_done, 5 * t + 3)
                act.wait_ge(tmp_read, 3 * t + 1)
                act.activation(tmp[:, :], pj[:, 2, :], ACT.Square).then_inc(sg_done, 1)
                if not first(t, 1):
                    act.wait_ge(tap_dve, t * ND)
                    act.wait_ge(tap_pool, t * NP)
                    if sample:
                        act.wait_ge(cached_ps, 1)
                        act.activation(ut[:, :, 0:HIST],
                                       pm[:, :].rearrange("p (a t) -> p a t", a=CT)[:, :, 0:HIST],
                                       ACT.Copy).then_inc(hist_done, 1)
                    else:
                        act.activation(ut[:, :, 0:HIST], ut[:, :, P:P + HIST], ACT.Copy).then_inc(hist_done, 1)
                act.wait_ge(hist_done, t + 1)
                act.wait_ge(ut_ps, t + 1)
                act.activation(ut[:, :, HIST:HIST + P], pm[:, :].rearrange("p (a t) -> p a t", a=CT),
                               ACT.Copy).then_inc(ut_done, 1)
                act.wait_ge(pj_done, 5 * t + 4)
                act.wait_ge(tmp_read, 3 * t + 2)
                act.activation(tmp[:, :], pj[:, 3, :], ACT.Square).then_inc(sg_done, 1)
                act.wait_ge(pj_done, 5 * t + 5)
                if not first(t, 1):
                    act.wait_ge(st_v, 16 * t)
                act.activation(v_sb[:, :], pj[:, 4, :], ACT.Copy, scale=rstd[:, b:b + 1]).then_inc(v_done, 1)
                if not first(t, 1):
                    ln_norm(t - 1)

            tiles(act, body)
            ln_out(PT - 1)
            ln_norm(PT)
            ln_out(PT)

        @block.vector
        def _(dve):
            def x_rest(t, b):
                dve.wait_ge(xt_hi_done, t + 1)
                dve.tensor_tensor(xt_lo[:, b, :, :], pxt[:, :, :], xt_hi[:, b, :, :].bitcast(F32),
                                  ALU.subtract).then_inc(xt_lo_done, 1)

            dve.wait_ge(const_dma, 16 * NCONST)
            for n, (c, k) in enumerate(pieces):
                dve.wait_ge(w_hi_done, n + 1)
                dve.scalar_tensor_tensor(w_lo[:, k, c * C:(c + 1) * C], w_raw[:, n % RAW, :], gcol[:, k:k + 1],
                                         w_hi[:, k, c * C:(c + 1) * C].bitcast(F32), ALU.mult,
                                         ALU.subtract).then_inc(w_lo_done, 1)
                if n == 1:
                    x_rest(0, 0)

            def taps(t, lo, hi):
                if lo == 0:
                    dve.wait_ge(ut_done, t + 1)
                    if first(t, 1):
                        dve.wait_ge(w_lo_done, NPIECE)
                    else:
                        dve.wait_ge(ln1_ps, t)
                for j in range(lo, hi):
                    for n, a in enumerate(DVE_CT):
                        if j == 0:
                            dve.tensor_scalar(conv[:, a, :], ut[:, a, 0:P], cw[:, a, 0:1], cb[:, a:a + 1],
                                              ALU.mult, ALU.add).then_inc(tap_dve, 1)
                        else:
                            dve.wait_ge(tap_dve, t * ND + len(DVE_CT) * (j - 1) + n + 1)
                            dve.scalar_tensor_tensor(conv[:, a, :], ut[:, a, j:j + P], cw[:, a, j:j + 1],
                                                     conv[:, a, :], ALU.mult, ALU.add).then_inc(tap_dve, 1)

            def heads(ap):
                return ap.rearrange("p (h d) -> p h d", h=NH)

            def ln_stats(t):
                dve.wait_ge(ln1_ps, t + 1)
                if not first(t, 1):
                    dve.wait_ge(ln_rs, t)
                dve.bn_stats(bnst, pm[:, :]).then_inc(ln_stat, 1)
                hold(dve, ln_stat, 2 * t + 1, passed_dve)
                dve.bn_aggr(mv, bnst).then_inc(ln_stat, 1)

            def body(t, b):
                sample = isinstance(t, int) and t == PT
                if not first(t, 1):
                    taps(t - 1, 0, 10)
                dve.wait_ge(pj_done, 5 * t + 2)
                dve.wait_ge(sg_done, 3 * t + 1)
                if not first(t, 1):
                    dve.wait_ge(ut_ps, t)
                    dve.wait_ge(st_u, 16 * t)
                dve.scalar_tensor_tensor(u[:, :], pj[:, 0, :], rstd[:, b:b + 1], tmp[:, :],
                                         ALU.mult, ALU.mult).then_inc(u_done, 1)
                dve.wait_ge(u_done, t + 1)
                dve.sem_inc(tmp_read, 1)
                if not sample:
                    x_rest(t + 1, 1 - b)
                if not first(t, 1):
                    taps(t - 1, 10, 21)
                for n, (c, ms, r, dst) in enumerate(((2, msq, rq, q_sb), (3, msk, rk, k_sb))):
                    dve.wait_ge(sg_done, 3 * t + 2 + n)
                    if not first(t, 1):
                        dve.wait_ge(r_done, 2 * t - 1 + n)
                    dve.tensor_reduce(ms, heads(tmp[:, :]), AX.X, ALU.add).then_inc(ms_done, 1)
                    dve.wait_ge(ms_done, 2 * t + n + 1)
                    dve.sem_inc(tmp_read, 1)
                    dve.wait_ge(r_done, 2 * t + n + 1)
                    if not first(t, 1):
                        dve.wait_ge(st_q if n == 0 else st_k, 16 * t)
                    dve.tensor_tensor(heads(dst[:, :]), heads(pj[:, c, :]),
                                      r.unsqueeze(2).broadcast_to([P, NH, HD]), ALU.mult).then_inc(qk_done, 1)
                    if n == 0 and not first(t, 1):
                        taps(t - 1, 21, W)
                if not first(t, 1):
                    ln_stats(t - 1)

            tiles(dve, body)
            taps(PT, 0, W)
            ln_stats(PT)

        @block.gpsimd
        def _(pool):
            pool.memset(ident[:, :], 0.0).then_inc(ident_done, 1)
            pool.memset(mhalf[:, :], -0.5).then_inc(ident_done, 1)
            hold(pool, ident_done, 1, passed)
            pool.affine_select(out=ident[:, :], in_=ident[:, :], compare_op=ALU.not_equal, fill=1.0, base=0,
                               pattern=[[-1, P]], channel_multiplier=1).then_inc(ident_done, 1)
            pool.memset(ut[:, :, 0:HIST], 0.0).then_inc(hist_done, 1)
            hold(pool, const_dma, 16 * NCONST, passed)
            hold(pool, ident_done, 3, passed)

            def inverse_rms(t, b):
                hold(pool, sq_done, t + 1, passed)
                if not first(t, 2):
                    hold(pool, v_done, t - 1, passed)
                    hold(pool, u_done, t - 1, passed)
                pool.tensor_scalar(rtmp, ss[:, b:b + 1], 1.0 / D, EPS, ALU.mult, ALU.add).then_inc(rstd_step, 1)
                hold(pool, rstd_step, 2 * t + 1, passed)
                pool.tensor_tensor(rstd[:, b:b + 1], rtmp, mhalf[:, 0:1], ALU.pow).then_inc(rstd_step, 1)
                hold(pool, rstd_step, 2 * t + 2, passed)
                pool.tensor_scalar(rs2[:, b:b + 1], rstd[:, b:b + 1], rstd[:, b:b + 1], 1.0 / HD,
                                   ALU.mult, ALU.mult).then_inc(rstd_done, 1)

            def head_rms(t, b, n, ms, r):
                hold(pool, ms_done, 2 * t + n + 1, passed)
                if not first(t, 1):
                    hold(pool, qk_done, 2 * t - 1 + n, passed)
                pool.tensor_scalar(rqt, ms, rs2[:, b:b + 1], EPS, ALU.mult, ALU.add).then_inc(r_step, 1)
                hold(pool, r_step, 4 * t + 2 * n + 1, passed)
                pool.tensor_tensor(r, rqt, mhalf[:, :], ALU.pow).then_inc(r_step, 1)
                hold(pool, r_step, 4 * t + 2 * n + 2, passed)
                pool.tensor_scalar(r, r, rstd[:, b:b + 1], None, ALU.mult).then_inc(r_done, 1)
                hold(pool, r_done, 2 * t + n + 1, passed)

            def taps(t, lo, hi):
                base, a = t * NP, POOL_CT
                if lo == 0:
                    hold(pool, ut_done, t + 1, passed)
                    if first(t, 1):
                        hold(pool, w_lo_done, NPIECE, passed)
                    else:
                        hold(pool, ln1_ps, t, passed)
                    pool.tensor_scalar(conv[:, a, :], ut[:, a, 0:P], cw[:, a, 0:1], cb[:, a:a + 1],
                                       ALU.mult, ALU.add).then_inc(tap_pool, 1)
                for j in range(max(lo, 1), hi):
                    if j > 2:
                        hold(pool, tap_pool, base + 2 * j - 3, passed)
                    pool.tensor_scalar(prod[:, j % 2, :], ut[:, a, j:j + P], cw[:, a, j:j + 1], None,
                                       ALU.mult).then_inc(tap_pool, 1)
                    hold(pool, tap_pool, base + 2 * j, passed)
                    pool.tensor_tensor(conv[:, a, :], conv[:, a, :], prod[:, j % 2, :],
                                       ALU.add).then_inc(tap_pool, 1)
                if hi == W:
                    hold(pool, tap_pool, base + NP, passed)

            def ln_scale(t):
                hold(pool, ln_stat, 2 * t + 2, passed)
                if not first(t, 1):
                    hold(pool, normed_done, t, passed)
                pool.tensor_scalar(lnr, mv[:, 1:2], EPS, None, ALU.add).then_inc(ln_step, 1)
                hold(pool, ln_step, 2 * t + 1, passed)
                pool.tensor_tensor(lnr, lnr, mhalf[:, 0:1], ALU.pow).then_inc(ln_step, 1)
                hold(pool, ln_step, 2 * t + 2, passed)
                pool.tensor_scalar(lnm, mv[:, 0:1], lnr, -1.0, ALU.mult, ALU.mult).then_inc(ln_rs, 1)

            def ln_swish(t):
                hold(pool, act_ln, t + 1, passed)
                pool.tensor_tensor(swish, swish, sig, ALU.mult).then_inc(swish_done, 1)

            inverse_rms(0, 0)

            def body(t, b):
                sample = isinstance(t, int) and t == PT
                if not first(t, 1):
                    taps(t - 1, 0, 8)
                if not first(t, 2):
                    ln_swish(t - 2)
                if not sample:
                    inverse_rms(t + 1, 1 - b)
                if not first(t, 1):
                    taps(t - 1, 8, 21)
                head_rms(t, b, 0, msq, rq)
                if not first(t, 1):
                    taps(t - 1, 21, W)
                head_rms(t, b, 1, msk, rk)
                hold(pool, qk_done, 2 * t + 2, passed)
                pool.tensor_tensor(k_sb[:, :].rearrange("p (h d) -> p h d", h=NH),
                                   k_sb[:, :].rearrange("p (h d) -> p h d", h=NH),
                                   gk[:, :].unsqueeze(1).broadcast_to([P, NH, HD]), ALU.mult).then_inc(kg_done, 1)
                if not first(t, 1):
                    ln_scale(t - 1)

            tiles(pool, body)
            taps(PT, 0, W)
            ln_swish(PT - 1)
            ln_scale(PT)
            ln_swish(PT)
    return sems


NKT = PT + PAST // P + 1
HG = NH // 2
GC = HG * HD
MAXU = 8
SCALE = HD ** -0.5


def key_tiles(t):
    return (0, t + 1) if t < PT else (PT, PAST // P + 1)


def attention_steps():
    steps = []
    for t in range(NT + 3):
        if t < NT:
            _, n = key_tiles(t)
            half = n if n <= MAXU else n // 2
            parts = [(0, n, False)] if n <= MAXU else [(half, n, False), (0, half, True)]
            units = [(t, h, lo, hi, more) for h in range(HG) for lo, hi, more in parts]
        else:
            units = [None] * 4
        per = len(units) // 4
        for i, unit in enumerate(units):
            steps.append((t, i // per if i % per == 0 else None, unit, i == 3))
    return steps


def phase_attend(nc, io, scr, g, logits):
    with ExitStack() as ctx:
        pre = f"p2{g}_"

        def sb(name, shape, dt=F32):
            return ctx.enter_context(nc.sbuf_tensor(pre + name, shape, dt))

        def ps(name, shape):
            return ctx.enter_context(nc.psum_tensor(pre + name, shape, F32))

        sems = []

        def sem(name):
            sems.append(nc.alloc_semaphore(pre + name))
            return sems[-1]

        NB = 4 - g
        NA = 4
        UW = MAXU * P
        kt_sb = sb("kt", [P, HG, NKT * P], F32R)
        v_sb = sb("v", [P, NKT, GC])
        wo_hi = sb("wo_hi", [P, CT, D], F32R)
        wo_lo = sb("wo_lo", [P, CT, D], F32R)
        q_hi = sb("q_hi", [P, 2, HG, P], F32R)
        q_lo = sb("q_lo", [P, 2, HG, P], F32R)
        keep = sb("keep", [P, NB, UW + 4])
        wgt = sb("wgt", [P, NB, UW])
        at = sb("at", [P, NA, 4 * P])
        kd = sb("kd", [P, 2, HG, 2, HD])
        qd = sb("qd", [P, 2, HG, 2, HD])
        m_hi = sb("m_hi", [P, 2, CT, P], F32R)
        m_lo = sb("m_lo", [P, 2, CT, P], F32R)
        o_raw = sb("o_raw", [P, 2, GC])
        o_sq = sb("o_sq", [P, GC])
        o_n = sb("o_n", [P, 4, GC])
        y = sb("y", [P, 3, D])
        ident = sb("ident", [P, P])
        identb = sb("identb", [P, P], mybir.dt.bfloat16)
        mask = sb("mask", [P, P], mybir.dt.bfloat16)
        gq = sb("gq", [P, 1])
        go = sb("go", [P, CT])
        st = sb("st", [P, 40])
        oms, orr, ort = st[:, 0:4], st[:, 4:8], st[:, 8:12]
        ss, rt, rstd = st[:, 12:13], st[:, 13:14], st[:, 14:15]
        mhalf = sb("mhalf", [P, 4])
        if g == 0:
            c_ld = sb("c_ld", [P, 2, CT, P])
        else:
            o_a = sb("o_a", [P, 2, GC])
            g2 = sb("g2", [P, D])
            h2 = sb("h2", [P, 2, D])
            h2t = sb("h2t", [P, KT, P])
            wr = sb("wr", [P, KT, NR])
        raw = [wgt[:, 0, :], wgt[:, 1, :], wgt[:, 2, :], keep[:, 0, 0:UW]]

        zp = ps("zp", [P, 2, UW])
        tp = ps("tp", [P, 2, 4 * P])
        op = ps("op", [P, 4 * P])
        mp = ps("mp", [P, 4 * P])

        ready, const_in, raw_in = sem("ready"), sem("const_in"), [sem(f"raw_in{i}") for i in range(CT)]
        wo_hi_done, wo_lo_done = sem("wo_hi_done"), sem("wo_lo_done")
        k_in, q_in = [sem("k_in0"), sem("k_in1")], [sem("q_in0"), sem("q_in1")]
        mp_full, mp_free = sem("mp_full"), sem("mp_free")
        k_hi_done, k_done, q_hi_done, q_done = sem("k_hi_done"), sem("k_done"), sem("q_hi_done"), sem("q_done")
        z_done, sig_done, edge_done, scan_done, a_done = (sem("z_done"), sem("sig_done"), sem("edge_done"),
                                                          sem("scan_done"), sem("a_done"))
        t_done, cp_dve, cp_act, av_done = sem("t_done"), sem("cp_dve"), sem("cp_act"), sem("av_done")
        o_out, o_sq_done, o_ms, o_step, o_done = (sem("o_out"), sem("o_sq_done"), sem("o_ms"), sem("o_step"),
                                                  sem("o_done"))
        m_in, m_hi_done, m_done, wo_done = ([sem("m_in0"), sem("m_in1")], sem("m_hi_done"), sem("m_done"),
                                            sem("wo_done"))
        y_in = [sem(f"y_in{i}") for i in range(3)]
        y_done = sem("y_done")
        st_y, st_o, st_h = [[sem(f"st_{x}{i}") for i in range(n)] for x, n in (("y", 3), ("o", 4), ("h", 2))]
        ss_done, rs_step, h2_step, h2_done = sem("ss_done"), sem("rs_step"), sem("h2_step"), sem("h2_done")
        h2t_done, rt_done, lg_done = sem("h2t_done"), sem("rt_done"), sem("lg_done")

        steps = attention_steps()
        units = [u for _, _, u, _ in steps if u]
        n_of = {u: i for i, u in enumerate(units)}
        last_of = {u[0]: i for i, u in enumerate(units)}
        halves, base = [], []
        for i, (_, _, lo, hi, _) in enumerate(units):
            base.append(len(halves))
            halves += [(i, a, min(a + 4, hi)) for a in range(lo, hi, 4)]
        by_act = [n % 4 == 3 for n in range(len(halves))]
        end_half = {t: base[i] + sum(1 for x in halves if x[0] == i) for t, i in last_of.items()}

        def jobs(t, slot):
            out = []
            if slot == 0 and t + 1 < PT:
                out.append(("k", t + 1))
            if slot == 0 and g == 1 and 0 <= t - 2 < NT:
                out.append(("mix", t - 2))
            if slot == 1 and t + 1 < NT:
                out.append(("q", t + 1))
            if slot == 2 and 7 <= t < PT:
                out.append(("k", PT + t - 7))
            lag = 0 if g == 0 else 2
            if slot in (2, 3) and 0 <= t - lag < NT:
                out.append(("wo", t - lag, slot - 2))
            if slot == 3 and g == 1 and 0 <= t - 3 < NT:
                out += [("h2t", t - 3, 0), ("h2t", t - 3, 1), ("route", t - 3)]
            return out

        order = [("k", 0), ("q", 0)]
        for t, slot, _, _ in steps:
            if slot is not None:
                order += jobs(t, slot)
        use = {job: n for n, job in enumerate(order)}
        k_order = [job[1] for job in order if job[0] == "k"]
        k_at = {kt: n for n, kt in enumerate(k_order)}

        def copies_before(n, act):
            return sum(1 for x in by_act[:n] if x == act)

        def copy_halves(eng, u, act):
            for n in range(base[u], base[u + 1] if u + 1 < len(units) else len(halves)):
                if by_act[n] != act:
                    continue
                _, a, e = halves[n]
                eng.wait_ge(t_done, n + 1)
                if n >= NA:
                    eng.wait_ge(av_done, n - NA + 1)
                dst, src = at[:, n % NA, 0:(e - a) * P], tp[:, n % 2, 0:(e - a) * P]
                if act:
                    eng.activation(dst, src, ACT.Copy).then_inc(cp_act, 1)
                else:
                    eng.tensor_copy(dst, src).then_inc(cp_dve, 1)

        block = ctx.enter_context(nc.Block())
        c0 = g * GC

        @block.sync
        def _(sp):
            sp.dma_start(gq[:, :], io["q_norm_g"]).then_inc(const_in, 16)
            sp.dma_start(go[:, :], io["attn_out_g"]).then_inc(const_in, 16)
            if g == 1:
                sp.dma_start(g2[:, :], io["norm_ffn_g"].partition_broadcast(P)).then_inc(const_in, 16)
                sp.dma_start(wr[:, :, :], io["w_router"]).then_inc(const_in, 16)

            def load_k(kt):
                n = k_at[kt]
                if kt < PT:
                    ksrc, vsrc, r = io["k_out"], io["v_out"], kt
                elif kt < NKT - 1:
                    ksrc, vsrc, r = io["cache_k"], io["cache_v"], kt - PT
                else:
                    ksrc, vsrc, r = io["k_out"], io["v_out"], PT
                if n >= 2:
                    sp.wait_ge(mp_full, use[("k", k_order[n - 2])] + 1)
                for a in range(2):
                    sp.dma_start(kd[:, n % 2, :, a, :],
                                 ksrc[r * P:(r + 1) * P, c0:c0 + GC].rearrange("p (h d) -> p h d", h=HG)
                                 ).then_inc(k_in[n % 2], 16)
                sp.dma_start(v_sb[:, kt, :], vsrc[r * P:(r + 1) * P, c0:c0 + GC]).then_inc(k_in[n % 2], 16)

            def load_q(t):
                if t >= 2:
                    sp.wait_ge(mp_full, use[("q", t - 2)] + 1)
                for a in range(2):
                    sp.dma_start(qd[:, t % 2, :, a, :],
                                 scr["q"][t * P:(t + 1) * P, c0:c0 + GC].rearrange("p (h d) -> p h d", h=HG)
                                 ).then_inc(q_in[t % 2], 16)

            def load_mix(t):
                if g == 0:
                    if t >= 2:
                        sp.wait_ge(m_done, t - 1)
                    sp.dma_start(c_ld[:, t % 2, :, :], scr["c"][:, :, t * P:(t + 1) * P]).then_inc(m_in[t % 2], 16)
                else:
                    if t >= 2:
                        sp.wait_ge(mp_full, use[("mix", t - 2)] + 1)
                    sp.dma_start(o_a[:, t % 2, :], scr["o"][t * P:(t + 1) * P, :]).then_inc(m_in[t % 2], 16)

            def load_y(t):
                if t >= 3:
                    sp.wait_ge(st_y[t % 3], 16 * (t // 3))
                    if g == 1:
                        sp.wait_ge(h2_step, t - 2)
                src = io["x"] if g == 0 else scr["y"]
                sp.dma_start(y[:, t % 3, :], src[t * P:(t + 1) * P, :]).then_inc(y_in[t % 3], 16)

            load_k(0)
            load_q(0)
            for k in range(CT):
                sp.dma_start(raw[k], io["w_out"][(g * CT + k) * P:(g * CT + k + 1) * P, :]).then_inc(raw_in[k], 16)
            load_k(1)
            load_q(1)
            load_mix(0)
            load_y(0)
            lag = 0 if g == 0 else 2
            for t in range(NT + 3):
                if t + 2 < PT:
                    load_k(t + 2)
                if t + 2 < NT:
                    load_q(t + 2)
                if 6 <= t < PT - 1:
                    load_k(PT + t - 6)
                if 0 <= t - lag + 1 < NT and t - lag + 1 > 0:
                    load_mix(t - lag + 1)
                    load_y(t - lag + 1)
                if 0 <= t - 1 < NT and g == 0:
                    sp.wait_ge(o_done, t)
                    sp.dma_start(scr["o"][(t - 1) * P:t * P, :], o_n[:, (t - 1) % 4, :]).then_inc(st_o[(t - 1) % 4], 16)
                if 0 <= t - lag < NT:
                    sp.wait_ge(y_done, 2 * (t - lag) + 2)
                    dst = scr["y"] if g == 0 else io["y_out"]
                    sp.dma_start(dst[(t - lag) * P:(t - lag + 1) * P, :], y[:, (t - lag) % 3, :]
                                 ).then_inc(st_y[(t - lag) % 3], 16)
                    if g == 1:
                        sp.wait_ge(h2_done, t - lag + 1)
                        sp.dma_start(scr["h2"][(t - lag) * P:(t - lag + 1) * P, :],
                                     h2[:, (t - lag) % 2, :]).then_inc(st_h[(t - lag) % 2], 16)
            for slots in (st_y, st_o) if g == 0 else (st_y, st_h):
                for i, s in enumerate(slots):
                    sp.wait_ge(s, 16 * len(range(i, NT, len(slots))))

        @block.tensor
        def _(pe):
            def job(j):
                if use[j]:
                    pe.wait_ge(mp_free, use[j])
                if j[0] in "kq":
                    n = k_at[j[1]] if j[0] == "k" else j[1]
                    if j[0] == "k":
                        pe.wait_ge(k_in[n % 2], 48 * (n // 2 + 1))
                    else:
                        pe.wait_ge(q_in[n % 2], 32 * (n // 2 + 1))
                    src = kd if j[0] == "k" else qd
                    for h in range(HG):
                        last = pe.transpose(mp[:, h * P:(h + 1) * P],
                                            src[:, n % 2, h, :, :].rearrange("p a d -> p (a d)"), ident[:, :])
                elif j[0] == "mix":
                    t = j[1]
                    pe.wait_ge(m_in[t % 2], 16 * (t // 2 + 1))
                    pe.wait_ge(o_done, t + 1)
                    for k in range(CT):
                        src = o_a[:, t % 2, :] if k < 2 else o_n[:, t % 4, :]
                        last = pe.transpose(mp[:, k * P:(k + 1) * P], src[:, (k % 2) * P:(k % 2 + 1) * P], ident[:, :])
                elif j[0] == "wo":
                    t, c = j[1], j[2]
                    pe.wait_ge(m_done, t + 1)
                    pe.wait_ge(m_hi_done, t + 1)
                    pe.wait_ge(wo_lo_done, CT)
                    pe.wait_ge(wo_hi_done, CT)
                    n = 0
                    for k in range(CT):
                        for ma, wa in ((m_hi, wo_hi), (m_hi, wo_lo), (m_lo, wo_hi)):
                            last = pe.matmul(mp[:, :], ma[:, t % 2, k, :], wa[:, k, c * C:(c + 1) * C],
                                             start=(n == 0), stop=(n == 3 * CT - 1))
                            n += 1
                    last.then_inc(wo_done, 1)
                    pe.wait_ge(wo_done, 2 * t + c + 1)
                    pe.sem_inc(mp_full, 1)
                    return
                elif j[0] == "h2t":
                    t, c = j[1], j[2]
                    pe.wait_ge(h2_done, t + 1)
                    for k in range(4):
                        last = pe.transpose(mp[:, k * P:(k + 1) * P],
                                            h2[:, t % 2, (4 * c + k) * P:(4 * c + k + 1) * P], ident[:, :])
                else:
                    t = j[1]
                    pe.wait_ge(h2t_done, 2 * t + 2)
                    for k in range(KT):
                        last = pe.matmul(mp[:, 0:NR], h2t[:, k, :], wr[:, k, :], start=(k == 0), stop=(k == KT - 1))
                last.then_inc(mp_full, 1)

            def scores(u):
                t, h, lo, hi, _ = unit = units[u]
                kb, n = key_tiles(t)
                if u >= 2:
                    pe.wait_ge(sig_done, u - 1)
                pe.wait_ge(q_done, t + 1)
                pe.wait_ge(k_done, k_at[kb + hi - 1] + 1)
                for a in range(lo, hi, 4):
                    e = min(a + 4, hi)
                    dst = zp[:, u % 2, (a - lo) * P:(e - lo) * P]
                    keys = kt_sb[:, h, (kb + a) * P:(kb + e) * P]
                    pe.matmul(dst, q_hi[:, t % 2, h, :], keys, start=True, stop=False)
                    if e == n:
                        pe.matmul(zp[:, u % 2, (n - 1 - lo) * P:(n - lo) * P], identb[:, :], mask[:, :],
                                  start=False, stop=False, skip_group_check=True)
                    last = pe.matmul(dst, q_lo[:, t % 2, h, :], keys, start=False, stop=True)
                last.then_inc(z_done, 1)

            def transpose_weights(u):
                lo = units[u][2]
                pe.wait_ge(a_done, u + 1)
                for n in range(base[u], end_of(u)):
                    _, a, e = halves[n]
                    if n >= 2:
                        pe.wait_ge(cp_act if by_act[n - 2] else cp_dve, copies_before(n - 1, by_act[n - 2]))
                    for i in range(a, e):
                        last = pe.transpose(tp[:, n % 2, (i - a) * P:(i - a + 1) * P],
                                            wgt[:, u % NB, (i - lo) * P:(i - lo + 1) * P], ident[:, :])
                    last.then_inc(t_done, 1)

            def end_of(u):
                return base[u + 1] if u + 1 < len(units) else len(halves)

            def values(u):
                t, h, lo, hi, _ = units[u]
                kb, _ = key_tiles(t)
                if h == 0 and u == first_unit(t):
                    if t:
                        pe.wait_ge(o_out, t)
                for n in range(base[u], end_of(u)):
                    _, a, e = halves[n]
                    pe.wait_ge(cp_act if by_act[n] else cp_dve, copies_before(n + 1, by_act[n]))
                    for i in range(a, e):
                        begin = u == first_unit(t) and n == base[u] and i == a
                        end = u == last_of[t] and n == end_of(u) - 1 and i == e - 1
                        last = pe.matmul(op[:, h * HD:(h + 1) * HD], at[:, n % NA, (i - a) * P:(i - a + 1) * P],
                                         v_sb[:, kb + i, h * HD:(h + 1) * HD], start=begin, stop=end,
                                         skip_group_check=True)
                    last.then_inc(av_done, 1)

            def first_unit(t):
                return last_of[t - 1] + 1 if t else 0

            pe.wait_ge(ready, 5)
            job(("k", 0))
            job(("q", 0))
            for s, (t, slot, unit, out) in enumerate(steps):
                if unit:
                    scores(n_of[unit])
                if slot is not None:
                    for j in jobs(t, slot):
                        job(j)
                if s >= 2 and steps[s - 2][2]:
                    transpose_weights(n_of[steps[s - 2][2]])
                if s >= 3 and steps[s - 3][2]:
                    values(n_of[steps[s - 3][2]])

        @block.scalar
        def _(act):
            act.wait_ge(const_in, 16 * (2 if g == 0 else 4))

            def job(j):
                act.wait_ge(mp_full, use[j] + 1)
                if j[0] == "k":
                    if k_at[j[1]]:
                        pass
                    act.activation(kt_sb[:, :, j[1] * P:(j[1] + 1) * P],
                                   mp[:, :].rearrange("p (h t) -> p h t", h=HG), ACT.Copy).then_inc(k_hi_done, 1)
                elif j[0] == "q":
                    t = j[1]
                    if t >= 2:
                        act.wait_ge(z_done, last_of[t - 2] + 1)
                    act.activation(q_hi[:, t % 2, :, :], mp[:, :].rearrange("p (h t) -> p h t", h=HG),
                                   ACT.Copy, scale=gq[:, 0:1]).then_inc(q_hi_done, 1)
                elif j[0] == "mix":
                    t = j[1]
                    if t >= 2:
                        act.wait_ge(wo_done, 2 * t - 2)
                    act.activation(m_hi[:, t % 2, :, :], mp[:, :].rearrange("p (h t) -> p h t", h=CT),
                                   ACT.Copy).then_inc(m_hi_done, 1)
                elif j[0] == "h2t":
                    t, c = j[1], j[2]
                    if t and c == 0:
                        act.wait_ge(mp_full, use[("route", t - 1)] + 1)
                    act.activation(h2t[:, 4 * c:4 * c + 4, :], mp[:, :].rearrange("p (h t) -> p h t", h=4),
                                   ACT.Copy).then_inc(h2t_done, 1)
                    act.wait_ge(h2t_done, 2 * t + c + 1)
                    act.sem_inc(mp_free, 1)

            for k in range(CT):
                act.wait_ge(raw_in[k], 16)
                if g == 0:
                    act.activation(wo_hi[:, k, :], raw[k], ACT.Copy).then_inc(wo_hi_done, 1)
                else:
                    act.activation(wo_hi[:, k, :], raw[k], ACT.Copy, scale=go[:, k:k + 1]).then_inc(wo_hi_done, 1)
            job(("k", 0))
            job(("q", 0))
            act.wait_ge(wo_lo_done, CT)
            for s, (t, slot, unit, out) in enumerate(steps):
                if unit:
                    u = n_of[unit]
                    w = (unit[3] - unit[2]) * P
                    act.wait_ge(z_done, u + 1)
                    if u >= NB:
                        act.wait_ge(t_done, base[u - NB + 1])
                        act.wait_ge(edge_done, u - NB + 2)
                        act.wait_ge(scan_done, u - NB + 2)
                    act.activation(wgt[:, u % NB, 0:w], zp[:, u % 2, 0:w], ACT.Sigmoid, scale=SCALE)
                    act.activation(keep[:, u % NB, 0:w], zp[:, u % 2, 0:w], ACT.Sigmoid,
                                   scale=-SCALE).then_inc(sig_done, 1)
                if slot is not None:
                    for j in jobs(t, slot):
                        if j[0] in ("k", "q", "mix", "h2t"):
                            job(j)
                if out and 0 <= t - 1 < NT:
                    act.wait_ge(av_done, end_half[t - 1])
                    if t >= 3:
                        act.wait_ge(o_done, t - 2)
                    act.activation(o_raw[:, (t - 1) % 2, :], op[:, 0:GC], ACT.Copy).then_inc(o_out, 1)
                if slot == 3 and g == 1 and 0 <= t - 2 < NT:
                    act.wait_ge(y_done, 2 * (t - 2) + 2)
                    if t >= 3:
                        act.wait_ge(rs_step, 2 * (t - 2))
                    if t >= 4:
                        act.wait_ge(st_h[t % 2], 16 * (t // 2 - 1))
                        act.wait_ge(mp_full, use[("h2t", t - 4, 1)] + 1)
                    act.activation(h2[:, t % 2, :], y[:, (t - 2) % 3, :], ACT.Square,
                                   accum_out=ss).then_inc(ss_done, 1)
                if s >= 2 and steps[s - 2][2]:
                    copy_halves(act, n_of[steps[s - 2][2]], True)

        @block.vector
        def _(dve):
            dve.wait_ge(const_in, 16 * (2 if g == 0 else 4))

            def heads(ap):
                return ap.rearrange("p (h t) -> p h t", h=HG)

            def job(j):
                if j[0] == "k":
                    dve.wait_ge(k_hi_done, k_at[j[1]] + 1)
                    low = kt_sb[64:128, :, j[1] * P:(j[1] + 1) * P]
                    dve.tensor_tensor(low, heads(mp[64:128, :]), low.bitcast(F32), ALU.subtract).then_inc(k_done, 1)
                    dve.wait_ge(k_done, k_at[j[1]] + 1)
                elif j[0] == "q":
                    t = j[1]
                    dve.wait_ge(q_hi_done, t + 1)
                    dve.scalar_tensor_tensor(q_lo[:, t % 2, :, :].rearrange("p h t -> p (h t)"), mp[:, :], gq[:, 0:1],
                                             q_hi[:, t % 2, :, :].rearrange("p h t -> p (h t)").bitcast(F32),
                                             ALU.mult, ALU.subtract).then_inc(q_done, 1)
                    dve.wait_ge(q_done, t + 1)
                elif j[0] == "mix":
                    t = j[1]
                    dve.wait_ge(m_hi_done, t + 1)
                    dve.tensor_tensor(m_lo[:, t % 2, :, :], heads(mp[:, :]), m_hi[:, t % 2, :, :].bitcast(F32),
                                      ALU.subtract).then_inc(m_done, 1)
                    dve.wait_ge(m_done, t + 1)
                elif j[0] == "wo":
                    t, c = j[1], j[2]
                    dve.wait_ge(mp_full, use[j] + 1)
                    dve.wait_ge(y_in[t % 3], 16 * (t // 3 + 1))
                    dve.tensor_tensor(y[:, t % 3, c * C:(c + 1) * C], mp[:, :], y[:, t % 3, c * C:(c + 1) * C],
                                      ALU.add).then_inc(y_done, 1)
                    dve.wait_ge(y_done, 2 * t + c + 1)
                elif j[0] == "route":
                    t = j[1]
                    dve.wait_ge(mp_full, use[j] + 1)
                    dve.tensor_copy(logits[:, t, :], mp[:, 0:NR]).then_inc(lg_done, 1)
                    dve.wait_ge(lg_done, t + 1)
                else:
                    return
                dve.sem_inc(mp_free, 1)

            for k in range(CT):
                dve.wait_ge(wo_hi_done, k + 1)
                if g == 0:
                    dve.tensor_tensor(wo_lo[:, k, :], raw[k], wo_hi[:, k, :].bitcast(F32),
                                      ALU.subtract).then_inc(wo_lo_done, 1)
                else:
                    dve.scalar_tensor_tensor(wo_lo[:, k, :], raw[k], go[:, k:k + 1],
                                             wo_hi[:, k, :].bitcast(F32), ALU.mult, ALU.subtract).then_inc(wo_lo_done, 1)
            job(("k", 0))
            job(("q", 0))
            for s, (t, slot, unit, out) in enumerate(steps):
                if unit:
                    u = n_of[unit]
                    w = (unit[3] - unit[2]) * P
                    dve.wait_ge(sig_done, u + 1)
                    dve.wait_ge(edge_done, u + 1)
                    part = keep[:, u % NB, w:0:-1]
                    if unit[4]:
                        dve.wait_ge(scan_done, u)
                    dve.tensor_tensor_scan(part, part, part, keep[:, (u - 1) % NB, 1:2] if unit[4] else 1.0,
                                           ALU.mult, ALU.bypass).then_inc(scan_done, 1)
                if slot is not None:
                    for j in jobs(t, slot):
                        job(j)
                if out and 0 <= t - 1 < NT:
                    dve.wait_ge(o_sq_done, t)
                    if t >= 2:
                        dve.wait_ge(o_step, 2 * (t - 1))
                    dve.tensor_reduce(oms, o_sq[:, :].rearrange("p (h d) -> p h d", h=HG), AX.X,
                                      ALU.add).then_inc(o_ms, 1)
                if s >= 2 and steps[s - 2][2]:
                    copy_halves(dve, n_of[steps[s - 2][2]], False)

        @block.gpsimd
        def _(pool):
            pool.memset(ident[:, :], 0.0).then_inc(ready, 1)
            pool.memset(mask[:, :], 0.0).then_inc(ready, 1)
            pool.memset(mhalf[:, :], -0.5)
            pool.wait_ge(ready, 2)
            pool.affine_select(out=ident[:, :], in_=ident[:, :], compare_op=ALU.not_equal, fill=1.0, base=0,
                               pattern=[[-1, P]], channel_multiplier=1).then_inc(ready, 1)
            pool.affine_select(out=mask[:, :], in_=mask[:, :], compare_op=ALU.is_gt, fill=-1e30, base=0,
                               pattern=[[-1, P]], channel_multiplier=1).then_inc(ready, 1)
            pool.wait_ge(ready, 4)
            pool.tensor_copy(identb[:, :], ident[:, :]).then_inc(ready, 1)
            pool.wait_ge(ready, 5)

            def mix(t):
                pool.wait_ge(m_in[t % 2], 16 * (t // 2 + 1))
                if t >= 2:
                    pool.wait_ge(wo_done, 2 * t - 2)
                pool.tensor_copy(m_hi[:, t % 2, :, :], c_ld[:, t % 2, :, :]).then_inc(m_hi_done, 1)
                pool.wait_ge(m_hi_done, t + 1)
                pool.tensor_tensor(m_lo[:, t % 2, :, :], c_ld[:, t % 2, :, :], m_hi[:, t % 2, :, :].bitcast(F32),
                                   ALU.subtract).then_inc(m_done, 1)

            def edge(u):
                unit = units[u]
                w = (unit[3] - unit[2]) * P
                if u >= NB:
                    pool.wait_ge(a_done, u - NB + 1)
                if unit[4]:
                    pool.wait_ge(sig_done, u)
                    pool.tensor_copy(keep[:, u % NB, w:w + 1], keep[:, (u - 1) % NB, 0:1]).then_inc(edge_done, 1)
                else:
                    pool.memset(keep[:, u % NB, w:w + 1], 1.0).then_inc(edge_done, 1)

            pool.wait_ge(wo_lo_done, CT)
            edge(0)
            for s, (t, slot, unit, out) in enumerate(steps):
                if g == 0 and slot == 0 and t < NT:
                    mix(t)
                if unit:
                    u = n_of[unit]
                    w = (unit[3] - unit[2]) * P
                    if u + 1 < len(units):
                        edge(u + 1)
                    pool.wait_ge(scan_done, u + 1)
                    pool.tensor_tensor(wgt[:, u % NB, 0:w], wgt[:, u % NB, 0:w], keep[:, u % NB, 1:w + 1],
                                       ALU.mult).then_inc(a_done, 1)
                if out and 0 <= t - 1 < NT:
                    n = t - 1
                    pool.wait_ge(o_out, t)
                    if n:
                        pool.wait_ge(o_ms, n)
                    pool.tensor_tensor(o_sq[:, :], o_raw[:, n % 2, :], o_raw[:, n % 2, :],
                                       ALU.mult).then_inc(o_sq_done, 1)
                    pool.wait_ge(o_ms, t)
                    pool.tensor_scalar(ort, oms, 1.0 / HD, EPS, ALU.mult, ALU.add).then_inc(o_step, 1)
                    pool.wait_ge(o_step, 2 * n + 1)
                    if n:
                        pool.wait_ge(o_done, n)
                    pool.tensor_tensor(orr, ort, mhalf[:, :], ALU.pow).then_inc(o_step, 1)
                    pool.wait_ge(o_step, 2 * n + 2)
                    if n >= 4:
                        if g == 0:
                            pool.wait_ge(st_o[n % 4], 16 * (n // 4))
                        else:
                            pool.wait_ge(mp_full, use[("mix", n - 4)] + 1)
                    pool.tensor_tensor(o_n[:, n % 4, :].rearrange("p (h d) -> p h d", h=HG),
                                       o_raw[:, n % 2, :].rearrange("p (h d) -> p h d", h=HG),
                                       orr.unsqueeze(2).broadcast_to([P, HG, HD]), ALU.mult).then_inc(o_done, 1)
                if slot == 3 and g == 1 and 0 <= t - 2 < NT:
                    n = t - 2
                    pool.wait_ge(ss_done, n + 1)
                    if n:
                        pool.wait_ge(h2_step, n)
                    pool.tensor_scalar(rt, ss, 1.0 / D, EPS, ALU.mult, ALU.add).then_inc(rs_step, 1)
                    pool.wait_ge(rs_step, 2 * n + 1)
                    pool.tensor_tensor(rstd, rt, mhalf[:, 0:1], ALU.pow).then_inc(rs_step, 1)
                    pool.wait_ge(rs_step, 2 * n + 2)
                    pool.tensor_scalar(h2[:, n % 2, :], y[:, n % 3, :], rstd, None, ALU.mult).then_inc(h2_step, 1)
                    pool.wait_ge(h2_step, n + 1)
                    pool.tensor_tensor(h2[:, n % 2, :], h2[:, n % 2, :], g2[:, :], ALU.mult).then_inc(h2_done, 1)
    return sems


NG, NE = 4, 32
EG = NE // NG
FF = 512
FT = FF // P
CAP = NT * P
BIG = 1e30


def phase_route(nc, io, scr, logits, table):
    with ExitStack() as ctx:
        def sb(name, shape, dt=F32):
            return ctx.enter_context(nc.sbuf_tensor("p3_" + name, shape, dt))

        def ps(name, shape):
            return ctx.enter_context(nc.psum_tensor("p3_" + name, shape, F32))

        sems = []

        def sem(name):
            sems.append(nc.alloc_semaphore("p3_" + name))
            return sems[-1]

        BF = mybir.dt.bfloat16
        iota_i, iota = sb("iota_i", [P, NE], I32), sb("iota", [P, NE])
        gmax, gi, se, psel = (sb(x, [P, NT]) for x in ("gmax", "gi", "se", "psel"))
        gd, geq, ohg = (sb(x, [P, NT, NG]) for x in ("gd", "geq", "ohg"))
        m = sb("m", [P, NT, NE])
        t1 = sb("t1", [P, NT, NE])
        oh = [sb("oh1", [P, NT, NE]), sb("oh2", [P, NT, NE])]
        v = [sb("v1", [P, NT]), sb("v2", [P, NT])]
        ix = [sb("i1", [P, NT]), sb("i2", [P, NT])]
        wt = [sb("w1", [P, NT]), sb("w2", [P, NT])]
        ex = sb("ex", [P, NT])
        chosen = sb("chosen", [P, NT, NE], BF)
        before, ones = sb("before", [P, P], BF), sb("ones", [P, P], BF)
        cum = sb("cum", [P, NT + 1, NE])
        full = sb("full", [P, NT, NE])
        rk, rki, hi = sb("rk", [P, NT]), sb("rki", [P, NT], I32), sb("hi", [P, NT])
        pos = [sb("pos1", [P, NT], I32), sb("pos2", [P, NT], I32)]
        rows = sb("rows", [P, NT, 2, 2], I32)
        empty = sb("empty", [P, NT, 2], I32)
        zero = sb("zero", [P, D])
        nb = sb("nb", [1, 2, NE])
        rank_ps = ps("rank", [P, 2, 512])
        count_ps = ps("count", [P, 2, 512])
        consts, chain, exped, act_in, chosen_in, chosen_done, ranked, rows_done = (
            sem(x) for x in ("consts", "chain", "exped", "act_in", "chosen_in", "chosen_done", "ranked", "rows_done"))
        filled, zeroed, scattered = sem("filled"), sem("zeroed"), sem("scattered")

        block = ctx.enter_context(nc.Block())

        @block.sync
        def _(sp):
            sp.wait_ge(consts, 9)
            slots = scr["slots"].rearrange("(e p) w -> p e w", p=P)
            sp.dma_start(slots, empty[:, :, :].rearrange("p j w -> p (j w)").unsqueeze(1).broadcast_to(
                [P, NE, 2 * NT])).then_inc(filled, 16)
            sp.dma_start(scr["h2"][CAP:ROWS, :], zero[:, :]).then_inc(zeroed, 16)
            sp.dma_start(io["y_out"][CAP:ROWS, :], zero[:, :]).then_inc(zeroed, 16)
            sp.wait_ge(zeroed, 32)

        @block.scalar
        def _(act):
            act.wait_ge(act_in, 1)
            act.activation(gd[:, :, :], gd[:, :, :], ACT.Exp).then_inc(exped, 1)
            act.wait_ge(act_in, 2)
            act.activation(ex[:, :], ex[:, :], ACT.Exp).then_inc(exped, 1)

        @block.tensor
        def _(pe):
            pe.wait_ge(chosen_done, 1)
            for dst, lhs in ((rank_ps, before), (count_ps, ones)):
                pe.matmul(dst[:, 0, :], lhs[:, :], chosen[:, 0:PT, :].rearrange("p t e -> p (t e)"),
                          start=True, stop=True)
                last = pe.matmul(dst[:, 1, 0:NE], lhs[:, :], chosen[:, PT, :], start=True, stop=True)
            last.then_inc(ranked, 1)

        @block.vector
        def _(dve):
            links = [0]

            def link(ins):
                links[0] += 1
                ins.then_inc(chain, 1)
                dve.wait_ge(chain, links[0])

            def tt(out, a, b, op):
                link(dve.tensor_tensor(out, a, b, op))

            def over(ap, n):
                return ap.unsqueeze(2).broadcast_to([P, NT, n])

            def tiled(ap, n):
                return ap.unsqueeze(1).broadcast_to([P, NT, n])

            def first_max(values, n, best, index, one_hot):
                link(dve.tensor_reduce(best, values, AX.X, ALU.max))
                tt(one_hot, values, over(best, n), ALU.is_equal)
                link(dve.scalar_tensor_tensor(one_hot, one_hot, -100.0, tiled(iota[:, 0:n], n), ALU.mult, ALU.add))
                link(dve.tensor_reduce(index, one_hot, AX.X, ALU.min))
                tt(one_hot, one_hot, over(index, n), ALU.is_equal)

            lg, le = logits[:, :, 0:NG], logits[:, :, NG:NR]
            dve.wait_ge(consts, 9)
            link(dve.tensor_copy(iota[:, :], iota_i[:, :]))
            first_max(lg, NG, gmax[:, :], gi[:, :], ohg[:, :, :])
            tt(gd[:, :, :], lg, over(gmax[:, :], NG), ALU.subtract)
            dve.sem_inc(act_in, 1)
            dve.wait_ge(exped, 1)
            link(dve.tensor_reduce(se[:, :], gd[:, :, :], AX.X, ALU.add))
            link(dve.reciprocal(psel[:, :], se[:, :]))
            by_group = m[:, :, :].rearrange("p t (g e) -> p t g e", g=NG)
            for tile in range(NT):
                last = dve.tensor_tensor(by_group[:, tile], le[:, tile, :].rearrange("p (g e) -> p g e", g=NG),
                                         ohg[:, tile, :].unsqueeze(2).broadcast_to([P, NG, EG]), ALU.mult)
            link(last)
            link(dve.tensor_scalar(geq[:, :, :], ohg[:, :, :], BIG, -BIG, ALU.mult, ALU.add))
            for tile in range(NT):
                last = dve.tensor_tensor(by_group[:, tile], by_group[:, tile],
                                         geq[:, tile, :].unsqueeze(2).broadcast_to([P, NG, EG]), ALU.add)
            link(last)
            first_max(m[:, :, :], NE, v[0][:, :], ix[0][:, :], oh[0][:, :, :])
            link(dve.scalar_tensor_tensor(m[:, :, :], oh[0][:, :, :], -2 * BIG, m[:, :, :], ALU.mult, ALU.add))
            first_max(m[:, :, :], NE, v[1][:, :], ix[1][:, :], oh[1][:, :, :])
            tt(chosen[:, :, :], oh[0][:, :, :], oh[1][:, :, :], ALU.add)
            dve.sem_inc(chosen_in, 1)
            tt(ex[:, :], v[1][:, :], v[0][:, :], ALU.subtract)
            dve.sem_inc(act_in, 1)
            dve.wait_ge(exped, 2)
            link(dve.tensor_scalar_add(v[0][:, :], ex[:, :], 1.0))
            link(dve.reciprocal(v[1][:, :], v[0][:, :]))
            tt(wt[0][:, :], v[1][:, :], psel[:, :], ALU.mult)
            tt(wt[1][:, :], wt[0][:, :], ex[:, :], ALU.mult)
            dve.wait_ge(ranked, 1)
            link(dve.memset(cum[:, 0, :], 0.0))
            for tile in range(NT):
                tt(cum[:, tile + 1, :], cum[:, tile, :],
                   count_ps[:, tile // PT, tile % PT * NE:tile % PT * NE + NE], ALU.add)
            tt(full[:, 0:PT, :], cum[:, 0:PT, :], rank_ps[:, 0, :].rearrange("p (t e) -> p t e", e=NE), ALU.add)
            tt(full[:, PT, :], cum[:, PT, :], rank_ps[:, 1, 0:NE], ALU.add)
            for k in range(2):
                tt(t1[:, :, :], oh[k][:, :, :], full[:, :, :], ALU.mult)
                link(dve.tensor_reduce(rk[:, :], t1[:, :, :], AX.X, ALU.add))
                link(dve.tensor_copy(rki[:, :], rk[:, :]))
                link(dve.tensor_scalar(rki[:, :], rki[:, :], 7, None, ALU.logical_shift_right))
                link(dve.tensor_copy(hi[:, :], rki[:, :]))
                link(dve.tensor_scalar(rk[:, :], rk[:, :], float(NT), 100.0 * CAP, ALU.mult, ALU.add))
                link(dve.scalar_tensor_tensor(rk[:, :], hi[:, :], -float(NT * P - 1), rk[:, :], ALU.mult, ALU.add))
                link(dve.scalar_tensor_tensor(rk[:, :], ix[k][:, :], float(CAP), rk[:, :], ALU.mult, ALU.add))
                link(dve.tensor_copy(pos[k][:, :], rk[:, :]))
                link(dve.tensor_copy(rows[:, :, k, 1].bitcast(F32), wt[k][:, :]))
            dve.sem_inc(rows_done, 1)
            link(dve.tensor_scalar(nb[0:1, 0, :], cum[0:1, NT, :], float(P - 1), None, ALU.add))
            link(dve.tensor_copy(table[0:1, 0, :], nb[0:1, 0, :]))
            link(dve.tensor_scalar(table[0:1, 0, :], table[0:1, 0, :], 7, None, ALU.logical_shift_right))
            link(dve.tensor_scalar(table[0:1, 0, :], table[0:1, 0, :], 1, None, ALU.max))
            link(dve.tensor_copy(nb[0:1, 0, :], table[0:1, 0, :]))
            link(dve.tensor_tensor_scan(nb[0:1, 1, :], nb[0:1, 0, :], nb[0:1, 0, :], 0.0, ALU.add, ALU.bypass))
            tt(nb[0:1, 1, :], nb[0:1, 1, :], nb[0:1, 0, :], ALU.subtract)
            link(dve.tensor_copy(table[0:1, 1, :], nb[0:1, 1, :]))

        @block.gpsimd
        def _(pool):
            pool.iota(iota_i[:, :], pattern=[[1, NE]], base=0, channel_multiplier=0).then_inc(consts, 1)
            for k in range(2):
                pool.iota(rows[:, :, k, 0], pattern=[[P, NT]], base=0, channel_multiplier=1).then_inc(consts, 1)
            pool.memset(zero[:, :], 0.0).then_inc(consts, 1)
            pool.iota(empty[:, :, 0], pattern=[[0, NT]], base=CAP, channel_multiplier=1).then_inc(consts, 1)
            pool.memset(empty[:, :, 1], 0).then_inc(consts, 1)
            pool.memset(ones[:, :], 1.0).then_inc(consts, 1)
            pool.memset(before[:, :], 1.0).then_inc(consts, 1)
            pool.wait_ge(consts, 8)
            pool.affine_select(out=before[:, :], in_=before[:, :], compare_op=ALU.is_gt, fill=0.0, base=0,
                               pattern=[[1, P]], channel_multiplier=-1).then_inc(consts, 1)
            pool.wait_ge(consts, 9)
            pool.wait_ge(chosen_in, 1)
            pool.affine_select(out=chosen[:, PT, :], in_=chosen[:, PT, :], compare_op=ALU.is_ge, fill=0.0,
                               base=DEC - 1, pattern=[[0, NE]], channel_multiplier=-1).then_inc(chosen_done, 1)
            pool.wait_ge(rows_done, 1)
            pool.wait_ge(filled, 16)
            slots = scr["slots"].rearrange("r (j w) -> (r j) w", w=2)
            for tile in range(NT):
                n = P if tile < PT else DEC
                for k in range(2):
                    pool.indirect_dma_start(
                        out=slots, out_offset=bass.IndirectOffsetOnAxis(ap=pos[k][0:n, tile:tile + 1], axis=0),
                        in_=rows[0:n, tile, k, :], in_offset=None).then_inc(scattered, 16)
            pool.wait_ge(scattered, 32 * NT)
    return sems


def phase_experts(nc, io, scr, table):
    with ExitStack() as ctx:
        def sb(name, shape, dt=F32):
            return ctx.enter_context(nc.sbuf_tensor("p4_" + name, shape, dt))

        def ps(name, shape):
            return ctx.enter_context(nc.psum_tensor("p4_" + name, shape, F32))

        sems = []

        def sem(name):
            sems.append(nc.alloc_semaphore("p4_" + name))
            return sems[-1]

        wg, wu = sb("wg", [P, 2, KT, FF]), sb("wu", [P, 2, KT, FF])
        wd = sb("wd", [P, 2, FT, D])
        slot = sb("slot", [P, 2, NT, 2], I32)
        xg = sb("xg", [P, D])
        xt = sb("xt", [P, KT, P])
        sg, gs, h = sb("sg", [P, FF]), sb("gs", [P, FF]), sb("h", [P, FF])
        ht = sb("ht", [P, FT, P])
        yo = sb("yo", [P, D])
        at_g, at_s = sb("at_g", [P, 1], I32), sb("at_s", [P, 1], I32)
        w_g, w_s = sb("w_g", [P, 1]), sb("w_s", [P, 1])
        dummy = sb("dummy", [P, 1], I32)
        ident = sb("ident", [P, P])

        xtp = ps("xtp", [P, KT, P])
        gp, up = ps("gp", [P, FF]), ps("up", [P, FF])
        htp = ps("htp", [P, FT, P])
        dp = ps("dp", [P, 2, 512])

        w_in = [[sem(f"w{x}{a}") for a in range(2)] for x in "gud"]
        slot_in = [sem("slot_in0"), sem("slot_in1")]
        expert_done, slots_used, ready = sem("expert_done"), sem("slots_used"), sem("ready")
        gathered, xt_ps, xt_done, gu_done = sem("gathered"), sem("xt_ps"), sem("xt_done"), sem("gu_done")
        sg_done, gs_done, h_done, ht_ps, ht_done = (sem("sg_done"), sem("gs_done"), sem("h_done"), sem("ht_ps"),
                                                    sem("ht_done"))
        d_done, yo_act, yo_dve, added = sem("d_done"), sem("yo_act"), sem("yo_dve"), sem("added")
        passed, passed_pe = sem("passed"), sem("passed_pe")
        rows_s, rows_g = sem("rows_s"), sem("rows_g")

        block = ctx.enter_context(nc.Block())

        def experts(eng, body):
            with eng.Fori(0, NE // 2) as i:
                for a in range(2):
                    e = i * 2 + a
                    n = eng.value_load(table[0:1, 0, bass.ds(e, 1)], min_val=1, max_val=NT)
                    b0 = eng.value_load(table[0:1, 1, bass.ds(e, 1)], min_val=0, max_val=NE * NT)
                    body(i, e, a, n, b0)

        @block.sync
        def _(sp):
            slots = scr["slots"]

            def load(e, a):
                sp.dma_start(slot[:, a, :, :].rearrange("p j w -> p (j w)"),
                             slots[bass.ts(e, P), :]).then_inc(slot_in[a], 16)
                for x, (dst, src, rows) in enumerate(((wg, "w_gate", D), (wu, "w_up", D), (wd, "w_down", FF))):
                    sp.dma_start(dst[:, a, :, :],
                                 io[src][bass.ts(e, rows), :].rearrange("(k p) f -> p k f", p=P)
                                 ).then_inc(w_in[x][a], 16)

            load(0, 0)
            load(1, 1)
            with sp.Fori(1, NE // 2) as i:
                for a in range(2):
                    sp.wait_ge(expert_done, i * 2 + a - 1)
                    sp.wait_ge(slots_used, i * 2 + a - 1)
                    load(i * 2 + a, a)

        @block.tensor
        def _(pe):
            def transpose_x(b):
                pe.wait_ge(gathered, b * 16 + 16)
                pe.wait_ge(xt_done, b + 1)
                for k in range(KT):
                    last = pe.transpose(xtp[:, k, :], xg[:, k * P:(k + 1) * P], ident[:, :])
                last.then_inc(xt_ps, 1)

            for done in (gu_done, d_done, ht_ps, xt_ps):
                pe.sem_inc(done, 1)
            pe.wait_ge(ready, 3)
            transpose_x(0)

            def body(i, e, a, n, b0):
                for x in range(3):
                    hold(pe, w_in[x][a], i * 16 + 16, passed_pe)
                with pe.Fori(0, n) as j:
                    b = b0 + j
                    pe.wait_ge(xt_done, b + 2)
                    pe.wait_ge(h_done, b + 1)
                    for dst, w in ((gp, wg), (up, wu)):
                        for k in range(KT):
                            last = pe.matmul(dst[:, :], xt[:, k, :], w[:, a, k, :], start=(k == 0), stop=(k == KT - 1))
                    last.then_inc(gu_done, 1)
                    transpose_x(b + 1)
                    pe.wait_ge(h_done, b + 2)
                    pe.wait_ge(ht_done, b + 1)
                    for k in range(FT):
                        last = pe.transpose(htp[:, k, :], h[:, k * P:(k + 1) * P], ident[:, :])
                    last.then_inc(ht_ps, 1)
                    pe.wait_ge(ht_done, b + 2)
                    pe.wait_ge(yo_act, b + 2)
                    pe.wait_ge(yo_dve, b + 2)
                    for c in range(2):
                        for k in range(FT):
                            last = pe.matmul(dp[:, c, :], ht[:, k, :], wd[:, a, k, c * 512:(c + 1) * 512],
                                             start=(k == 0), stop=(k == FT - 1))
                    last.then_inc(d_done, 1)
                pe.wait_ge(d_done, b0 + n + 1)
                pe.sem_inc(expert_done, 1)

            experts(pe, body)

        @block.scalar
        def _(act):
            def evac_x(b):
                act.wait_ge(xt_ps, b + 2)
                act.wait_ge(gu_done, b + 1)
                act.activation(xt[:, :, :], xtp[:, :, :], ACT.Copy).then_inc(xt_done, 1)

            for done in (xt_done, ht_done):
                act.sem_inc(done, 1)
            act.wait_ge(ready, 3)
            evac_x(0)
            act.wait_ge(yo_act, 2)

            def body(i, e, a, n, b0):
                with act.Fori(0, n) as j:
                    b = b0 + j
                    act.wait_ge(gu_done, b + 2)
                    act.wait_ge(gs_done, b + 1)
                    act.activation(sg[:, :], gp[:, :], ACT.Sigmoid).then_inc(sg_done, 1)
                    evac_x(b + 1)
                    act.wait_ge(ht_ps, b + 2)
                    act.wait_ge(d_done, b + 1)
                    act.activation(ht[:, :, :], htp[:, :, :], ACT.Copy).then_inc(ht_done, 1)
                    act.wait_ge(d_done, b + 2)
                    act.wait_ge(rows_s, b + 2)
                    act.wait_ge(added, b * 16 + 32)
                    act.activation(yo[:, 0:512], dp[:, 0, :], ACT.Copy, scale=w_s[:, 0:1]).then_inc(yo_act, 1)

            experts(act, body)

        @block.vector
        def _(dve):
            for done in (gs_done, h_done):
                dve.sem_inc(done, 1)
            dve.wait_ge(ready, 3)

            def body(i, e, a, n, b0):
                with dve.Fori(0, n) as j:
                    b = b0 + j
                    dve.wait_ge(sg_done, b + 1)
                    dve.tensor_tensor(gs[:, :], gp[:, :], sg[:, :], ALU.mult).then_inc(gs_done, 1)
                    dve.wait_ge(gs_done, b + 2)
                    dve.wait_ge(ht_ps, b + 1)
                    dve.tensor_tensor(h[:, :], up[:, :], gs[:, :], ALU.mult).then_inc(h_done, 1)
                    dve.wait_ge(d_done, b + 2)
                    dve.wait_ge(rows_s, b + 2)
                    dve.wait_ge(added, b * 16 + 32)
                    dve.tensor_scalar(yo[:, 512:D], dp[:, 1, :], w_s[:, 0:1], None, ALU.mult).then_inc(yo_dve, 1)

            experts(dve, body)

        @block.gpsimd
        def _(pool):
            pool.memset(ident[:, :], 0.0).then_inc(ready, 1)
            hold(pool, ready, 1, passed)
            pool.affine_select(out=ident[:, :], in_=ident[:, :], compare_op=ALU.not_equal, fill=1.0, base=0,
                               pattern=[[-1, P]], channel_multiplier=1).then_inc(ready, 1)
            pool.iota(dummy[:, :], pattern=[[0, 1]], base=CAP, channel_multiplier=1).then_inc(ready, 1)
            hold(pool, ready, 3, passed)
            pool.memset(yo[:, 0:512], 0.0).then_inc(yo_act, 1)
            pool.memset(yo[:, 512:D], 0.0).then_inc(yo_dve, 1)
            pool.sem_inc(yo_act, 1)
            pool.sem_inc(yo_dve, 1)
            pool.wait_ge(yo_act, 2)
            pool.wait_ge(yo_dve, 2)
            pool.indirect_dma_start(out=io["y_out"], out_offset=bass.IndirectOffsetOnAxis(ap=dummy[:, 0:1], axis=0),
                                    in_=yo[:, :], in_offset=None, compute_op=ALU.add).then_inc(added, 16)
            pool.tensor_copy(at_g[:, :], dummy[:, :])
            pool.memset(w_g[:, :], 0.0).then_inc(rows_g, 1)

            def turn(b):
                hold(pool, rows_g, b + 1, passed)
                hold(pool, added, b * 16 + 16, passed)
                hold(pool, yo_act, b + 1, passed)
                hold(pool, yo_dve, b + 1, passed)
                hold(pool, xt_ps, b + 1, passed)
                pool.tensor_copy(at_s[:, :], at_g[:, :])
                pool.tensor_copy(w_s[:, :], w_g[:, :]).then_inc(rows_s, 1)
                hold(pool, rows_s, b + 1, passed)

            def gather(b):
                hold(pool, rows_g, b + 2, passed)
                hold(pool, xt_ps, b + 1, passed)
                pool.indirect_dma_start(out=xg[:, :], out_offset=None, in_=scr["h2"],
                                        in_offset=bass.IndirectOffsetOnAxis(ap=at_g[:, 0:1], axis=0)
                                        ).then_inc(gathered, 16)

            def add(b):
                hold(pool, yo_act, b + 2, passed)
                hold(pool, yo_dve, b + 2, passed)
                pool.indirect_dma_start(out=io["y_out"], out_offset=bass.IndirectOffsetOnAxis(ap=at_s[:, 0:1], axis=0),
                                        in_=yo[:, :], in_offset=None, compute_op=ALU.add).then_inc(added, 16)

            def body(i, e, a, n, b0):
                hold(pool, slot_in[a], i * 16 + 16, passed)
                with pool.Fori(0, n) as j:
                    b = b0 + j
                    turn(b)
                    pool.tensor_copy(at_g[:, :], slot[:, a, bass.ds(j, 1), 0])
                    pool.tensor_copy(w_g[:, :], slot[:, a, bass.ds(j, 1), 1].bitcast(F32)).then_inc(rows_g, 1)
                    gather(b)
                    add(b)
                hold(pool, rows_g, b0 + n + 1, passed)
                pool.sem_inc(slots_used, 1)

            experts(pool, body)
            last = pool.value_load(table[0:1, 1, NE - 1:NE], min_val=0, max_val=NE * NT)
            count = pool.value_load(table[0:1, 0, NE - 1:NE], min_val=1, max_val=NT)
            total = last + count
            turn(total)
            pool.tensor_copy(at_g[:, :], dummy[:, :]).then_inc(rows_g, 1)
            gather(total)
            add(total)
            hold(pool, added, total * 16 + 32, passed)
            hold(pool, gathered, total * 16 + 16, passed)
    return sems


def build(nc, io):
    scr = {
        "q": nc.dram_tensor("scr_q", [NT * P, C], F32, kind=SCRATCH).ap(),
        "c": nc.dram_tensor("scr_c", [P, CT, NT * P], F32, kind=SCRATCH).ap(),
        "o": nc.dram_tensor("scr_o", [NT * P, GC], F32, kind=SCRATCH).ap(),
        "y": nc.dram_tensor("scr_y", [NT * P, D], F32, kind=SCRATCH).ap(),
        "h2": nc.dram_tensor("scr_h2", [ROWS, D], F32, kind=SCRATCH).ap(),
        "slots": nc.dram_tensor("scr_slots", [NE * P, 2 * NT], I32, kind=SCRATCH).ap(),
    }

    def phase_ends(sems):
        nc.clear_and_free_semaphores(sems)
        nc.all_engine_barrier()

    phase_ends(phase_project(nc, io, scr))
    with nc.sbuf_tensor("table", [1, 2, NE], I32) as table:
        with nc.sbuf_tensor("logits", [P, NT, NR], F32) as logits:
            for g in range(2):
                phase_ends(phase_attend(nc, io, scr, g, logits))
            phase_ends(phase_route(nc, io, scr, logits, table))
        phase_ends(phase_experts(nc, io, scr, table))


def kernel(**inputs):
    import concourse.bacc as bacc
    import numpy as np
    from concourse.bass_utils import run_bass_kernel_spmd

    def cols(v, n):
        return np.ascontiguousarray(v.reshape(n, P).T)

    a = {k: np.asarray(v) for k, v in inputs.items()}
    x = np.zeros((ROWS, D), a["x_prompt"].dtype)
    x[:SEQ], x[SEQ:TOK] = a["x_prompt"][0], a["x_sample"][0]
    router = np.concatenate([a["w_router_group"][0], a["w_router_expert"][0]], axis=1)
    arrays = {
        "x": x,
        "norm_mix_g": cols(a["norm_mix_g"][0], KT),
        "w_in": a["w_in"][0],
        "k_norm_g": a["k_norm_g"][0],
        "q_norm_g": np.ascontiguousarray(np.concatenate([a["q_norm_g"][0]] * 2)[:, None]),
        "conv_w": np.ascontiguousarray(a["conv_w"][0].reshape(W, CT, P).transpose(2, 1, 0)),
        "conv_b": cols(a["conv_b"][0], CT),
        "conv_ln_g": cols(a["conv_ln_g"][0], CT),
        "conv_ln_b": cols(a["conv_ln_b"][0], CT),
        "cache_conv": a["cache_conv"][0, 0],
        "cache_k": a["cache_k"][0, 0].reshape(PAST, C),
        "cache_v": a["cache_v"][0, 0].reshape(PAST, C),
        "attn_out_g": cols(a["attn_out_g"][0].reshape(-1), CT),
        "norm_ffn_g": a["norm_ffn_g"][0],
        "w_out": a["w_out"][0],
        "w_router": np.ascontiguousarray(router.reshape(KT, P, NR).transpose(1, 0, 2)),
        "w_gate": a["w_exp_gate"][0].reshape(NE * D, FF),
        "w_up": a["w_exp_up"][0].reshape(NE * D, FF),
        "w_down": a["w_exp_down"][0].reshape(NE * FF, D),
    }
    arrays = {"in_" + k: np.ascontiguousarray(v) for k, v in arrays.items()}

    nc = bacc.Bacc("TRN2", target_bir_lowering=False, num_devices=1)
    io = {k[3:]: nc.dram_tensor(k, list(v.shape), F32, kind="ExternalInput").ap() for k, v in arrays.items()}
    for name in ("k_out", "v_out", "u_out"):
        io[name] = nc.dram_tensor(name, [NT * P, C], F32, kind="ExternalOutput").ap()
    io["y_out"] = nc.dram_tensor("y_out", [ROWS, D], F32, kind="ExternalOutput").ap()
    build(nc, io)
    got = run_bass_kernel_spmd(nc, [arrays], core_ids=[0]).results[0]

    y, k, v, u = (got[name] for name in ("y_out", "k_out", "v_out", "u_out"))
    k, v = k.reshape(-1, NH, HD), v.reshape(-1, NH, HD)
    return (y[None, :SEQ], y[None, SEQ:TOK], k[None, None, :SEQ], v[None, None, :SEQ],
            u[None, None, SEQ - HIST:SEQ], k[None, None, SEQ:TOK], v[None, None, SEQ:TOK],
            u[None, None, TOK - HIST:TOK])
```

```python
from contextlib import ExitStack

import concourse.bass as bass
from concourse import mybir

F32 = mybir.dt.float32
F32R = mybir.dt.float32r
I32 = mybir.dt.int32
ALU = mybir.AluOpType
ACT = mybir.ActivationFunctionType
AX = mybir.AxisListType

P = 128
D = 1024
KT = D // P
C = 512
CT = C // P
NH, HD = 8, 64
W = 31
HIST = W - 1
SEQ, DEC, PAST = 2048, 32, 1024
PT = SEQ // P
NT = PT + 1
TOK = SEQ + DEC
ROWS = (NT + 1) * P
NR = 36
NCH = 5
EPS = 1e-6
SCRATCH = "Internal"
CHUNKS = [1, 0, 2, 3, 4]


def tiles(eng, body):
    body(0, 0)
    body(1, 1)
    with eng.Fori(1, PT // 2) as i:
        body(i * 2, 0)
        body(i * 2 + 1, 1)
    body(PT, 0)


def first(t, n):
    return isinstance(t, int) and t < n


def hold(eng, signal, value, passed):
    eng.wait_ge(signal, value)
    if not isinstance(value, int):
        eng.sem_inc(passed, 1)


def phase_project(nc, io, scr):
    with ExitStack() as ctx:
        def sb(name, shape, dt=F32):
            return ctx.enter_context(nc.sbuf_tensor("p1_" + name, shape, dt))

        def ps(name, shape):
            return ctx.enter_context(nc.psum_tensor("p1_" + name, shape, F32))

        sems = []

        def sem(name):
            sems.append(nc.alloc_semaphore("p1_" + name))
            return sems[-1]

        w_hi = sb("w_hi", [P, KT, NCH * C], F32R)
        w_lo = sb("w_lo", [P, KT, NCH * C], F32R)
        RAW = 4
        w_raw = sb("w_raw", [P, RAW, C])
        conv = w_raw[:, 0, :].rearrange("p (a t) -> p a t", a=CT)
        normed, sig, swish = w_raw[:, 1, :], w_raw[:, 2, :], w_raw[:, 3, :]
        x_sb = sb("x", [P, 2, D])
        xt_hi = sb("xt_hi", [P, 2, KT, P], F32R)
        xt_lo = sb("xt_lo", [P, 2, KT, P], F32R)
        u = sb("u", [P, C])
        tmp = sb("tmp", [P, C])
        q_sb, k_sb, v_sb = sb("q", [P, C]), sb("k", [P, C]), sb("v", [P, C])
        ut = sb("ut", [P, CT, HIST + P])
        ident = sb("ident", [P, P])
        gcol = sb("gcol", [P, KT])
        gk = sb("gk", [P, HD])
        cw = sb("cw", [P, CT, W])
        cb, lng, lnb = sb("cb", [P, CT]), sb("lng", [P, CT]), sb("lnb", [P, CT])
        prod = sb("prod", [P, 2, P])
        st = sb("st", [P, 64])
        ss, rstd, rs2 = st[:, 0:2], st[:, 2:4], st[:, 4:6]
        rtmp = st[:, 6:7]
        msq, msk = st[:, 8:16], st[:, 16:24]
        rq, rk = st[:, 24:32], st[:, 32:40]
        bnst, mv, lnr, lnm = st[:, 40:46], st[:, 46:48], st[:, 48:49], st[:, 49:50]
        rqt = st[:, 50:58]
        mhalf = sb("mhalf", [P, NH])
        cached = x_sb[:, 1, 0:C]

        pj = ps("pj", [P, NCH, C])
        pxt = ps("pxt", [P, KT, P])
        pm = ps("pm", [P, C])

        ident_done, const_dma = sem("ident_done"), sem("const_dma")
        x_in = [sem("x_in0"), sem("x_in1")]
        piece_in = [sem(f"piece_in{i}") for i in range(RAW)]
        w_hi_done, w_lo_done = sem("w_hi_done"), sem("w_lo_done")
        xt_ps, xt_hi_done, xt_lo_done = sem("xt_ps"), sem("xt_hi_done"), sem("xt_lo_done")
        sq_done, rstd_step, rstd_done = sem("sq_done"), sem("rstd_step"), sem("rstd_done")
        pj_done = sem("pj_done")
        sg_done, tmp_read = sem("sg_done"), sem("tmp_read")
        u_done, ut_ps, ut_done, hist_done = sem("u_done"), sem("ut_ps"), sem("ut_done"), sem("hist_done")
        ms_done, r_step, r_done = sem("ms_done"), sem("r_step"), sem("r_done")
        qk_done, kg_done, v_done = sem("qk_done"), sem("kg_done"), sem("v_done")
        tap_dve, tap_pool = sem("tap_dve"), sem("tap_pool")
        ln1_ps, ln_stat, ln_step, ln_rs = sem("ln1_ps"), sem("ln_stat"), sem("ln_step"), sem("ln_rs")
        normed_done, ln2_ps, act_ln, swish_done = sem("normed_done"), sem("ln2_ps"), sem("act_ln"), sem("swish_done")
        st_q, st_k, st_v, st_c, st_u = sem("st_q"), sem("st_k"), sem("st_v"), sem("st_c"), sem("st_u")
        passed, passed_dve = sem("passed"), sem("passed_dve")
        cached_in, cached_ps = sem("cached_in"), sem("cached_ps")

        DVE_CT = [0, 1, 2]
        POOL_CT = 3
        ND = W * len(DVE_CT)
        NP = 2 * W - 1
        NPIECE = NCH * KT
        NCONST = 6
        pieces = [(c, k) for c in CHUNKS for k in range(KT)]

        block = ctx.enter_context(nc.Block())

        @block.sync
        def _(sp):
            sp.dma_start(gcol[:, :], io["norm_mix_g"]).then_inc(const_dma, 16)
            sp.dma_start(x_sb[:, 0, :], io["x"][0:P, :]).then_inc(x_in[0], 16)
            sp.dma_start(gk[:, :], io["k_norm_g"].partition_broadcast(P)).then_inc(const_dma, 16)
            sp.dma_start(cw[:, :, :], io["conv_w"]).then_inc(const_dma, 16)
            sp.dma_start(cb[:, :], io["conv_b"]).then_inc(const_dma, 16)
            sp.dma_start(lng[:, :], io["conv_ln_g"]).then_inc(const_dma, 16)
            sp.dma_start(lnb[:, :], io["conv_ln_b"]).then_inc(const_dma, 16)
            for n, (c, k) in enumerate(pieces):
                if n >= RAW:
                    sp.wait_ge(w_lo_done, n - RAW + 1)
                sp.dma_start(w_raw[:, n % RAW, :],
                             io["w_in"][k * P:(k + 1) * P, c * C:(c + 1) * C]).then_inc(piece_in[n % RAW], 16)
                if n == KT:
                    sp.dma_start(x_sb[:, 1, :], io["x"][P:2 * P, :]).then_inc(x_in[1], 16)

            def store_swish(t):
                sp.wait_ge(swish_done, t + 1)
                sp.dma_start(scr["c"][:, :, bass.ts(t, P)],
                             swish.rearrange("p (a t) -> p a t", a=CT)).then_inc(st_c, 16)

            def body(t, b):
                if isinstance(t, int) and t == PT:
                    sp.wait_ge(x_in[1], 8 * PT + 16)
                    sp.dma_start(cached[0:HIST, :], io["cache_conv"]).then_inc(cached_in, 16)
                else:
                    sp.wait_ge(sq_done, t + 1)
                    sp.dma_start(x_sb[:, b, :], io["x"][bass.ts(t + 2, P), :]).then_inc(x_in[b], 16)
                if not first(t, 2):
                    store_swish(t - 2)
                sp.wait_ge(u_done, t + 1)
                sp.dma_start(io["u_out"][bass.ts(t, P), :], u[:, :]).then_inc(st_u, 16)
                sp.wait_ge(qk_done, 2 * t + 1)
                sp.dma_start(scr["q"][bass.ts(t, P), :], q_sb[:, :]).then_inc(st_q, 16)
                sp.wait_ge(kg_done, t + 1)
                sp.dma_start(io["k_out"][bass.ts(t, P), :], k_sb[:, :]).then_inc(st_k, 16)
                sp.wait_ge(v_done, t + 1)
                sp.dma_start(io["v_out"][bass.ts(t, P), :], v_sb[:, :]).then_inc(st_v, 16)

            tiles(sp, body)
            store_swish(PT - 1)
            store_swish(PT)
            for s in (st_q, st_k, st_v, st_c, st_u):
                sp.wait_ge(s, 16 * NT)

        @block.tensor
        def _(pe):
            def transpose_x(t, b):
                pe.wait_ge(x_in[b], (t - b) * 8 + 16)
                if not first(t, 1):
                    pe.wait_ge(xt_lo_done, t)
                for k in range(KT):
                    last = pe.transpose(pxt[:, k, :], x_sb[:, b, k * P:(k + 1) * P], ident[:, :])
                last.then_inc(xt_ps, 1)

            def project(t, b, i):
                c = CHUNKS[i]
                if i == 0:
                    pe.wait_ge(xt_lo_done, t + 1)
                    pe.wait_ge(xt_hi_done, t + 1)
                if first(t, 1):
                    pe.wait_ge(w_lo_done, KT * (i + 1))
                    pe.wait_ge(w_hi_done, KT * (i + 1))
                elif c < 2:
                    pe.wait_ge(u_done, t)
                elif c < 4:
                    pe.wait_ge(qk_done, 2 * t - 3 + c)
                else:
                    pe.wait_ge(v_done, t)
                n = 0
                for k in range(KT):
                    for xa, wa in ((xt_hi, w_hi), (xt_hi, w_lo), (xt_lo, w_hi)):
                        last = pe.matmul(pj[:, c, :], xa[:, b, k, :], wa[:, k, c * C:(c + 1) * C],
                                         start=(n == 0), stop=(n == 3 * KT - 1))
                        n += 1
                last.then_inc(pj_done, 1)

            def four(src, done):
                for a in range(CT):
                    last = pe.transpose(pm[:, a * P:(a + 1) * P], src(a), ident[:, :])
                last.then_inc(done, 1)

            def ln1(t):
                pe.wait_ge(tap_dve, (t + 1) * ND)
                pe.wait_ge(tap_pool, (t + 1) * NP)
                if isinstance(t, int) and t == PT:
                    pe.wait_ge(act_ln, PT)
                else:
                    pe.wait_ge(ut_done, t + 2)
                four(lambda a: conv[:, a, :], ln1_ps)

            def ln2(t):
                pe.wait_ge(normed_done, t + 1)
                four(lambda a: normed[:, a * P:(a + 1) * P], ln2_ps)

            def ut_transpose(t):
                pe.wait_ge(u_done, t + 1)
                if not first(t, 2):
                    pe.wait_ge(act_ln, t - 1)
                if not first(t, 1):
                    pe.wait_ge(hist_done, t + 1)
                four(lambda a: u[:, a * P:(a + 1) * P], ut_ps)

            pe.wait_ge(ident_done, 3)
            transpose_x(0, 0)

            def body(t, b):
                sample = isinstance(t, int) and t == PT
                project(t, b, 0)
                if not first(t, 2):
                    ln2(t - 2)
                project(t, b, 1)
                if sample:
                    pe.wait_ge(cached_in, 16)
                    pe.wait_ge(act_ln, t - 1)
                    for a in range(CT):
                        last = pe.transpose(pm[:, a * P:a * P + HIST], cached[0:HIST, a * P:(a + 1) * P],
                                            ident[0:HIST, 0:HIST])
                    last.then_inc(cached_ps, 1)
                else:
                    transpose_x(t + 1, 1 - b)
                project(t, b, 2)
                project(t, b, 3)
                ut_transpose(t)
                project(t, b, 4)
                if not first(t, 1):
                    ln1(t - 1)

            tiles(pe, body)
            ln2(PT - 1)
            ln1(PT)
            ln2(PT)

        @block.scalar
        def _(act):
            act.wait_ge(const_dma, 16 * NCONST)

            def x_parts(t, b):
                act.wait_ge(xt_ps, t + 1)
                if not first(t, 2):
                    act.wait_ge(pj_done, 5 * t - 5)
                    act.wait_ge(rstd_done, t - 1)
                act.activation(xt_hi[:, b, :, :], pxt[:, :, :], ACT.Copy).then_inc(xt_hi_done, 1)
                act.activation(x_sb[:, b, :], x_sb[:, b, :], ACT.Square,
                               accum_out=ss[:, b:b + 1]).then_inc(sq_done, 1)

            for n, (c, k) in enumerate(pieces):
                act.wait_ge(piece_in[n % RAW], 16 * (n // RAW + 1))
                act.activation(w_hi[:, k, c * C:(c + 1) * C], w_raw[:, n % RAW, :], ACT.Copy,
                               scale=gcol[:, k:k + 1]).then_inc(w_hi_done, 1)
                if n == 1:
                    x_parts(0, 0)

            def ln_norm(t):
                act.wait_ge(ln_rs, t + 1)
                if not first(t, 1):
                    act.wait_ge(ln2_ps, t)
                act.activation(normed, pm[:, :], ACT.Identity, scale=lnr, bias=lnm).then_inc(normed_done, 1)

            def ln_out(t):
                act.wait_ge(ln2_ps, t + 1)
                if not first(t, 1):
                    act.wait_ge(st_c, 16 * t)
                for a in range(CT):
                    act.activation(sig[:, a * P:(a + 1) * P], pm[:, a * P:(a + 1) * P], ACT.Sigmoid,
                                   scale=lng[:, a:a + 1], bias=lnb[:, a:a + 1])
                    last = act.activation(swish[:, a * P:(a + 1) * P], pm[:, a * P:(a + 1) * P], ACT.Identity,
                                          scale=lng[:, a:a + 1], bias=lnb[:, a:a + 1])
                last.then_inc(act_ln, 1)

            def body(t, b):
                sample = isinstance(t, int) and t == PT
                act.wait_ge(pj_done, 5 * t + 1)
                act.wait_ge(rstd_done, t + 1)
                if not first(t, 1):
                    act.wait_ge(tmp_read, 3 * t)
                act.activation(tmp[:, :], pj[:, 1, :], ACT.Sigmoid, scale=rstd[:, b:b + 1]).then_inc(sg_done, 1)
                if not first(t, 2):
                    ln_out(t - 2)
                if not sample:
                    x_parts(t + 1, 1 - b)
                act.wait_ge(pj_done, 5 * t + 3)
                act.wait_ge(tmp_read, 3 * t + 1)
                act.activation(tmp[:, :], pj[:, 2, :], ACT.Square).then_inc(sg_done, 1)
                if not first(t, 1):
                    act.wait_ge(tap_dve, t * ND)
                    act.wait_ge(tap_pool, t * NP)
                    if sample:
                        act.wait_ge(cached_ps, 1)
                        act.activation(ut[:, :, 0:HIST],
                                       pm[:, :].rearrange("p (a t) -> p a t", a=CT)[:, :, 0:HIST],
                                       ACT.Copy).then_inc(hist_done, 1)
                    else:
                        act.activation(ut[:, :, 0:HIST], ut[:, :, P:P + HIST], ACT.Copy).then_inc(hist_done, 1)
                act.wait_ge(hist_done, t + 1)
                act.wait_ge(ut_ps, t + 1)
                act.activation(ut[:, :, HIST:HIST + P], pm[:, :].rearrange("p (a t) -> p a t", a=CT),
                               ACT.Copy).then_inc(ut_done, 1)
                act.wait_ge(pj_done, 5 * t + 4)
                act.wait_ge(tmp_read, 3 * t + 2)
                act.activation(tmp[:, :], pj[:, 3, :], ACT.Square).then_inc(sg_done, 1)
                act.wait_ge(pj_done, 5 * t + 5)
                if not first(t, 1):
                    act.wait_ge(st_v, 16 * t)
                act.activation(v_sb[:, :], pj[:, 4, :], ACT.Copy, scale=rstd[:, b:b + 1]).then_inc(v_done, 1)
                if not first(t, 1):
                    ln_norm(t - 1)

            tiles(act, body)
            ln_out(PT - 1)
            ln_norm(PT)
            ln_out(PT)

        @block.vector
        def _(dve):
            def x_rest(t, b):
                dve.wait_ge(xt_hi_done, t + 1)
                dve.tensor_tensor(xt_lo[:, b, :, :], pxt[:, :, :], xt_hi[:, b, :, :].bitcast(F32),
                                  ALU.subtract).then_inc(xt_lo_done, 1)

            dve.wait_ge(const_dma, 16 * NCONST)
            for n, (c, k) in enumerate(pieces):
                dve.wait_ge(w_hi_done, n + 1)
                dve.scalar_tensor_tensor(w_lo[:, k, c * C:(c + 1) * C], w_raw[:, n % RAW, :], gcol[:, k:k + 1],
                                         w_hi[:, k, c * C:(c + 1) * C].bitcast(F32), ALU.mult,
                                         ALU.subtract).then_inc(w_lo_done, 1)
                if n == 1:
                    x_rest(0, 0)

            def taps(t, lo, hi):
                if lo == 0:
                    dve.wait_ge(ut_done, t + 1)
                    if first(t, 1):
                        dve.wait_ge(w_lo_done, NPIECE)
                    else:
                        dve.wait_ge(ln1_ps, t)
                for j in range(lo, hi):
                    for n, a in enumerate(DVE_CT):
                        if j == 0:
                            dve.tensor_scalar(conv[:, a, :], ut[:, a, 0:P], cw[:, a, 0:1], cb[:, a:a + 1],
                                              ALU.mult, ALU.add).then_inc(tap_dve, 1)
                        else:
                            dve.wait_ge(tap_dve, t * ND + len(DVE_CT) * (j - 1) + n + 1)
                            dve.scalar_tensor_tensor(conv[:, a, :], ut[:, a, j:j + P], cw[:, a, j:j + 1],
                                                     conv[:, a, :], ALU.mult, ALU.add).then_inc(tap_dve, 1)

            def heads(ap):
                return ap.rearrange("p (h d) -> p h d", h=NH)

            def ln_stats(t):
                dve.wait_ge(ln1_ps, t + 1)
                if not first(t, 1):
                    dve.wait_ge(ln_rs, t)
                dve.bn_stats(bnst, pm[:, :]).then_inc(ln_stat, 1)
                hold(dve, ln_stat, 2 * t + 1, passed_dve)
                dve.bn_aggr(mv, bnst).then_inc(ln_stat, 1)

            def body(t, b):
                sample = isinstance(t, int) and t == PT
                if not first(t, 1):
                    taps(t - 1, 0, 10)
                dve.wait_ge(pj_done, 5 * t + 2)
                dve.wait_ge(sg_done, 3 * t + 1)
                if not first(t, 1):
                    dve.wait_ge(ut_ps, t)
                    dve.wait_ge(st_u, 16 * t)
                dve.scalar_tensor_tensor(u[:, :], pj[:, 0, :], rstd[:, b:b + 1], tmp[:, :],
                                         ALU.mult, ALU.mult).then_inc(u_done, 1)
                dve.wait_ge(u_done, t + 1)
                dve.sem_inc(tmp_read, 1)
                if not sample:
                    x_rest(t + 1, 1 - b)
                if not first(t, 1):
                    taps(t - 1, 10, 21)
                for n, (c, ms, r, dst) in enumerate(((2, msq, rq, q_sb), (3, msk, rk, k_sb))):
                    dve.wait_ge(sg_done, 3 * t + 2 + n)
                    if not first(t, 1):
                        dve.wait_ge(r_done, 2 * t - 1 + n)
                    dve.tensor_reduce(ms, heads(tmp[:, :]), AX.X, ALU.add).then_inc(ms_done, 1)
                    dve.wait_ge(ms_done, 2 * t + n + 1)
                    dve.sem_inc(tmp_read, 1)
                    dve.wait_ge(r_done, 2 * t + n + 1)
                    if not first(t, 1):
                        dve.wait_ge(st_q if n == 0 else st_k, 16 * t)
                    dve.tensor_tensor(heads(dst[:, :]), heads(pj[:, c, :]),
                                      r.unsqueeze(2).broadcast_to([P, NH, HD]), ALU.mult).then_inc(qk_done, 1)
                    if n == 0 and not first(t, 1):
                        taps(t - 1, 21, W)
                if not first(t, 1):
                    ln_stats(t - 1)

            tiles(dve, body)
            taps(PT, 0, W)
            ln_stats(PT)

        @block.gpsimd
        def _(pool):
            pool.memset(ident[:, :], 0.0).then_inc(ident_done, 1)
            pool.memset(mhalf[:, :], -0.5).then_inc(ident_done, 1)
            hold(pool, ident_done, 1, passed)
            pool.affine_select(out=ident[:, :], in_=ident[:, :], compare_op=ALU.not_equal, fill=1.0, base=0,
                               pattern=[[-1, P]], channel_multiplier=1).then_inc(ident_done, 1)
            pool.memset(ut[:, :, 0:HIST], 0.0).then_inc(hist_done, 1)
            hold(pool, const_dma, 16 * NCONST, passed)
            hold(pool, ident_done, 3, passed)

            def inverse_rms(t, b):
                hold(pool, sq_done, t + 1, passed)
                if not first(t, 2):
                    hold(pool, v_done, t - 1, passed)
                    hold(pool, u_done, t - 1, passed)
                pool.tensor_scalar(rtmp, ss[:, b:b + 1], 1.0 / D, EPS, ALU.mult, ALU.add).then_inc(rstd_step, 1)
                hold(pool, rstd_step, 2 * t + 1, passed)
                pool.tensor_tensor(rstd[:, b:b + 1], rtmp, mhalf[:, 0:1], ALU.pow).then_inc(rstd_step, 1)
                hold(pool, rstd_step, 2 * t + 2, passed)
                pool.tensor_scalar(rs2[:, b:b + 1], rstd[:, b:b + 1], rstd[:, b:b + 1], 1.0 / HD,
                                   ALU.mult, ALU.mult).then_inc(rstd_done, 1)

            def head_rms(t, b, n, ms, r):
                hold(pool, ms_done, 2 * t + n + 1, passed)
                if not first(t, 1):
                    hold(pool, qk_done, 2 * t - 1 + n, passed)
                pool.tensor_scalar(rqt, ms, rs2[:, b:b + 1], EPS, ALU.mult, ALU.add).then_inc(r_step, 1)
                hold(pool, r_step, 4 * t + 2 * n + 1, passed)
                pool.tensor_tensor(r, rqt, mhalf[:, :], ALU.pow).then_inc(r_step, 1)
                hold(pool, r_step, 4 * t + 2 * n + 2, passed)
                pool.tensor_scalar(r, r, rstd[:, b:b + 1], None, ALU.mult).then_inc(r_done, 1)
                hold(pool, r_done, 2 * t + n + 1, passed)

            def taps(t, lo, hi):
                base, a = t * NP, POOL_CT
                if lo == 0:
                    hold(pool, ut_done, t + 1, passed)
                    if first(t, 1):
                        hold(pool, w_lo_done, NPIECE, passed)
                    else:
                        hold(pool, ln1_ps, t, passed)
                    pool.tensor_scalar(conv[:, a, :], ut[:, a, 0:P], cw[:, a, 0:1], cb[:, a:a + 1],
                                       ALU.mult, ALU.add).then_inc(tap_pool, 1)
                for j in range(max(lo, 1), hi):
                    if j > 2:
                        hold(pool, tap_pool, base + 2 * j - 3, passed)
                    pool.tensor_scalar(prod[:, j % 2, :], ut[:, a, j:j + P], cw[:, a, j:j + 1], None,
                                       ALU.mult).then_inc(tap_pool, 1)
                    hold(pool, tap_pool, base + 2 * j, passed)
                    pool.tensor_tensor(conv[:, a, :], conv[:, a, :], prod[:, j % 2, :],
                                       ALU.add).then_inc(tap_pool, 1)
                if hi == W:
                    hold(pool, tap_pool, base + NP, passed)

            def ln_scale(t):
                hold(pool, ln_stat, 2 * t + 2, passed)
                if not first(t, 1):
                    hold(pool, normed_done, t, passed)
                pool.tensor_scalar(lnr, mv[:, 1:2], EPS, None, ALU.add).then_inc(ln_step, 1)
                hold(pool, ln_step, 2 * t + 1, passed)
                pool.tensor_tensor(lnr, lnr, mhalf[:, 0:1], ALU.pow).then_inc(ln_step, 1)
                hold(pool, ln_step, 2 * t + 2, passed)
                pool.tensor_scalar(lnm, mv[:, 0:1], lnr, -1.0, ALU.mult, ALU.mult).then_inc(ln_rs, 1)

            def ln_swish(t):
                hold(pool, act_ln, t + 1, passed)
                pool.tensor_tensor(swish, swish, sig, ALU.mult).then_inc(swish_done, 1)

            inverse_rms(0, 0)

            def body(t, b):
                sample = isinstance(t, int) and t == PT
                if not first(t, 1):
                    taps(t - 1, 0, 8)
                if not first(t, 2):
                    ln_swish(t - 2)
                if not sample:
                    inverse_rms(t + 1, 1 - b)
                if not first(t, 1):
                    taps(t - 1, 8, 21)
                head_rms(t, b, 0, msq, rq)
                if not first(t, 1):
                    taps(t - 1, 21, W)
                head_rms(t, b, 1, msk, rk)
                hold(pool, qk_done, 2 * t + 2, passed)
                pool.tensor_tensor(k_sb[:, :].rearrange("p (h d) -> p h d", h=NH),
                                   k_sb[:, :].rearrange("p (h d) -> p h d", h=NH),
                                   gk[:, :].unsqueeze(1).broadcast_to([P, NH, HD]), ALU.mult).then_inc(kg_done, 1)
                if not first(t, 1):
                    ln_scale(t - 1)

            tiles(pool, body)
            taps(PT, 0, W)
            ln_swish(PT - 1)
            ln_scale(PT)
            ln_swish(PT)
    return sems


NKT = PT + PAST // P + 1
HG = NH // 2
GC = HG * HD
MAXU = 8
SCALE = HD ** -0.5


def key_tiles(t):
    return (0, t + 1) if t < PT else (PT, PAST // P + 1)


def attention_steps():
    steps = []
    for t in range(NT + 3):
        if t < NT:
            _, n = key_tiles(t)
            half = n if n <= MAXU else n // 2
            parts = [(0, n, False)] if n <= MAXU else [(half, n, False), (0, half, True)]
            units = [(t, h, lo, hi, more) for h in range(HG) for lo, hi, more in parts]
        else:
            units = [None] * 4
        per = len(units) // 4
        for i, unit in enumerate(units):
            steps.append((t, i // per if i % per == 0 else None, unit, i == 3))
    return steps


def phase_attend(nc, io, scr, g, logits):
    with ExitStack() as ctx:
        pre = f"p2{g}_"

        def sb(name, shape, dt=F32):
            return ctx.enter_context(nc.sbuf_tensor(pre + name, shape, dt))

        def ps(name, shape):
            return ctx.enter_context(nc.psum_tensor(pre + name, shape, F32))

        sems = []

        def sem(name):
            sems.append(nc.alloc_semaphore(pre + name))
            return sems[-1]

        NB = 4 - g
        NA = 4
        UW = MAXU * P
        kt_sb = sb("kt", [P, HG, NKT * P], F32R)
        v_sb = sb("v", [P, NKT, GC])
        wo_hi = sb("wo_hi", [P, CT, D], F32R)
        wo_lo = sb("wo_lo", [P, CT, D], F32R)
        q_hi = sb("q_hi", [P, 2, HG, P], F32R)
        q_lo = sb("q_lo", [P, 2, HG, P], F32R)
        keep = sb("keep", [P, NB, UW + 4])
        wgt = sb("wgt", [P, NB, UW])
        at = sb("at", [P, NA, 4 * P])
        kd = sb("kd", [P, 2, HG, 2, HD])
        qd = sb("qd", [P, 2, HG, 2, HD])
        m_hi = sb("m_hi", [P, 2, CT, P], F32R)
        m_lo = sb("m_lo", [P, 2, CT, P], F32R)
        o_raw = sb("o_raw", [P, 2, GC])
        o_sq = sb("o_sq", [P, GC])
        o_n = sb("o_n", [P, 4, GC])
        y = sb("y", [P, 3, D])
        ident = sb("ident", [P, P])
        identb = sb("identb", [P, P], mybir.dt.bfloat16)
        mask = sb("mask", [P, P], mybir.dt.bfloat16)
        gq = sb("gq", [P, 1])
        go = sb("go", [P, CT])
        st = sb("st", [P, 40])
        oms, orr, ort = st[:, 0:4], st[:, 4:8], st[:, 8:12]
        ss, rt, rstd = st[:, 12:13], st[:, 13:14], st[:, 14:15]
        mhalf = sb("mhalf", [P, 4])
        if g == 0:
            c_ld = sb("c_ld", [P, 2, CT, P])
        else:
            o_a = sb("o_a", [P, 2, GC])
            g2 = sb("g2", [P, D])
            h2 = sb("h2", [P, 2, D])
            h2t = sb("h2t", [P, KT, P])
            wr = sb("wr", [P, KT, NR])
        raw = [wgt[:, 0, :], wgt[:, 1, :], wgt[:, 2, :], keep[:, 0, 0:UW]]

        zp = ps("zp", [P, 2, UW])
        tp = ps("tp", [P, 2, 4 * P])
        op = ps("op", [P, 4 * P])
        mp = ps("mp", [P, 4 * P])

        ready, const_in, raw_in = sem("ready"), sem("const_in"), [sem(f"raw_in{i}") for i in range(CT)]
        wo_hi_done, wo_lo_done = sem("wo_hi_done"), sem("wo_lo_done")
        k_in, q_in = [sem("k_in0"), sem("k_in1")], [sem("q_in0"), sem("q_in1")]
        mp_full, mp_free = sem("mp_full"), sem("mp_free")
        k_hi_done, k_done, q_hi_done, q_done = sem("k_hi_done"), sem("k_done"), sem("q_hi_done"), sem("q_done")
        z_done, sig_done, edge_done, scan_done, a_done = (sem("z_done"), sem("sig_done"), sem("edge_done"),
                                                          sem("scan_done"), sem("a_done"))
        t_done, cp_dve, cp_act, av_done = sem("t_done"), sem("cp_dve"), sem("cp_act"), sem("av_done")
        o_out, o_sq_done, o_ms, o_step, o_done = (sem("o_out"), sem("o_sq_done"), sem("o_ms"), sem("o_step"),
                                                  sem("o_done"))
        m_in, m_hi_done, m_done, wo_done = ([sem("m_in0"), sem("m_in1")], sem("m_hi_done"), sem("m_done"),
                                            sem("wo_done"))
        y_in = [sem(f"y_in{i}") for i in range(3)]
        y_done = sem("y_done")
        st_y, st_o, st_h = [[sem(f"st_{x}{i}") for i in range(n)] for x, n in (("y", 3), ("o", 4), ("h", 2))]
        ss_done, rs_step, h2_step, h2_done = sem("ss_done"), sem("rs_step"), sem("h2_step"), sem("h2_done")
        h2t_done, rt_done, lg_done = sem("h2t_done"), sem("rt_done"), sem("lg_done")

        steps = attention_steps()
        units = [u for _, _, u, _ in steps if u]
        n_of = {u: i for i, u in enumerate(units)}
        last_of = {u[0]: i for i, u in enumerate(units)}
        halves, base = [], []
        for i, (_, _, lo, hi, _) in enumerate(units):
            base.append(len(halves))
            halves += [(i, a, min(a + 4, hi)) for a in range(lo, hi, 4)]
        by_act = [n % 4 == 3 for n in range(len(halves))]
        end_half = {t: base[i] + sum(1 for x in halves if x[0] == i) for t, i in last_of.items()}

        def jobs(t, slot):
            out = []
            if slot == 0 and t + 1 < PT:
                out.append(("k", t + 1))
            if slot == 0 and g == 1 and 0 <= t - 2 < NT:
                out.append(("mix", t - 2))
            if slot == 1 and t + 1 < NT:
                out.append(("q", t + 1))
            if slot == 2 and 7 <= t < PT:
                out.append(("k", PT + t - 7))
            lag = 0 if g == 0 else 2
            if slot in (2, 3) and 0 <= t - lag < NT:
                out.append(("wo", t - lag, slot - 2))
            if slot == 3 and g == 1 and 0 <= t - 3 < NT:
                out += [("h2t", t - 3, 0), ("h2t", t - 3, 1), ("route", t - 3)]
            return out

        order = [("k", 0), ("q", 0)]
        for t, slot, _, _ in steps:
            if slot is not None:
                order += jobs(t, slot)
        use = {job: n for n, job in enumerate(order)}
        k_order = [job[1] for job in order if job[0] == "k"]
        k_at = {kt: n for n, kt in enumerate(k_order)}

        def copies_before(n, act):
            return sum(1 for x in by_act[:n] if x == act)

        def copy_halves(eng, u, act):
            for n in range(base[u], base[u + 1] if u + 1 < len(units) else len(halves)):
                if by_act[n] != act:
                    continue
                _, a, e = halves[n]
                eng.wait_ge(t_done, n + 1)
                if n >= NA:
                    eng.wait_ge(av_done, n - NA + 1)
                dst, src = at[:, n % NA, 0:(e - a) * P], tp[:, n % 2, 0:(e - a) * P]
                if act:
                    eng.activation(dst, src, ACT.Copy).then_inc(cp_act, 1)
                else:
                    eng.tensor_copy(dst, src).then_inc(cp_dve, 1)

        block = ctx.enter_context(nc.Block())
        c0 = g * GC

        @block.sync
        def _(sp):
            sp.dma_start(gq[:, :], io["q_norm_g"]).then_inc(const_in, 16)
            sp.dma_start(go[:, :], io["attn_out_g"]).then_inc(const_in, 16)
            if g == 1:
                sp.dma_start(g2[:, :], io["norm_ffn_g"].partition_broadcast(P)).then_inc(const_in, 16)
                sp.dma_start(wr[:, :, :], io["w_router"]).then_inc(const_in, 16)

            def load_k(kt):
                n = k_at[kt]
                if kt < PT:
                    ksrc, vsrc, r = io["k_out"], io["v_out"], kt
                elif kt < NKT - 1:
                    ksrc, vsrc, r = io["cache_k"], io["cache_v"], kt - PT
                else:
                    ksrc, vsrc, r = io["k_out"], io["v_out"], PT
                if n >= 2:
                    sp.wait_ge(mp_full, use[("k", k_order[n - 2])] + 1)
                for a in range(2):
                    sp.dma_start(kd[:, n % 2, :, a, :],
                                 ksrc[r * P:(r + 1) * P, c0:c0 + GC].rearrange("p (h d) -> p h d", h=HG)
                                 ).then_inc(k_in[n % 2], 16)
                sp.dma_start(v_sb[:, kt, :], vsrc[r * P:(r + 1) * P, c0:c0 + GC]).then_inc(k_in[n % 2], 16)

            def load_q(t):
                if t >= 2:
                    sp.wait_ge(mp_full, use[("q", t - 2)] + 1)
                for a in range(2):
                    sp.dma_start(qd[:, t % 2, :, a, :],
                                 scr["q"][t * P:(t + 1) * P, c0:c0 + GC].rearrange("p (h d) -> p h d", h=HG)
                                 ).then_inc(q_in[t % 2], 16)

            def load_mix(t):
                if g == 0:
                    if t >= 2:
                        sp.wait_ge(m_done, t - 1)
                    sp.dma_start(c_ld[:, t % 2, :, :], scr["c"][:, :, t * P:(t + 1) * P]).then_inc(m_in[t % 2], 16)
                else:
                    if t >= 2:
                        sp.wait_ge(mp_full, use[("mix", t - 2)] + 1)
                    sp.dma_start(o_a[:, t % 2, :], scr["o"][t * P:(t + 1) * P, :]).then_inc(m_in[t % 2], 16)

            def load_y(t):
                if t >= 3:
                    sp.wait_ge(st_y[t % 3], 16 * (t // 3))
                    if g == 1:
                        sp.wait_ge(h2_step, t - 2)
                src = io["x"] if g == 0 else scr["y"]
                sp.dma_start(y[:, t % 3, :], src[t * P:(t + 1) * P, :]).then_inc(y_in[t % 3], 16)

            load_k(0)
            load_q(0)
            for k in range(CT):
                sp.dma_start(raw[k], io["w_out"][(g * CT + k) * P:(g * CT + k + 1) * P, :]).then_inc(raw_in[k], 16)
            load_k(1)
            load_q(1)
            load_mix(0)
            load_y(0)
            lag = 0 if g == 0 else 2
            for t in range(NT + 3):
                if t + 2 < PT:
                    load_k(t + 2)
                if t + 2 < NT:
                    load_q(t + 2)
                if 6 <= t < PT - 1:
                    load_k(PT + t - 6)
                if 0 <= t - lag + 1 < NT and t - lag + 1 > 0:
                    load_mix(t - lag + 1)
                    load_y(t - lag + 1)
                if 0 <= t - 1 < NT and g == 0:
                    sp.wait_ge(o_done, t)
                    sp.dma_start(scr["o"][(t - 1) * P:t * P, :], o_n[:, (t - 1) % 4, :]).then_inc(st_o[(t - 1) % 4], 16)
                if 0 <= t - lag < NT:
                    sp.wait_ge(y_done, 2 * (t - lag) + 2)
                    dst = scr["y"] if g == 0 else io["y_out"]
                    sp.dma_start(dst[(t - lag) * P:(t - lag + 1) * P, :], y[:, (t - lag) % 3, :]
                                 ).then_inc(st_y[(t - lag) % 3], 16)
                    if g == 1:
                        sp.wait_ge(h2_done, t - lag + 1)
                        sp.dma_start(scr["h2"][(t - lag) * P:(t - lag + 1) * P, :],
                                     h2[:, (t - lag) % 2, :]).then_inc(st_h[(t - lag) % 2], 16)
            for slots in (st_y, st_o) if g == 0 else (st_y, st_h):
                for i, s in enumerate(slots):
                    sp.wait_ge(s, 16 * len(range(i, NT, len(slots))))

        @block.tensor
        def _(pe):
            def job(j):
                if use[j]:
                    pe.wait_ge(mp_free, use[j])
                if j[0] in "kq":
                    n = k_at[j[1]] if j[0] == "k" else j[1]
                    if j[0] == "k":
                        pe.wait_ge(k_in[n % 2], 48 * (n // 2 + 1))
                    else:
                        pe.wait_ge(q_in[n % 2], 32 * (n // 2 + 1))
                    src = kd if j[0] == "k" else qd
                    for h in range(HG):
                        last = pe.transpose(mp[:, h * P:(h + 1) * P],
                                            src[:, n % 2, h, :, :].rearrange("p a d -> p (a d)"), ident[:, :])
                elif j[0] == "mix":
                    t = j[1]
                    pe.wait_ge(m_in[t % 2], 16 * (t // 2 + 1))
                    pe.wait_ge(o_done, t + 1)
                    for k in range(CT):
                        src = o_a[:, t % 2, :] if k < 2 else o_n[:, t % 4, :]
                        last = pe.transpose(mp[:, k * P:(k + 1) * P], src[:, (k % 2) * P:(k % 2 + 1) * P], ident[:, :])
                elif j[0] == "wo":
                    t, c = j[1], j[2]
                    pe.wait_ge(m_done, t + 1)
                    pe.wait_ge(m_hi_done, t + 1)
                    pe.wait_ge(wo_lo_done, CT)
                    pe.wait_ge(wo_hi_done, CT)
                    n = 0
                    for k in range(CT):
                        for ma, wa in ((m_hi, wo_hi), (m_hi, wo_lo), (m_lo, wo_hi)):
                            last = pe.matmul(mp[:, :], ma[:, t % 2, k, :], wa[:, k, c * C:(c + 1) * C],
                                             start=(n == 0), stop=(n == 3 * CT - 1))
                            n += 1
                    last.then_inc(wo_done, 1)
                    pe.wait_ge(wo_done, 2 * t + c + 1)
                    pe.sem_inc(mp_full, 1)
                    return
                elif j[0] == "h2t":
                    t, c = j[1], j[2]
                    pe.wait_ge(h2_done, t + 1)
                    for k in range(4):
                        last = pe.transpose(mp[:, k * P:(k + 1) * P],
                                            h2[:, t % 2, (4 * c + k) * P:(4 * c + k + 1) * P], ident[:, :])
                else:
                    t = j[1]
                    pe.wait_ge(h2t_done, 2 * t + 2)
                    for k in range(KT):
                        last = pe.matmul(mp[:, 0:NR], h2t[:, k, :], wr[:, k, :], start=(k == 0), stop=(k == KT - 1))
                last.then_inc(mp_full, 1)

            def scores(u):
                t, h, lo, hi, _ = unit = units[u]
                kb, n = key_tiles(t)
                if u >= 2:
                    pe.wait_ge(sig_done, u - 1)
                pe.wait_ge(q_done, t + 1)
                pe.wait_ge(k_done, k_at[kb + hi - 1] + 1)
                for a in range(lo, hi, 4):
                    e = min(a + 4, hi)
                    dst = zp[:, u % 2, (a - lo) * P:(e - lo) * P]
                    keys = kt_sb[:, h, (kb + a) * P:(kb + e) * P]
                    pe.matmul(dst, q_hi[:, t % 2, h, :], keys, start=True, stop=False)
                    if e == n:
                        pe.matmul(zp[:, u % 2, (n - 1 - lo) * P:(n - lo) * P], identb[:, :], mask[:, :],
                                  start=False, stop=False, skip_group_check=True)
                    last = pe.matmul(dst, q_lo[:, t % 2, h, :], keys, start=False, stop=True)
                last.then_inc(z_done, 1)

            def transpose_weights(u):
                lo = units[u][2]
                pe.wait_ge(a_done, u + 1)
                for n in range(base[u], end_of(u)):
                    _, a, e = halves[n]
                    if n >= 2:
                        pe.wait_ge(cp_act if by_act[n - 2] else cp_dve, copies_before(n - 1, by_act[n - 2]))
                    for i in range(a, e):
                        last = pe.transpose(tp[:, n % 2, (i - a) * P:(i - a + 1) * P],
                                            wgt[:, u % NB, (i - lo) * P:(i - lo + 1) * P], ident[:, :])
                    last.then_inc(t_done, 1)

            def end_of(u):
                return base[u + 1] if u + 1 < len(units) else len(halves)

            def values(u):
                t, h, lo, hi, _ = units[u]
                kb, _ = key_tiles(t)
                if h == 0 and u == first_unit(t):
                    if t:
                        pe.wait_ge(o_out, t)
                for n in range(base[u], end_of(u)):
                    _, a, e = halves[n]
                    pe.wait_ge(cp_act if by_act[n] else cp_dve, copies_before(n + 1, by_act[n]))
                    for i in range(a, e):
                        begin = u == first_unit(t) and n == base[u] and i == a
                        end = u == last_of[t] and n == end_of(u) - 1 and i == e - 1
                        last = pe.matmul(op[:, h * HD:(h + 1) * HD], at[:, n % NA, (i - a) * P:(i - a + 1) * P],
                                         v_sb[:, kb + i, h * HD:(h + 1) * HD], start=begin, stop=end,
                                         skip_group_check=True)
                    last.then_inc(av_done, 1)

            def first_unit(t):
                return last_of[t - 1] + 1 if t else 0

            pe.wait_ge(ready, 5)
            job(("k", 0))
            job(("q", 0))
            for s, (t, slot, unit, out) in enumerate(steps):
                if unit:
                    scores(n_of[unit])
                if slot is not None:
                    for j in jobs(t, slot):
                        job(j)
                if s >= 2 and steps[s - 2][2]:
                    transpose_weights(n_of[steps[s - 2][2]])
                if s >= 3 and steps[s - 3][2]:
                    values(n_of[steps[s - 3][2]])

        @block.scalar
        def _(act):
            act.wait_ge(const_in, 16 * (2 if g == 0 else 4))

            def job(j):
                act.wait_ge(mp_full, use[j] + 1)
                if j[0] == "k":
                    if k_at[j[1]]:
                        pass
                    act.activation(kt_sb[:, :, j[1] * P:(j[1] + 1) * P],
                                   mp[:, :].rearrange("p (h t) -> p h t", h=HG), ACT.Copy).then_inc(k_hi_done, 1)
                elif j[0] == "q":
                    t = j[1]
                    if t >= 2:
                        act.wait_ge(z_done, last_of[t - 2] + 1)
                    act.activation(q_hi[:, t % 2, :, :], mp[:, :].rearrange("p (h t) -> p h t", h=HG),
                                   ACT.Copy, scale=gq[:, 0:1]).then_inc(q_hi_done, 1)
                elif j[0] == "mix":
                    t = j[1]
                    if t >= 2:
                        act.wait_ge(wo_done, 2 * t - 2)
                    act.activation(m_hi[:, t % 2, :, :], mp[:, :].rearrange("p (h t) -> p h t", h=CT),
                                   ACT.Copy).then_inc(m_hi_done, 1)
                elif j[0] == "h2t":
                    t, c = j[1], j[2]
                    if t and c == 0:
                        act.wait_ge(mp_full, use[("route", t - 1)] + 1)
                    act.activation(h2t[:, 4 * c:4 * c + 4, :], mp[:, :].rearrange("p (h t) -> p h t", h=4),
                                   ACT.Copy).then_inc(h2t_done, 1)
                    act.wait_ge(h2t_done, 2 * t + c + 1)
                    act.sem_inc(mp_free, 1)

            for k in range(CT):
                act.wait_ge(raw_in[k], 16)
                if g == 0:
                    act.activation(wo_hi[:, k, :], raw[k], ACT.Copy).then_inc(wo_hi_done, 1)
                else:
                    act.activation(wo_hi[:, k, :], raw[k], ACT.Copy, scale=go[:, k:k + 1]).then_inc(wo_hi_done, 1)
            job(("k", 0))
            job(("q", 0))
            act.wait_ge(wo_lo_done, CT)
            for s, (t, slot, unit, out) in enumerate(steps):
                if unit:
                    u = n_of[unit]
                    w = (unit[3] - unit[2]) * P
                    act.wait_ge(z_done, u + 1)
                    if u >= NB:
                        act.wait_ge(t_done, base[u - NB + 1])
                        act.wait_ge(edge_done, u - NB + 2)
                        act.wait_ge(scan_done, u - NB + 2)
                    act.activation(wgt[:, u % NB, 0:w], zp[:, u % 2, 0:w], ACT.Sigmoid, scale=SCALE)
                    act.activation(keep[:, u % NB, 0:w], zp[:, u % 2, 0:w], ACT.Sigmoid,
                                   scale=-SCALE).then_inc(sig_done, 1)
                if slot is not None:
                    for j in jobs(t, slot):
                        if j[0] in ("k", "q", "mix", "h2t"):
                            job(j)
                if out and 0 <= t - 1 < NT:
                    act.wait_ge(av_done, end_half[t - 1])
                    if t >= 3:
                        act.wait_ge(o_done, t - 2)
                    act.activation(o_raw[:, (t - 1) % 2, :], op[:, 0:GC], ACT.Copy).then_inc(o_out, 1)
                if slot == 3 and g == 1 and 0 <= t - 2 < NT:
                    act.wait_ge(y_done, 2 * (t - 2) + 2)
                    if t >= 3:
                        act.wait_ge(rs_step, 2 * (t - 2))
                    if t >= 4:
                        act.wait_ge(st_h[t % 2], 16 * (t // 2 - 1))
                        act.wait_ge(mp_full, use[("h2t", t - 4, 1)] + 1)
                    act.activation(h2[:, t % 2, :], y[:, (t - 2) % 3, :], ACT.Square,
                                   accum_out=ss).then_inc(ss_done, 1)
                if s >= 2 and steps[s - 2][2]:
                    copy_halves(act, n_of[steps[s - 2][2]], True)

        @block.vector
        def _(dve):
            dve.wait_ge(const_in, 16 * (2 if g == 0 else 4))

            def heads(ap):
                return ap.rearrange("p (h t) -> p h t", h=HG)

            def job(j):
                if j[0] == "k":
                    dve.wait_ge(k_hi_done, k_at[j[1]] + 1)
                    low = kt_sb[64:128, :, j[1] * P:(j[1] + 1) * P]
                    dve.tensor_tensor(low, heads(mp[64:128, :]), low.bitcast(F32), ALU.subtract).then_inc(k_done, 1)
                    dve.wait_ge(k_done, k_at[j[1]] + 1)
                elif j[0] == "q":
                    t = j[1]
                    dve.wait_ge(q_hi_done, t + 1)
                    dve.scalar_tensor_tensor(q_lo[:, t % 2, :, :].rearrange("p h t -> p (h t)"), mp[:, :], gq[:, 0:1],
                                             q_hi[:, t % 2, :, :].rearrange("p h t -> p (h t)").bitcast(F32),
                                             ALU.mult, ALU.subtract).then_inc(q_done, 1)
                    dve.wait_ge(q_done, t + 1)
                elif j[0] == "mix":
                    t = j[1]
                    dve.wait_ge(m_hi_done, t + 1)
                    dve.tensor_tensor(m_lo[:, t % 2, :, :], heads(mp[:, :]), m_hi[:, t % 2, :, :].bitcast(F32),
                                      ALU.subtract).then_inc(m_done, 1)
                    dve.wait_ge(m_done, t + 1)
                elif j[0] == "wo":
                    t, c = j[1], j[2]
                    dve.wait_ge(mp_full, use[j] + 1)
                    dve.wait_ge(y_in[t % 3], 16 * (t // 3 + 1))
                    dve.tensor_tensor(y[:, t % 3, c * C:(c + 1) * C], mp[:, :], y[:, t % 3, c * C:(c + 1) * C],
                                      ALU.add).then_inc(y_done, 1)
                    dve.wait_ge(y_done, 2 * t + c + 1)
                elif j[0] == "route":
                    t = j[1]
                    dve.wait_ge(mp_full, use[j] + 1)
                    dve.tensor_copy(logits[:, t, :], mp[:, 0:NR]).then_inc(lg_done, 1)
                    dve.wait_ge(lg_done, t + 1)
                else:
                    return
                dve.sem_inc(mp_free, 1)

            for k in range(CT):
                dve.wait_ge(wo_hi_done, k + 1)
                if g == 0:
                    dve.tensor_tensor(wo_lo[:, k, :], raw[k], wo_hi[:, k, :].bitcast(F32),
                                      ALU.subtract).then_inc(wo_lo_done, 1)
                else:
                    dve.scalar_tensor_tensor(wo_lo[:, k, :], raw[k], go[:, k:k + 1],
                                             wo_hi[:, k, :].bitcast(F32), ALU.mult, ALU.subtract).then_inc(wo_lo_done, 1)
            job(("k", 0))
            job(("q", 0))
            for s, (t, slot, unit, out) in enumerate(steps):
                if unit:
                    u = n_of[unit]
                    w = (unit[3] - unit[2]) * P
                    dve.wait_ge(sig_done, u + 1)
                    dve.wait_ge(edge_done, u + 1)
                    part = keep[:, u % NB, w:0:-1]
                    if unit[4]:
                        dve.wait_ge(scan_done, u)
                    dve.tensor_tensor_scan(part, part, part, keep[:, (u - 1) % NB, 1:2] if unit[4] else 1.0,
                                           ALU.mult, ALU.bypass).then_inc(scan_done, 1)
                if slot is not None:
                    for j in jobs(t, slot):
                        job(j)
                if out and 0 <= t - 1 < NT:
                    dve.wait_ge(o_sq_done, t)
                    if t >= 2:
                        dve.wait_ge(o_step, 2 * (t - 1))
                    dve.tensor_reduce(oms, o_sq[:, :].rearrange("p (h d) -> p h d", h=HG), AX.X,
                                      ALU.add).then_inc(o_ms, 1)
                if s >= 2 and steps[s - 2][2]:
                    copy_halves(dve, n_of[steps[s - 2][2]], False)

        @block.gpsimd
        def _(pool):
            pool.memset(ident[:, :], 0.0).then_inc(ready, 1)
            pool.memset(mask[:, :], 0.0).then_inc(ready, 1)
            pool.memset(mhalf[:, :], -0.5)
            pool.wait_ge(ready, 2)
            pool.affine_select(out=ident[:, :], in_=ident[:, :], compare_op=ALU.not_equal, fill=1.0, base=0,
                               pattern=[[-1, P]], channel_multiplier=1).then_inc(ready, 1)
            pool.affine_select(out=mask[:, :], in_=mask[:, :], compare_op=ALU.is_gt, fill=-1e30, base=0,
                               pattern=[[-1, P]], channel_multiplier=1).then_inc(ready, 1)
            pool.wait_ge(ready, 4)
            pool.tensor_copy(identb[:, :], ident[:, :]).then_inc(ready, 1)
            pool.wait_ge(ready, 5)

            def mix(t):
                pool.wait_ge(m_in[t % 2], 16 * (t // 2 + 1))
                if t >= 2:
                    pool.wait_ge(wo_done, 2 * t - 2)
                pool.tensor_copy(m_hi[:, t % 2, :, :], c_ld[:, t % 2, :, :]).then_inc(m_hi_done, 1)
                pool.wait_ge(m_hi_done, t + 1)
                pool.tensor_tensor(m_lo[:, t % 2, :, :], c_ld[:, t % 2, :, :], m_hi[:, t % 2, :, :].bitcast(F32),
                                   ALU.subtract).then_inc(m_done, 1)

            def edge(u):
                unit = units[u]
                w = (unit[3] - unit[2]) * P
                if u >= NB:
                    pool.wait_ge(a_done, u - NB + 1)
                if unit[4]:
                    pool.wait_ge(sig_done, u)
                    pool.tensor_copy(keep[:, u % NB, w:w + 1], keep[:, (u - 1) % NB, 0:1]).then_inc(edge_done, 1)
                else:
                    pool.memset(keep[:, u % NB, w:w + 1], 1.0).then_inc(edge_done, 1)

            pool.wait_ge(wo_lo_done, CT)
            edge(0)
            for s, (t, slot, unit, out) in enumerate(steps):
                if g == 0 and slot == 0 and t < NT:
                    mix(t)
                if unit:
                    u = n_of[unit]
                    w = (unit[3] - unit[2]) * P
                    if u + 1 < len(units):
                        edge(u + 1)
                    pool.wait_ge(scan_done, u + 1)
                    pool.tensor_tensor(wgt[:, u % NB, 0:w], wgt[:, u % NB, 0:w], keep[:, u % NB, 1:w + 1],
                                       ALU.mult).then_inc(a_done, 1)
                if out and 0 <= t - 1 < NT:
                    n = t - 1
                    pool.wait_ge(o_out, t)
                    if n:
                        pool.wait_ge(o_ms, n)
                    pool.tensor_tensor(o_sq[:, :], o_raw[:, n % 2, :], o_raw[:, n % 2, :],
                                       ALU.mult).then_inc(o_sq_done, 1)
                    pool.wait_ge(o_ms, t)
                    pool.tensor_scalar(ort, oms, 1.0 / HD, EPS, ALU.mult, ALU.add).then_inc(o_step, 1)
                    pool.wait_ge(o_step, 2 * n + 1)
                    if n:
                        pool.wait_ge(o_done, n)
                    pool.tensor_tensor(orr, ort, mhalf[:, :], ALU.pow).then_inc(o_step, 1)
                    pool.wait_ge(o_step, 2 * n + 2)
                    if n >= 4:
                        if g == 0:
                            pool.wait_ge(st_o[n % 4], 16 * (n // 4))
                        else:
                            pool.wait_ge(mp_full, use[("mix", n - 4)] + 1)
                    pool.tensor_tensor(o_n[:, n % 4, :].rearrange("p (h d) -> p h d", h=HG),
                                       o_raw[:, n % 2, :].rearrange("p (h d) -> p h d", h=HG),
                                       orr.unsqueeze(2).broadcast_to([P, HG, HD]), ALU.mult).then_inc(o_done, 1)
                if slot == 3 and g == 1 and 0 <= t - 2 < NT:
                    n = t - 2
                    pool.wait_ge(ss_done, n + 1)
                    if n:
                        pool.wait_ge(h2_step, n)
                    pool.tensor_scalar(rt, ss, 1.0 / D, EPS, ALU.mult, ALU.add).then_inc(rs_step, 1)
                    pool.wait_ge(rs_step, 2 * n + 1)
                    pool.tensor_tensor(rstd, rt, mhalf[:, 0:1], ALU.pow).then_inc(rs_step, 1)
                    pool.wait_ge(rs_step, 2 * n + 2)
                    pool.tensor_scalar(h2[:, n % 2, :], y[:, n % 3, :], rstd, None, ALU.mult).then_inc(h2_step, 1)
                    pool.wait_ge(h2_step, n + 1)
                    pool.tensor_tensor(h2[:, n % 2, :], h2[:, n % 2, :], g2[:, :], ALU.mult).then_inc(h2_done, 1)
    return sems


NG, NE = 4, 32
EG = NE // NG
FF = 512
FT = FF // P
HF = FF // 2
PIECES = 12
RING = 16
PAD = NT * P
NBL = NE + 2 * TOK // P + 3
BIG = 1e30


def phase_moe(nc, io, scr, logits):
    with ExitStack() as ctx:
        def sb(name, shape, dt=F32):
            return ctx.enter_context(nc.sbuf_tensor("p3_" + name, shape, dt))

        def ps(name, shape):
            return ctx.enter_context(nc.psum_tensor("p3_" + name, shape, F32))

        sems = []

        def sem(name):
            sems.append(nc.alloc_semaphore("p3_" + name))
            return sems[-1]

        BF = mybir.dt.bfloat16
        iota_i, iota = sb("iota_i", [P, NE], I32), sb("iota", [P, NE])
        gmax, gi, se, psel = (sb(x, [P, NT]) for x in ("gmax", "gi", "se", "psel"))
        gd, geq, ohg = (sb(x, [P, NT, NG]) for x in ("gd", "geq", "ohg"))
        m = sb("m", [P, NT, NE])
        t1 = sb("t1", [P, NT, NE])
        oh = [sb("oh1", [P, NT, NE]), sb("oh2", [P, NT, NE])]
        v = [sb("v1", [P, NT]), sb("v2", [P, NT])]
        ix = [sb("i1", [P, NT]), sb("i2", [P, NT])]
        wt = [sb("w1", [P, NT]), sb("w2", [P, NT])]
        ex = sb("ex", [P, NT])
        chosen = sb("chosen", [P, NT, NE], BF)
        before, ones = sb("before", [P, P], BF), sb("ones", [P, P], BF)
        cum = sb("cum", [P, NT + 1, NE])
        full = sb("full", [P, NT, NE])
        rk, rki, hi = sb("rk", [P, NT]), sb("rki", [P, NT], I32), sb("hi", [P, NT])
        pos = [sb("pos1", [P, NT], I32), sb("pos2", [P, NT], I32)]
        rows = sb("rows", [P, NT, 2, 2], I32)
        empty = sb("empty", [P, NBL, 2], I32)
        nb, nbi = sb("nb", [P, 2, NE]), sb("nbi", [P, NE], I32)
        table = sb("table", [1, 2, NE], I32)
        sel = sb("sel", [P, NT])

        w_hi, w_lo = sb("w_hi", [P, PIECES, 2 * FF], F32R), sb("w_lo", [P, PIECES, 2 * FF], F32R)
        raw = sb("raw", [P, RING, 2 * FF])
        slots = sb("slots", [P, NBL, 2], I32)
        xg = sb("xg", [P, D])
        xt_hi, xt_lo = sb("xt_hi", [P, KT, P], F32R), sb("xt_lo", [P, KT, P], F32R)
        sg, h = sb("sg", [P, FF]), sb("h", [P, FF])
        ht_hi, ht_lo = sb("ht_hi", [P, FT, P], F32R), sb("ht_lo", [P, FT, P], F32R)
        yo = sb("yo", [P, D])
        at_g, at_s = sb("at_g", [P, 1], I32), sb("at_s", [P, 1], I32)
        ident = sb("ident", [P, P])

        xtp = ps("xtp", [P, KT, P])
        dp = ps("dp", [P, 2, 512])
        gp, up = ps("gp", [P, 2, 512]), ps("up", [P, FF])
        htp = ps("htp", [P, FT, P])
        rank_ps, count_ps = xtp[:, :, :].rearrange("p (a k) q -> p a (k q)", a=2), dp
        consts, chain, exped, act_in, chosen_in, chosen_done, ranked, rows_done = (
            sem(x) for x in ("consts", "chain", "exped", "act_in", "chosen_in", "chosen_done", "ranked", "rows_done"))
        filled, zeroed, scattered = sem("filled"), sem("zeroed"), sem("scattered")
        ident_done, zero_yo, ranks_used = sem("ident_done"), sem("zero_yo"), sem("ranks_used")
        at_g_done, at_s_done = sem("at_g_done"), sem("at_s_done")
        table_done, slots_in, passed = sem("table_done"), sem("slots_in"), sem("passed")
        raw_in = [sem(f"raw_in{i}") for i in range(RING)]
        whi_done, wlo_done = sem("whi_done"), sem("wlo_done")
        gathered, added = sem("gathered"), sem("added")
        xt_ps, xh_done, xl_done = sem("xt_ps"), sem("xh_done"), sem("xl_done")
        up_done, g_done, sg_done, h_done = (sem("up_done"), [sem("g_done0"), sem("g_done1")],
                                            [sem("sg_done0"), sem("sg_done1")], [sem("h_done0"), sem("h_done1")])
        ht_ps, hh_done, hl_done = ([sem(f"{x}{i}") for i in range(2)] for x in ("ht_ps", "hh_done", "hl_done"))
        gs_mid, gs_done = [sem("gs_mid0"), sem("gs_mid1")], [sem("gs_done0"), sem("gs_done1")]
        d_done, yo_done = sem("d_done"), sem("yo_done")

        block = ctx.enter_context(nc.Block())

        def pieces(e):
            out = [io[src][bass.ds(e * D + q * 2 * P, 2 * P), :].rearrange("(k p) f -> p k f", p=P)
                   for src in ("w_up", "w_gate") for q in range(KT // 2)]
            return out + [io["w_down"][bass.ds(e * FF + k * P, P), :] for k in range(FT)]

        @block.sync
        def _(sp):
            def load(i, a):
                for p, src in enumerate(pieces(i * 4 + a)):
                    n = a * PIECES + p
                    if not (isinstance(i, int) and n < RING):
                        sp.wait_ge(wlo_done, i * (4 * PIECES) + n - RING + 1)
                    dst = raw[:, n % RING, :]
                    sp.dma_start(dst.rearrange("p (k f) -> p k f", k=2) if p < 2 * KT // 2 else dst,
                                 src).then_inc(raw_in[n % RING], 16)

            sp.wait_ge(consts, 9)
            sp.dma_start(scr["slots"].rearrange("(p b) w -> p (b w)", p=P),
                         empty[:, :, :].rearrange("p b w -> p (b w)")).then_inc(filled, 16)
            sp.dma_start(scr["h2"][PAD:ROWS, :], yo[:, :]).then_inc(zeroed, 16)
            sp.dma_start(io["y_out"][PAD:ROWS, :], yo[:, :]).then_inc(zeroed, 16)
            for a in range(4):
                load(0, a)
            with sp.Fori(1, NE // 4) as i:
                for a in range(4):
                    load(i, a)
            sp.wait_ge(zeroed, 32)

        def experts(eng, block_of):
            with eng.Fori(0, NE // 4 - 1) as i:
                for a in range(4):
                    blocks(eng, i, a, block_of)
            for a in range(4):
                blocks(eng, NE // 4 - 1, a, block_of)

        def blocks(eng, i, a, block_of):
            e = i * 4 + a
            start, end = (eng.value_load(table[0:1, x, bass.ds(e, 1)], min_val=1, max_val=NBL - 2) for x in range(2))
            with eng.If(end > start):
                with eng.Fori(start, end) as b:
                    block_of(b, None)
            block_of(end, None if isinstance(e, int) and e == NE - 1 else (i, a + 1))

        @block.scalar
        def _(act):
            act.wait_ge(act_in, 1)
            act.activation(gd[:, :, :], gd[:, :, :], ACT.Exp).then_inc(exped, 1)
            act.wait_ge(act_in, 2)
            act.activation(ex[:, :], ex[:, :], ACT.Exp).then_inc(exped, 1)

            def lead(at, lo, hi):
                if at is None:
                    return
                i, a = at
                for p in range(lo, hi):
                    n = a * PIECES + p
                    act.wait_ge(raw_in[n % RING], (i * (4 * PIECES // RING) + n // RING + 1) * 16)
                    act.activation(w_hi[:, p, :], raw[:, n % RING, :], ACT.Copy).then_inc(whi_done, 1)

            def x_hi(b):
                act.wait_ge(xt_ps, b + 1)
                act.activation(xt_hi[:, :, :], xtp[:, :, :], ACT.Copy).then_inc(xh_done, 1)

            def sigmoid(b, k):
                act.wait_ge(g_done[k], b + 1)
                act.wait_ge(gs_done[k], b)
                act.activation(sg[:, bass.ts(k, HF)], gp[:, k, 0:HF], ACT.Sigmoid).then_inc(sg_done[k], 1)

            def h_hi(b, k):
                act.wait_ge(ht_ps[k], b + 1)
                act.wait_ge(d_done, b)
                act.activation(ht_hi[:, 2 * k:2 * k + 2, :], htp[:, 2 * k:2 * k + 2, :], ACT.Copy).then_inc(hh_done[k], 1)

            def block_of(b, at):
                if at is not None:
                    act.wait_ge(up_done, b + 1)
                lead(at, 0, 2)
                sigmoid(b, 0)
                lead(at, 2, 3)
                sigmoid(b, 1)
                h_hi(b, 0)
                x_hi(b + 1)
                lead(at, 3, 4)
                h_hi(b, 1)
                lead(at, 4, 6)
                act.wait_ge(d_done, b + 1)
                act.wait_ge(added, b * 16)
                act.activation(yo[:, :], dp[:, :, :].rearrange("p c f -> p (c f)"), ACT.Copy,
                               scale=slots[:, bass.ds(b, 1), 1].bitcast(F32)).then_inc(yo_done, 1)
                lead(at, 6, PIECES)

            for done in (xh_done, *sg_done, *hh_done):
                act.sem_inc(done, 1)
            act.wait_ge(zero_yo, 1)
            act.sem_inc(yo_done, 1)
            lead((0, 0), 0, PIECES)
            x_hi(1)
            act.wait_ge(table_done, 1)
            act.wait_ge(slots_in, 16)
            experts(act, block_of)

        @block.tensor
        def _(pe):
            pe.wait_ge(chosen_done, 1)
            for dst, lhs in ((rank_ps, before), (count_ps, ones)):
                pe.matmul(dst[:, 0, :], lhs[:, :], chosen[:, 0:PT, :].rearrange("p t e -> p (t e)"),
                          start=True, stop=True)
                last = pe.matmul(dst[:, 1, 0:NE], lhs[:, :], chosen[:, PT, :], start=True, stop=True)
            last.then_inc(ranked, 1)

            def transpose_x(b):
                pe.wait_ge(gathered, b * 16)
                pe.wait_ge(xl_done, b)
                for k in range(KT):
                    last = pe.transpose(xtp[:, k, :], xg[:, k * P:(k + 1) * P], ident[:, :])
                last.then_inc(xt_ps, 1)

            def transpose_h(b, k):
                pe.wait_ge(h_done[k], b + 1)
                for f in (2 * k, 2 * k + 1):
                    last = pe.transpose(htp[:, f, :], h[:, f * P:(f + 1) * P], ident[:, :])
                last.then_inc(ht_ps[k], 1)

            def weights(e, groups):
                pe.wait_ge(whi_done, e * PIECES + groups * 4)
                pe.wait_ge(wlo_done, e * PIECES + groups * 4)

            def half_down(c, k, start):
                n = 0
                for f in (2 * k, 2 * k + 1):
                    for ha, wa in ((ht_hi, w_hi), (ht_hi, w_lo), (ht_lo, w_hi)):
                        last = pe.matmul(dp[:, c, :], ha[:, f, :], wa[:, KT + f, c * 512:(c + 1) * 512],
                                         start=(start and n == 0), stop=(not start and n == 5))
                        n += 1
                return last

            def hidden(dst, group, lo, hi):
                n = 0
                for k in range(KT):
                    for xa, wa in ((xt_hi, w_hi), (xt_hi, w_lo), (xt_lo, w_hi)):
                        piece, at = group * (KT // 2) + k // 2, k % 2 * FF
                        last = pe.matmul(dst, xa[:, k, :], wa[:, piece, at + lo:at + hi],
                                         start=(n == 0), stop=(n == 3 * KT - 1))
                        n += 1
                return last

            for done in (xt_ps, up_done, *g_done, *ht_ps, d_done):
                pe.sem_inc(done, 1)
            pe.wait_ge(zero_yo, 1)
            pe.wait_ge(ranks_used, 1)
            transpose_x(1)
            pe.wait_ge(table_done, 1)
            with pe.Fori(0, NE) as e:
                start, end = (pe.value_load(table[0:1, x, bass.ds(e, 1)], min_val=1, max_val=NBL - 2) for x in range(2))
                with pe.Fori(start, end + 1) as b:
                    pe.wait_ge(xh_done, b + 1)
                    pe.wait_ge(xl_done, b + 1)
                    weights(e, 1)
                    pe.wait_ge(h_done[1], b)
                    hidden(up[:, :], 0, 0, FF).then_inc(up_done, 1)
                    weights(e, 2)
                    hidden(gp[:, 0, 0:HF], 1, 0, HF).then_inc(g_done[0], 1)
                    hidden(gp[:, 1, 0:HF], 1, HF, FF).then_inc(g_done[1], 1)
                    pe.wait_ge(hl_done[1], b)
                    transpose_h(b, 0)
                    transpose_x(b + 1)
                    weights(e, 3)
                    pe.wait_ge(hl_done[0], b + 1)
                    pe.wait_ge(yo_done, b)
                    half_down(0, 0, True)
                    transpose_h(b, 1)
                    half_down(1, 0, True)
                    pe.wait_ge(hl_done[1], b + 1)
                    half_down(0, 1, False)
                    half_down(1, 1, False).then_inc(d_done, 1)

        @block.vector
        def _(dve):
            links = [0]

            def link(ins):
                links[0] += 1
                ins.then_inc(chain, 1)
                dve.wait_ge(chain, links[0])

            def tt(out, a, b, op):
                link(dve.tensor_tensor(out, a, b, op))

            def over(ap, n):
                return ap.unsqueeze(2).broadcast_to([P, NT, n])

            def tiled(ap, n):
                return ap.unsqueeze(1).broadcast_to([P, NT, n])

            def first_max(values, n, best, index, one_hot):
                link(dve.tensor_reduce(best, values, AX.X, ALU.max))
                tt(one_hot, values, over(best, n), ALU.is_equal)
                link(dve.scalar_tensor_tensor(one_hot, one_hot, -100.0, tiled(iota[:, 0:n], n), ALU.mult, ALU.add))
                link(dve.tensor_reduce(index, one_hot, AX.X, ALU.min))
                tt(one_hot, one_hot, over(index, n), ALU.is_equal)

            lg, le = logits[:, :, 0:NG], logits[:, :, NG:NR]
            dve.wait_ge(consts, 9)
            link(dve.tensor_copy(iota[:, :], iota_i[:, :]))
            first_max(lg, NG, gmax[:, :], gi[:, :], ohg[:, :, :])
            tt(gd[:, :, :], lg, over(gmax[:, :], NG), ALU.subtract)
            dve.sem_inc(act_in, 1)
            dve.wait_ge(exped, 1)
            link(dve.tensor_reduce(se[:, :], gd[:, :, :], AX.X, ALU.add))
            link(dve.reciprocal(psel[:, :], se[:, :]))
            by_group = m[:, :, :].rearrange("p t (g e) -> p t g e", g=NG)
            for tile in range(NT):
                last = dve.tensor_tensor(by_group[:, tile], le[:, tile, :].rearrange("p (g e) -> p g e", g=NG),
                                         ohg[:, tile, :].unsqueeze(2).broadcast_to([P, NG, EG]), ALU.mult)
            link(last)
            link(dve.tensor_scalar(geq[:, :, :], ohg[:, :, :], BIG, -BIG, ALU.mult, ALU.add))
            for tile in range(NT):
                last = dve.tensor_tensor(by_group[:, tile], by_group[:, tile],
                                         geq[:, tile, :].unsqueeze(2).broadcast_to([P, NG, EG]), ALU.add)
            link(last)
            first_max(m[:, :, :], NE, v[0][:, :], ix[0][:, :], oh[0][:, :, :])
            link(dve.scalar_tensor_tensor(m[:, :, :], oh[0][:, :, :], -2 * BIG, m[:, :, :], ALU.mult, ALU.add))
            first_max(m[:, :, :], NE, v[1][:, :], ix[1][:, :], oh[1][:, :, :])
            tt(chosen[:, :, :], oh[0][:, :, :], oh[1][:, :, :], ALU.add)
            dve.sem_inc(chosen_in, 1)
            tt(ex[:, :], v[1][:, :], v[0][:, :], ALU.subtract)
            dve.sem_inc(act_in, 1)
            dve.wait_ge(exped, 2)
            link(dve.tensor_scalar_add(v[0][:, :], ex[:, :], 1.0))
            link(dve.reciprocal(v[1][:, :], v[0][:, :]))
            tt(wt[0][:, :], v[1][:, :], psel[:, :], ALU.mult)
            tt(wt[1][:, :], wt[0][:, :], ex[:, :], ALU.mult)
            dve.wait_ge(ranked, 1)
            link(dve.memset(cum[:, 0, :], 0.0))
            for tile in range(NT):
                tt(cum[:, tile + 1, :], cum[:, tile, :],
                   count_ps[:, tile // PT, tile % PT * NE:tile % PT * NE + NE], ALU.add)
            tt(full[:, 0:PT, :], cum[:, 0:PT, :], rank_ps[:, 0, :].rearrange("p (t e) -> p t e", e=NE), ALU.add)
            tt(full[:, PT, :], cum[:, PT, :], rank_ps[:, 1, 0:NE], ALU.add)
            dve.sem_inc(ranks_used, 1)
            link(dve.tensor_scalar(nb[:, 0, :], cum[:, NT, :], float(P - 1), None, ALU.add))
            link(dve.tensor_copy(nbi[:, :], nb[:, 0, :]))
            link(dve.tensor_scalar(nbi[:, :], nbi[:, :], 7, None, ALU.logical_shift_right))
            link(dve.tensor_scalar(nbi[:, :], nbi[:, :], 1, None, ALU.max))
            link(dve.tensor_copy(nb[:, 0, :], nbi[:, :]))
            link(dve.tensor_tensor_scan(nb[:, 1, :], nb[:, 0, :], nb[:, 0, :], 1.0, ALU.add, ALU.bypass))
            tt(nb[:, 1, :], nb[:, 1, :], nb[:, 0, :], ALU.subtract)
            link(dve.tensor_copy(table[0:1, 0, :], nb[0:1, 1, :]))
            link(dve.scalar_tensor_tensor(nb[0:1, 0, :], nb[0:1, 0, :], -1.0, nb[0:1, 1, :], ALU.add, ALU.add))
            link(dve.tensor_copy(table[0:1, 1, :], nb[0:1, 0, :]))
            dve.sem_inc(table_done, 1)
            for k in range(2):
                tt(t1[:, :, :], oh[k][:, :, :], full[:, :, :], ALU.mult)
                link(dve.tensor_reduce(rk[:, :], t1[:, :, :], AX.X, ALU.add))
                link(dve.tensor_copy(rki[:, :], rk[:, :]))
                link(dve.tensor_scalar(rki[:, :], rki[:, :], 7, None, ALU.logical_shift_right))
                link(dve.tensor_copy(hi[:, :], rki[:, :]))
                link(dve.tensor_scalar(rk[:, :], rk[:, :], float(NBL), None, ALU.mult))
                link(dve.scalar_tensor_tensor(rk[:, :], hi[:, :], 1.0 - NBL * P, rk[:, :], ALU.mult, ALU.add))
                tt(t1[:, :, :], oh[k][:, :, :], tiled(nb[:, 1, :], NE), ALU.mult)
                link(dve.tensor_reduce(sel[:, :], t1[:, :, :], AX.X, ALU.add))
                tt(rk[:, :], rk[:, :], sel[:, :], ALU.add)
                link(dve.tensor_copy(pos[k][:, :], rk[:, :]))
                link(dve.tensor_copy(rows[:, :, k, 1].bitcast(F32), wt[k][:, :]))
            dve.sem_inc(rows_done, 1)
            def rest(at, lo, hi):
                if at is None:
                    return
                i, a = at
                for p in range(lo, hi):
                    n = a * PIECES + p
                    dve.wait_ge(whi_done, i * (4 * PIECES) + n + 1)
                    dve.tensor_tensor(w_lo[:, p, :], raw[:, n % RING, :], w_hi[:, p, :].bitcast(F32),
                                      ALU.subtract).then_inc(wlo_done, 1)

            def x_rest(b):
                dve.wait_ge(xh_done, b + 1)
                dve.tensor_tensor(xt_lo[:, :, :], xtp[:, :, :], xt_hi[:, :, :].bitcast(F32),
                                  ALU.subtract).then_inc(xl_done, 1)

            def silu(b, k):
                cols = bass.ts(k, HF)
                dve.wait_ge(sg_done[k], b + 1)
                dve.tensor_tensor(sg[:, cols], gp[:, k, 0:HF], sg[:, cols], ALU.mult).then_inc(gs_mid[k], 1)
                dve.wait_ge(gs_mid[k], b + 1)
                dve.wait_ge(ht_ps[k], b)
                dve.tensor_tensor(h[:, cols], up[:, cols], sg[:, cols], ALU.mult).then_inc(h_done[k], 1)
                dve.wait_ge(h_done[k], b + 1)
                dve.sem_inc(gs_done[k], 1)

            def h_rest(b, k):
                dve.wait_ge(hh_done[k], b + 1)
                dve.tensor_tensor(ht_lo[:, 2 * k:2 * k + 2, :], htp[:, 2 * k:2 * k + 2, :],
                                  ht_hi[:, 2 * k:2 * k + 2, :].bitcast(F32), ALU.subtract).then_inc(hl_done[k], 1)

            def block_of(b, at):
                rest(at, 0, 2)
                silu(b, 0)
                h_rest(b, 0)
                silu(b, 1)
                rest(at, 2, 3)
                x_rest(b + 1)
                h_rest(b, 1)
                rest(at, 3, PIECES)

            for done in (xl_done, *gs_mid, *gs_done, *h_done, *hl_done):
                dve.sem_inc(done, 1)
            rest((0, 0), 0, PIECES)
            x_rest(1)
            experts(dve, block_of)

        @block.gpsimd
        def _(pool):
            pool.iota(iota_i[:, :], pattern=[[1, NE]], base=0, channel_multiplier=0).then_inc(consts, 1)
            for k in range(2):
                pool.iota(rows[:, :, k, 0], pattern=[[P, NT]], base=0, channel_multiplier=1).then_inc(consts, 1)
            pool.memset(yo[:, :], 0.0).then_inc(consts, 1)
            pool.iota(empty[:, :, 0], pattern=[[0, NBL]], base=PAD, channel_multiplier=1).then_inc(consts, 1)
            pool.memset(empty[:, :, 1], 0).then_inc(consts, 1)
            pool.memset(ones[:, :], 1.0).then_inc(consts, 1)
            pool.memset(before[:, :], 1.0).then_inc(consts, 1)
            pool.memset(ident[:, :], 0.0).then_inc(ident_done, 1)
            pool.wait_ge(ident_done, 1)
            pool.affine_select(out=ident[:, :], in_=ident[:, :], compare_op=ALU.not_equal, fill=1.0, base=0,
                               pattern=[[-1, P]], channel_multiplier=1).then_inc(ident_done, 1)
            pool.wait_ge(ident_done, 2)
            pool.wait_ge(consts, 8)
            pool.sem_inc(zero_yo, 1)
            pool.affine_select(out=before[:, :], in_=before[:, :], compare_op=ALU.is_gt, fill=0.0, base=0,
                               pattern=[[1, P]], channel_multiplier=-1).then_inc(consts, 1)
            pool.wait_ge(consts, 9)
            pool.wait_ge(chosen_in, 1)
            pool.affine_select(out=chosen[:, PT, :], in_=chosen[:, PT, :], compare_op=ALU.is_ge, fill=0.0,
                               base=DEC - 1, pattern=[[0, NE]], channel_multiplier=-1).then_inc(chosen_done, 1)
            pool.wait_ge(rows_done, 1)
            pool.wait_ge(filled, 16)
            for tile in range(NT):
                n = P if tile < PT else DEC
                for k in range(2):
                    pool.indirect_dma_start(
                        out=scr["slots"], out_offset=bass.IndirectOffsetOnAxis(ap=pos[k][0:n, tile:tile + 1], axis=0),
                        in_=rows[0:n, tile, k, :], in_offset=None).then_inc(scattered, 16)
            pool.wait_ge(scattered, 32 * NT)
            pool.dma_start(slots[:, 0:NBL, :].rearrange("p b w -> p (b w)"),
                           scr["slots"].rearrange("(p b) w -> p (b w)", p=P)).then_inc(slots_in, 16)
            pool.wait_ge(slots_in, 16)

            def gather(b):
                hold(pool, xt_ps, b, passed)
                pool.tensor_copy(at_g[:, :], slots[:, bass.ds(b, 1), 0]).then_inc(at_g_done, 1)
                hold(pool, at_g_done, b, passed)
                pool.indirect_dma_start(out=xg[:, :], out_offset=None, in_=scr["h2"],
                                        in_offset=bass.IndirectOffsetOnAxis(ap=at_g[:, 0:1], axis=0)
                                        ).then_inc(gathered, 16)

            def add(b):
                if not isinstance(b, int):
                    hold(pool, added, b * 16, passed)
                pool.tensor_copy(at_s[:, :], slots[:, bass.ds(b, 1), 0]).then_inc(at_s_done, 1)
                hold(pool, at_s_done, b + 1, passed)
                hold(pool, yo_done, b + 1, passed)
                pool.indirect_dma_start(out=io["y_out"], out_offset=bass.IndirectOffsetOnAxis(ap=at_s[:, 0:1], axis=0),
                                        in_=yo[:, :], in_offset=None, compute_op=ALU.add).then_inc(added, 16)

            pool.wait_ge(zeroed, 32)
            gather(1)
            pool.wait_ge(table_done, 1)
            end = pool.value_load(table[0:1, 1, NE - 1:NE], min_val=NE, max_val=NBL - 2)
            gather(2)
            add(0)
            with pool.Fori(1, end) as b:
                gather(b + 2)
                add(b)
            add(end)
            hold(pool, added, end * 16 + 16, passed)
            hold(pool, gathered, end * 16 + 16, passed)
    return sems


def build(nc, io):
    scr = {
        "q": nc.dram_tensor("scr_q", [NT * P, C], F32, kind=SCRATCH).ap(),
        "c": nc.dram_tensor("scr_c", [P, CT, NT * P], F32, kind=SCRATCH).ap(),
        "o": nc.dram_tensor("scr_o", [NT * P, GC], F32, kind=SCRATCH).ap(),
        "y": nc.dram_tensor("scr_y", [NT * P, D], F32, kind=SCRATCH).ap(),
        "h2": nc.dram_tensor("scr_h2", [ROWS, D], F32, kind=SCRATCH).ap(),
        "slots": nc.dram_tensor("scr_slots", [P * NBL, 2], I32, kind=SCRATCH).ap(),
    }

    def phase_ends(sems):
        nc.clear_and_free_semaphores(sems)
        nc.all_engine_barrier()

    phase_ends(phase_project(nc, io, scr))
    with nc.sbuf_tensor("logits", [P, NT, NR], F32) as logits:
        for g in range(2):
            phase_ends(phase_attend(nc, io, scr, g, logits))
        phase_ends(phase_moe(nc, io, scr, logits))


def kernel(**inputs):
    import concourse.bacc as bacc
    import numpy as np
    from concourse.bass_utils import run_bass_kernel_spmd

    def cols(v, n):
        return np.ascontiguousarray(v.reshape(n, P).T)

    a = {k: np.asarray(v) for k, v in inputs.items()}
    x = np.zeros((ROWS, D), a["x_prompt"].dtype)
    x[:SEQ], x[SEQ:TOK] = a["x_prompt"][0], a["x_sample"][0]
    router = np.concatenate([a["w_router_group"][0], a["w_router_expert"][0]], axis=1)
    arrays = {
        "x": x,
        "norm_mix_g": cols(a["norm_mix_g"][0], KT),
        "w_in": a["w_in"][0],
        "k_norm_g": a["k_norm_g"][0],
        "q_norm_g": np.ascontiguousarray(np.concatenate([a["q_norm_g"][0]] * 2)[:, None]),
        "conv_w": np.ascontiguousarray(a["conv_w"][0].reshape(W, CT, P).transpose(2, 1, 0)),
        "conv_b": cols(a["conv_b"][0], CT),
        "conv_ln_g": cols(a["conv_ln_g"][0], CT),
        "conv_ln_b": cols(a["conv_ln_b"][0], CT),
        "cache_conv": a["cache_conv"][0, 0],
        "cache_k": a["cache_k"][0, 0].reshape(PAST, C),
        "cache_v": a["cache_v"][0, 0].reshape(PAST, C),
        "attn_out_g": cols(a["attn_out_g"][0].reshape(-1), CT),
        "norm_ffn_g": a["norm_ffn_g"][0],
        "w_out": a["w_out"][0],
        "w_router": np.ascontiguousarray(router.reshape(KT, P, NR).transpose(1, 0, 2)),
        "w_gate": a["w_exp_gate"][0].reshape(NE * D, FF),
        "w_up": a["w_exp_up"][0].reshape(NE * D, FF),
        "w_down": a["w_exp_down"][0].reshape(NE * FF, D),
    }
    arrays = {"in_" + k: np.ascontiguousarray(v) for k, v in arrays.items()}

    nc = bacc.Bacc("TRN2", target_bir_lowering=False, num_devices=1)
    io = {k[3:]: nc.dram_tensor(k, list(v.shape), F32, kind="ExternalInput").ap() for k, v in arrays.items()}
    for name in ("k_out", "v_out", "u_out"):
        io[name] = nc.dram_tensor(name, [NT * P, C], F32, kind="ExternalOutput").ap()
    io["y_out"] = nc.dram_tensor("y_out", [ROWS, D], F32, kind="ExternalOutput").ap()
    build(nc, io)
    got = run_bass_kernel_spmd(nc, [arrays], core_ids=[0]).results[0]

    y, k, v, u = (got[name] for name in ("y_out", "k_out", "v_out", "u_out"))
    k, v = k.reshape(-1, NH, HD), v.reshape(-1, NH, HD)
    return (y[None, :SEQ], y[None, SEQ:TOK], k[None, None, :SEQ], v[None, None, :SEQ],
            u[None, None, SEQ - HIST:SEQ], k[None, None, SEQ:TOK], v[None, None, SEQ:TOK],
            u[None, None, TOK - HIST:TOK])
```

```python
from contextlib import ExitStack

import concourse.bass as bass
from concourse import mybir

F32 = mybir.dt.float32
F32R = mybir.dt.float32r
I32 = mybir.dt.int32
ALU = mybir.AluOpType
ACT = mybir.ActivationFunctionType
AX = mybir.AxisListType

P = 128
D = 1024
KT = D // P
C = 512
CT = C // P
NH, HD = 8, 64
W = 31
HIST = W - 1
SEQ, DEC, PAST = 2048, 32, 1024
PT = SEQ // P
NT = PT + 1
TOK = SEQ + DEC
ROWS = (NT + 1) * P
NR = 36
NCH = 5
EPS = 1e-6
SCRATCH = "Internal"
CHUNKS = [1, 0, 2, 3, 4]


def pairs(eng, body):
    body(0, 0, 0)
    body(1, 2, 1)
    with eng.Fori(1, PT // 4) as i:
        body(i * 2, i * 4, 0)
        body(i * 2 + 1, i * 4 + 2, 1)
    body(PT // 2, PT, 0)


def first(t, n):
    return isinstance(t, int) and t < n


def hold(eng, signal, value, passed):
    eng.wait_ge(signal, value)
    if not isinstance(value, int):
        eng.sem_inc(passed, 1)


def phase_project(nc, io, scr):
    with ExitStack() as ctx:
        def sb(name, shape, dt=F32):
            return ctx.enter_context(nc.sbuf_tensor("p1_" + name, shape, dt))

        def ps(name, shape):
            return ctx.enter_context(nc.psum_tensor("p1_" + name, shape, F32))

        sems = []

        def sem(name):
            sems.append(nc.alloc_semaphore("p1_" + name))
            return sems[-1]

        w_hi = sb("w_hi", [P, KT, NCH * C], F32R)
        w_lo = sb("w_lo", [P, KT, NCH * C], F32R)
        RAW = 5
        w_raw = sb("w_raw", [P, RAW, C])
        conv = w_raw[:, 0:2, :].rearrange("p r f -> p (r f)").rearrange("p (a t) -> p a t", a=CT)
        normed = w_raw[:, 2:4, :]
        sig = w_raw[:, 4, :]
        x_sb = sb("x", [P, D])
        xt_hi = sb("xt_hi", [P, 2, KT, P], F32R)
        xt_lo = sb("xt_lo", [P, 2, KT, P], F32R)
        u = sb("u", [P, C])
        qv_sb, k_sb = sb("qv", [P, C]), sb("k", [P, C])
        ut = sb("ut", [P, 2, CT, HIST + 2 * P])
        ident = sb("ident", [P, P])
        gcol = sb("gcol", [P, KT])
        gk = sb("gk", [P, HD])
        cw = sb("cw", [P, CT, W])
        cb, lng, lnb = sb("cb", [P, CT]), sb("lng", [P, CT]), sb("lnb", [P, CT])
        st = sb("st", [P, 64])
        ss, rstd, rs2 = st[:, 0:2], st[:, 2:4], st[:, 4:6]
        rtmp = st[:, 6:7]
        msq, msk = st[:, 8:16], st[:, 16:24]
        rq, rk = st[:, 24:32], st[:, 32:40]
        rqt = st[:, 40:48]
        bnst, mv = sb("bnst", [P, 2, 6]), sb("mv", [P, 2, 2])
        lnr, lnm = st[:, 48:50], st[:, 50:52]
        mhalf = sb("mhalf", [P, NH])
        cached = x_sb[:, 0:C]

        pj = ps("pj", [P, NCH, C])
        pxt = ps("pxt", [P, KT, P])
        pm = ps("pm", [P, C])

        ident_done, const_dma = sem("ident_done"), sem("const_dma")
        x_in = sem("x_in")
        piece_in = [sem(f"piece_in{i}") for i in range(RAW)]
        w_hi_done, w_lo_done = sem("w_hi_done"), sem("w_lo_done")
        xt_ps, xt_hi_done, xt_lo_done = sem("xt_ps"), sem("xt_hi_done"), sem("xt_lo_done")
        sq_done, rstd_step, rstd_done = sem("sq_done"), sem("rstd_step"), sem("rstd_done")
        pj_done = sem("pj_done")
        sg_done = sem("sg_done")
        u_done, ut_ps, ut_done, hist_done = sem("u_done"), sem("ut_ps"), sem("ut_done"), sem("hist_done")
        ms_done, r_step, r_done = sem("ms_done"), sem("r_step"), sem("r_done")
        qk_done, kg_done, v_done = sem("qk_done"), sem("kg_done"), sem("v_done")
        tap_done, pad_done = sem("tap_done"), sem("pad_done")
        ln1_ps, ln_stat, ln_step, ln_rs = sem("ln1_ps"), sem("ln_stat"), sem("ln_step"), sem("ln_rs")
        normed_done, ln2_ps, act_ln, swish_done = sem("normed_done"), sem("ln2_ps"), sem("act_ln"), sem("swish_done")
        st_q, st_k, st_v, st_u = sem("st_q"), sem("st_k"), sem("st_v"), sem("st_u")
        st_c = [sem("st_c0"), sem("st_c1")]
        passed, passed_dve = sem("passed"), sem("passed_dve")
        cached_in, cached_ps = sem("cached_in"), sem("cached_ps")

        NTAP = W * CT
        NPIECE = NCH * KT
        NCONST = 6
        pieces = [(c, k) for c in CHUNKS for k in range(KT)]

        def last_pair(p):
            return isinstance(p, int) and p == PT // 2

        block = ctx.enter_context(nc.Block())

        @block.sync
        def _(sp):
            sp.dma_start(gcol[:, :], io["norm_mix_g"]).then_inc(const_dma, 16)
            sp.dma_start(x_sb[:, :], io["x"][0:P, :]).then_inc(x_in, 16)
            sp.dma_start(gk[:, :], io["k_norm_g"].partition_broadcast(P)).then_inc(const_dma, 16)
            sp.dma_start(cw[:, :, :], io["conv_w"]).then_inc(const_dma, 16)
            sp.dma_start(cb[:, :], io["conv_b"]).then_inc(const_dma, 16)
            sp.dma_start(lng[:, :], io["conv_ln_g"]).then_inc(const_dma, 16)
            sp.dma_start(lnb[:, :], io["conv_ln_b"]).then_inc(const_dma, 16)
            def load_x(t):
                sp.wait_ge(sq_done, t)
                sp.dma_start(x_sb[:, :], io["x"][bass.ts(t, P), :]).then_inc(x_in, 16)

            for n, (c, k) in enumerate(pieces):
                if n >= RAW:
                    sp.wait_ge(w_lo_done, n - RAW + 1)
                sp.dma_start(w_raw[:, n % RAW, :],
                             io["w_in"][k * P:(k + 1) * P, c * C:(c + 1) * C]).then_inc(piece_in[n % RAW], 16)
                if n == KT:
                    load_x(1)

            def store_swish(t, b):
                sp.wait_ge(swish_done, t + b + 1)
                sp.dma_start(scr["c"][:, :, bass.ts(t + b, P)],
                             normed[:, b, :].rearrange("p (a t) -> p a t", a=CT)).then_inc(st_c[b], 16)

            def tile(t):
                sp.wait_ge(u_done, t + 1)
                sp.dma_start(io["u_out"][bass.ts(t, P), :], u[:, :]).then_inc(st_u, 16)
                sp.wait_ge(qk_done, 2 * t + 1)
                sp.dma_start(scr["q"][bass.ts(t, P), :], qv_sb[:, :]).then_inc(st_q, 16)
                sp.wait_ge(kg_done, t + 1)
                sp.dma_start(io["k_out"][bass.ts(t, P), :], k_sb[:, :]).then_inc(st_k, 16)
                sp.wait_ge(v_done, t + 1)
                sp.dma_start(io["v_out"][bass.ts(t, P), :], qv_sb[:, :]).then_inc(st_v, 16)

            def body(p, t, s):
                if last_pair(p):
                    sp.wait_ge(sq_done, NT)
                    sp.dma_start(cached[0:HIST, :], io["cache_conv"]).then_inc(cached_in, 16)
                elif not first(p, 1):
                    load_x(t + 1)
                if not first(p, 2):
                    store_swish(t - 4, 0)
                    store_swish(t - 4, 1)
                tile(t)
                if not last_pair(p):
                    load_x(t + 2)
                    tile(t + 1)

            pairs(sp, body)
            store_swish(PT - 2, 0)
            store_swish(PT - 2, 1)
            store_swish(PT, 0)
            for done in (st_q, st_k, st_v, st_u):
                sp.wait_ge(done, 16 * NT)
            sp.wait_ge(st_c[0], 16 * (PT // 2 + 1))
            sp.wait_ge(st_c[1], 16 * (PT // 2))

        @block.tensor
        def _(pe):
            def transpose_x(t, after_conv):
                pe.wait_ge(x_in, 16 * t + 16)
                if after_conv:
                    pe.wait_ge(normed_done, t - 3)
                elif not first(t, 1):
                    pe.wait_ge(xt_lo_done, t)
                for k in range(KT):
                    last = pe.transpose(pxt[:, k, :], x_sb[:, k * P:(k + 1) * P], ident[:, :])
                last.then_inc(xt_ps, 1)

            def project(t, b, i):
                c = CHUNKS[i]
                if i == 0:
                    pe.wait_ge(xt_lo_done, t + 1)
                    pe.wait_ge(xt_hi_done, t + 1)
                if first(t, 1):
                    pe.wait_ge(w_lo_done, KT * (i + 1))
                    pe.wait_ge(w_hi_done, KT * (i + 1))
                elif c < 2:
                    pe.wait_ge(u_done, t)
                elif c < 4:
                    pe.wait_ge(qk_done, 2 * t - 3 + c)
                else:
                    pe.wait_ge(v_done, t)
                n = 0
                for k in range(KT):
                    for xa, wa in ((xt_hi, w_hi), (xt_hi, w_lo), (xt_lo, w_hi)):
                        last = pe.matmul(pj[:, c, :], xa[:, b, k, :], wa[:, k, c * C:(c + 1) * C],
                                         start=(n == 0), stop=(n == 3 * KT - 1))
                        n += 1
                last.then_inc(pj_done, 1)

            def four(dst, src, done):
                for a in range(CT):
                    last = pe.transpose(dst(a), src(a), ident[:, :])
                last.then_inc(done, 1)

            def in_pm(a):
                return pm[:, a * P:(a + 1) * P]

            def ln1(p, t, n):
                pe.wait_ge(tap_done, (p + 1) * NTAP)
                pe.wait_ge(xt_lo_done, NT if isinstance(p, int) and p >= PT // 2 - 1 else t + 5)
                if last_pair(p):
                    pe.wait_ge(pad_done, 1)
                    pe.wait_ge(normed_done, PT)
                for b in range(n):
                    for a in range(CT):
                        last = pe.transpose(pxt[:, b * CT + a, :], conv[:, a, b * P:(b + 1) * P], ident[:, :])
                last.then_inc(ln1_ps, 1)

            def ln2(t, b):
                pe.wait_ge(normed_done, t + b + 1)
                if b == 0 and last_unit(t):
                    pe.wait_ge(act_ln, PT)
                elif b == 0:
                    pe.wait_ge(ut_done, min(t + 4, NT) if isinstance(t, int) else t + 4)
                else:
                    pe.wait_ge(act_ln, t + 1)
                four(in_pm, lambda a: normed[:, b, a * P:(a + 1) * P], ln2_ps)

            def ut_transpose(p, t, b):
                pe.wait_ge(u_done, t + b + 1)
                if b == 1:
                    pe.wait_ge(ut_done, t + 1)
                elif last_pair(p):
                    pe.wait_ge(hist_done, PT // 2 + 1)
                elif not first(p, 2):
                    pe.wait_ge(act_ln, t - 2)
                elif not first(p, 1):
                    pe.wait_ge(ut_done, t)
                four(in_pm, lambda a: u[:, a * P:(a + 1) * P], ut_ps)

            def last_unit(t):
                return isinstance(t, int) and t == PT

            pe.wait_ge(ident_done, 3)
            transpose_x(0, False)

            def body(p, t, s):
                project(t, 0, 0)
                if not first(p, 2):
                    ln2(t - 4, 0)
                project(t, 0, 1)
                if not last_pair(p):
                    transpose_x(t + 1, not first(p, 2))
                if not first(p, 2):
                    ln2(t - 4, 1)
                project(t, 0, 2)
                if last_pair(p):
                    pe.wait_ge(cached_in, 16)
                    pe.wait_ge(act_ln, PT - 2)
                    for a in range(CT):
                        last = pe.transpose(pm[:, a * P:a * P + HIST], cached[0:HIST, a * P:(a + 1) * P],
                                            ident[0:HIST, 0:HIST])
                    last.then_inc(cached_ps, 1)
                project(t, 0, 3)
                ut_transpose(p, t, 0)
                project(t, 0, 4)
                if last_pair(p):
                    ln1(p - 1, t - 2, 2)
                if not last_pair(p):
                    project(t + 1, 1, 0)
                    project(t + 1, 1, 1)
                    transpose_x(t + 2, False)
                    project(t + 1, 1, 2)
                    project(t + 1, 1, 3)
                    ut_transpose(p, t, 1)
                    project(t + 1, 1, 4)
                    if not first(p, 1):
                        ln1(p - 1, t - 2, 2)

            pairs(pe, body)
            ln2(PT - 2, 0)
            ln2(PT - 2, 1)
            ln1(PT // 2, PT, 1)
            ln2(PT, 0)

        @block.scalar
        def _(act):
            act.wait_ge(const_dma, 16 * NCONST)

            def x_parts(t, b):
                act.wait_ge(xt_ps, t + 1)
                if not first(t, 2):
                    act.wait_ge(pj_done, 5 * t - 5)
                    act.wait_ge(rstd_done, t - 1)
                act.activation(xt_hi[:, b, :, :], pxt[:, :, :], ACT.Copy).then_inc(xt_hi_done, 1)
                act.activation(x_sb[:, :], x_sb[:, :], ACT.Square, accum_out=ss[:, b:b + 1]).then_inc(sq_done, 1)

            for n, (c, k) in enumerate(pieces):
                act.wait_ge(piece_in[n % RAW], 16 * (n // RAW + 1))
                act.activation(w_hi[:, k, c * C:(c + 1) * C], w_raw[:, n % RAW, :], ACT.Copy,
                               scale=gcol[:, k:k + 1]).then_inc(w_hi_done, 1)
                if n == 1:
                    x_parts(0, 0)

            def ln_norm(p, t, n):
                act.wait_ge(ln_rs, p + 1)
                for b in range(n):
                    if not first(p, 1):
                        act.wait_ge(st_c[b], 16 * p)
                    act.activation(normed[:, b, :], pxt[:, b * CT:(b + 1) * CT, :], ACT.Identity,
                                   scale=lnr[:, b:b + 1], bias=lnm[:, b:b + 1]).then_inc(normed_done, 1)

            def ln_out(t, b):
                act.wait_ge(ln2_ps, t + b + 1)
                if not (b == 0 and first(t, 1)):
                    act.wait_ge(swish_done, t + b)
                for a in range(CT):
                    act.activation(sig[:, a * P:(a + 1) * P], pm[:, a * P:(a + 1) * P], ACT.Sigmoid,
                                   scale=lng[:, a:a + 1], bias=lnb[:, a:a + 1])
                for a in range(CT):
                    last = act.activation(normed[:, b, a * P:(a + 1) * P], pm[:, a * P:(a + 1) * P], ACT.Identity,
                                          scale=lng[:, a:a + 1], bias=lnb[:, a:a + 1])
                last.then_inc(act_ln, 1)

            def gate(t, b):
                act.wait_ge(pj_done, 5 * t + 1)
                act.wait_ge(rstd_done, t + 1)
                if not first(t, 1):
                    act.wait_ge(ut_ps, t)
                    act.wait_ge(st_u, 16 * t)
                act.activation(u[:, :], pj[:, 1, :], ACT.Sigmoid, scale=rstd[:, b:b + 1]).then_inc(sg_done, 1)

            def squares(t, n):
                act.wait_ge(pj_done, 5 * t + 3 + n)
                if not first(t, 1):
                    act.wait_ge(st_v if n == 0 else st_k, 16 * t)
                act.activation((qv_sb, k_sb)[n][:, :], pj[:, 2 + n, :], ACT.Square).then_inc(sg_done, 1)

            def history(p, t, s):
                if first(p, 1):
                    return
                if not first(p, 2):
                    act.wait_ge(tap_done, (p - 1) * NTAP)
                if last_pair(p):
                    act.wait_ge(cached_ps, 1)
                    act.activation(ut[:, s, :, 0:HIST], pm[:, :].rearrange("p (a t) -> p a t", a=CT)[:, :, 0:HIST],
                                   ACT.Copy).then_inc(hist_done, 1)
                else:
                    act.wait_ge(ut_done, t)
                    act.activation(ut[:, s, :, 0:HIST], ut[:, 1 - s, :, 2 * P:2 * P + HIST],
                                   ACT.Copy).then_inc(hist_done, 1)

            def u_out(p, t, b, s):
                act.wait_ge(hist_done, p + 1)
                act.wait_ge(ut_ps, t + b + 1)
                act.activation(ut[:, s, :, HIST + b * P:HIST + (b + 1) * P],
                               pm[:, :].rearrange("p (a t) -> p a t", a=CT), ACT.Copy).then_inc(ut_done, 1)

            def values(t, b):
                act.wait_ge(pj_done, 5 * t + 5)
                act.wait_ge(st_q, 16 * t + 16)
                act.activation(qv_sb[:, :], pj[:, 4, :], ACT.Copy, scale=rstd[:, b:b + 1]).then_inc(v_done, 1)

            def body(p, t, s):
                gate(t, 0)
                if not first(p, 2):
                    ln_out(t - 4, 0)
                if not last_pair(p):
                    x_parts(t + 1, 1)
                squares(t, 0)
                if not first(p, 2):
                    ln_out(t - 4, 1)
                history(p, t, s)
                u_out(p, t, 0, s)
                squares(t, 1)
                values(t, 0)
                if not last_pair(p):
                    gate(t + 1, 1)
                    x_parts(t + 2, 0)
                    squares(t + 1, 0)
                    u_out(p, t, 1, s)
                    squares(t + 1, 1)
                    values(t + 1, 1)
                if not first(p, 1):
                    ln_norm(p - 1, t - 2, 2)

            pairs(act, body)
            ln_out(PT - 2, 0)
            ln_out(PT - 2, 1)
            ln_norm(PT // 2, PT, 1)
            ln_out(PT, 0)

        @block.vector
        def _(dve):
            def x_rest(t, b):
                dve.wait_ge(xt_hi_done, t + 1)
                dve.tensor_tensor(xt_lo[:, b, :, :], pxt[:, :, :], xt_hi[:, b, :, :].bitcast(F32),
                                  ALU.subtract).then_inc(xt_lo_done, 1)

            dve.wait_ge(const_dma, 16 * NCONST)
            for n, (c, k) in enumerate(pieces):
                dve.wait_ge(w_hi_done, n + 1)
                dve.scalar_tensor_tensor(w_lo[:, k, c * C:(c + 1) * C], w_raw[:, n % RAW, :], gcol[:, k:k + 1],
                                         w_hi[:, k, c * C:(c + 1) * C].bitcast(F32), ALU.mult,
                                         ALU.subtract).then_inc(w_lo_done, 1)
                if n == 1:
                    x_rest(0, 0)

            def taps(p, t, s, lo, hi):
                wide = DEC if last_pair(p) else 2 * P
                if lo == 0:
                    dve.wait_ge(ut_done, NT if last_pair(p) else t + 2)
                    if last_pair(p):
                        dve.wait_ge(ln1_ps, p)
                        dve.memset(conv[:, :, DEC:P], 0.0).then_inc(pad_done, 1)
                    if first(p, 1):
                        dve.wait_ge(w_lo_done, NPIECE)
                    else:
                        dve.wait_ge(ln1_ps, p)
                for j in range(lo, hi):
                    for a in range(CT):
                        src, dst = ut[:, s, a, j:j + wide], conv[:, a, 0:wide]
                        if j == 0:
                            dve.tensor_scalar(dst, src, cw[:, a, 0:1], cb[:, a:a + 1], ALU.mult,
                                              ALU.add).then_inc(tap_done, 1)
                        else:
                            dve.wait_ge(tap_done, p * NTAP + CT * (j - 1) + a + 1)
                            dve.scalar_tensor_tensor(dst, src, cw[:, a, j:j + 1], dst, ALU.mult,
                                                     ALU.add).then_inc(tap_done, 1)

            def heads(ap):
                return ap.rearrange("p (h d) -> p h d", h=NH)

            def ln_stats(p, n):
                dve.wait_ge(ln1_ps, p + 1)
                if not first(p, 1):
                    dve.wait_ge(ln_rs, p)
                for b in range(n):
                    dve.bn_stats(bnst[:, b, :], pxt[:, b * CT:(b + 1) * CT, :].rearrange("p a t -> p (a t)")
                                 ).then_inc(ln_stat, 1)
                for b in range(n):
                    hold(dve, ln_stat, 4 * p + n + b, passed_dve)
                    dve.bn_aggr(mv[:, b, :], bnst[:, b, :]).then_inc(ln_stat, 1)

            def glu(t, b):
                dve.wait_ge(pj_done, 5 * t + 2)
                dve.wait_ge(sg_done, 3 * t + 1)
                dve.scalar_tensor_tensor(u[:, :], pj[:, 0, :], rstd[:, b:b + 1], u[:, :],
                                         ALU.mult, ALU.mult).then_inc(u_done, 1)

            def mean_squares(t, n):
                ms, dst = ((msq, qv_sb), (msk, k_sb))[n]
                dve.wait_ge(sg_done, 3 * t + 2 + n)
                if not first(t, 1):
                    dve.wait_ge(r_done, 2 * t - 1 + n)
                dve.tensor_reduce(ms, heads(dst[:, :]), AX.X, ALU.add).then_inc(ms_done, 1)

            def normalise(t, n):
                c, r, dst = ((2, rq, qv_sb), (3, rk, k_sb))[n]
                dve.wait_ge(ms_done, 2 * t + n + 1)
                dve.wait_ge(r_done, 2 * t + n + 1)
                dve.tensor_tensor(heads(dst[:, :]), heads(pj[:, c, :]),
                                  r.unsqueeze(2).broadcast_to([P, NH, HD]), ALU.mult).then_inc(qk_done, 1)

            def body(p, t, s):
                def conv_before(lo, hi):
                    if not first(p, 1):
                        taps(p - 1, t - 2, 1 - s, lo, hi)

                def tile(t, b, steps):
                    conv_before(steps[0], steps[1])
                    glu(t, b)
                    if not last_pair(p):
                        x_rest(t + 1, 1 - b)
                    conv_before(steps[1], steps[2])
                    mean_squares(t, 0)
                    conv_before(steps[2], steps[3])
                    normalise(t, 0)
                    mean_squares(t, 1)
                    conv_before(steps[3], steps[4])
                    normalise(t, 1)

                if last_pair(p):
                    tile(t, 0, (0, 8, 16, 24, W))
                else:
                    tile(t, 0, (0, 6, 10, 13, 16))
                    tile(t + 1, 1, (16, 21, 25, 28, W))
                if not first(p, 1):
                    ln_stats(p - 1, 2)

            pairs(dve, body)
            taps(PT // 2, PT, 0, 0, W)
            ln_stats(PT // 2, 1)

        @block.gpsimd
        def _(pool):
            pool.memset(ident[:, :], 0.0).then_inc(ident_done, 1)
            pool.memset(mhalf[:, :], -0.5).then_inc(ident_done, 1)
            hold(pool, ident_done, 1, passed)
            pool.affine_select(out=ident[:, :], in_=ident[:, :], compare_op=ALU.not_equal, fill=1.0, base=0,
                               pattern=[[-1, P]], channel_multiplier=1).then_inc(ident_done, 1)
            pool.memset(ut[:, 0, :, 0:HIST], 0.0).then_inc(hist_done, 1)
            hold(pool, const_dma, 16 * NCONST, passed)
            hold(pool, ident_done, 3, passed)

            def inverse_rms(t, b):
                hold(pool, sq_done, t + 1, passed)
                if not first(t, 2):
                    hold(pool, v_done, t - 1, passed)
                    hold(pool, u_done, t - 1, passed)
                pool.tensor_scalar(rtmp, ss[:, b:b + 1], 1.0 / D, EPS, ALU.mult, ALU.add).then_inc(rstd_step, 1)
                hold(pool, rstd_step, 2 * t + 1, passed)
                pool.tensor_tensor(rstd[:, b:b + 1], rtmp, mhalf[:, 0:1], ALU.pow).then_inc(rstd_step, 1)
                hold(pool, rstd_step, 2 * t + 2, passed)
                pool.tensor_scalar(rs2[:, b:b + 1], rstd[:, b:b + 1], rstd[:, b:b + 1], 1.0 / HD,
                                   ALU.mult, ALU.mult).then_inc(rstd_done, 1)

            def head_rms(t, b, n, ms, r):
                hold(pool, ms_done, 2 * t + n + 1, passed)
                if not first(t, 1):
                    hold(pool, qk_done, 2 * t - 1 + n, passed)
                pool.tensor_scalar(rqt, ms, rs2[:, b:b + 1], EPS, ALU.mult, ALU.add).then_inc(r_step, 1)
                hold(pool, r_step, 4 * t + 2 * n + 1, passed)
                pool.tensor_tensor(r, rqt, mhalf[:, :], ALU.pow).then_inc(r_step, 1)
                hold(pool, r_step, 4 * t + 2 * n + 2, passed)
                pool.tensor_scalar(r, r, rstd[:, b:b + 1], None, ALU.mult).then_inc(r_done, 1)
                hold(pool, r_done, 2 * t + n + 1, passed)

            def ln_scale(p, n):
                hold(pool, ln_stat, 4 * p + 2 * n, passed)
                if not first(p, 1):
                    hold(pool, normed_done, 2 * p, passed)
                pool.tensor_scalar(lnr[:, 0:n], mv[:, 0:n, 1], EPS, None, ALU.add).then_inc(ln_step, 1)
                hold(pool, ln_step, 3 * p + 1, passed)
                pool.tensor_tensor(lnr[:, 0:n], lnr[:, 0:n], mhalf[:, 0:n], ALU.pow).then_inc(ln_step, 1)
                hold(pool, ln_step, 3 * p + 2, passed)
                pool.tensor_tensor(lnm[:, 0:n], mv[:, 0:n, 0], lnr[:, 0:n], ALU.mult).then_inc(ln_step, 1)
                hold(pool, ln_step, 3 * p + 3, passed)
                pool.tensor_scalar(lnm[:, 0:n], lnm[:, 0:n], -1.0, None, ALU.mult).then_inc(ln_rs, 1)

            def ln_swish(t, b):
                hold(pool, act_ln, t + b + 1, passed)
                pool.tensor_tensor(normed[:, b, :], normed[:, b, :], sig, ALU.mult).then_inc(swish_done, 1)

            def key_gain(t):
                hold(pool, qk_done, 2 * t + 2, passed)
                k_heads = k_sb[:, :].rearrange("p (h d) -> p h d", h=NH)
                pool.tensor_tensor(k_heads, k_heads, gk[:, :].unsqueeze(1).broadcast_to([P, NH, HD]),
                                   ALU.mult).then_inc(kg_done, 1)

            inverse_rms(0, 0)

            def body(p, t, s):
                if not first(p, 2):
                    ln_swish(t - 4, 0)
                if not last_pair(p):
                    inverse_rms(t + 1, 1)
                head_rms(t, 0, 0, msq, rq)
                if not first(p, 2):
                    ln_swish(t - 4, 1)
                head_rms(t, 0, 1, msk, rk)
                key_gain(t)
                if not last_pair(p):
                    inverse_rms(t + 2, 0)
                    head_rms(t + 1, 1, 0, msq, rq)
                    head_rms(t + 1, 1, 1, msk, rk)
                    key_gain(t + 1)
                if not first(p, 1):
                    ln_scale(p - 1, 2)

            pairs(pool, body)
            ln_swish(PT - 2, 0)
            ln_swish(PT - 2, 1)
            ln_scale(PT // 2, 1)
            ln_swish(PT, 0)
    return sems


NKT = PT + PAST // P + 1
HG = NH // 2
GC = HG * HD
MAXU = 8
SCALE = HD ** -0.5


def key_tiles(t):
    return (0, t + 1) if t < PT else (PT, PAST // P + 1)


def attention_steps(g):
    steps = []
    past = iter([("k", PT + n) for n in range(PAST // P + 1)])
    for t in range(NT + 3):
        if t < NT:
            _, n = key_tiles(t)
            half = n if n <= MAXU else n // 2
            parts = [(0, n, False)] if n <= MAXU else [(half, n, False), (0, half, True)]
            units = [(t, h, lo, hi, more) for h in range(HG) for lo, hi, more in parts]
        else:
            units = [None] * 4
        jobs = []
        if t + 1 < PT:
            jobs.append(("k", t + 1))
        if g == 1 and 0 <= t - 2 < NT:
            jobs.append(("mix", t - 2))
        if t + 1 < NT:
            jobs.append(("q", t + 1))
        extra = [next(past) for _ in range(int(7 <= t < PT) if g == 0 else {0: 3, 1: 3, 2: 2, PT - 1: 1}.get(t, 0))]
        if 0 <= t - 2 * g < NT:
            jobs += [("wo", t - 2 * g, 0), ("wo", t - 2 * g, 1)]
        jobs += extra
        if g == 1 and 0 <= t - 3 < NT:
            jobs += [("h2t", t - 3, 0), ("h2t", t - 3, 1), ("route", t - 3)]
        placed = [[] for _ in range(2 * len(units))]
        every = 2 if len(jobs) <= len(units) else 1
        for n, job in enumerate(jobs):
            placed[n * len(placed) // every // len(jobs) * every].append(job)
        for i, unit in enumerate(units):
            steps.append((t, i, i == len(units) - 1, unit, placed[2 * i], placed[2 * i + 1]))
    return steps


def phase_attend(nc, io, scr, g, logits):
    with ExitStack() as ctx:
        pre = f"p2{g}_"

        def sb(name, shape, dt=F32):
            return ctx.enter_context(nc.sbuf_tensor(pre + name, shape, dt))

        def ps(name, shape):
            return ctx.enter_context(nc.psum_tensor(pre + name, shape, F32))

        sems = []

        def sem(name):
            sems.append(nc.alloc_semaphore(pre + name))
            return sems[-1]

        NB = 4 - g
        NA = 4
        UW = MAXU * P
        kt_sb = sb("kt", [P, HG, NKT * P], F32R)
        v_sb = sb("v", [P, NKT, GC])
        wo_hi = sb("wo_hi", [P, CT, D], F32R)
        wo_lo = sb("wo_lo", [P, CT, D], F32R)
        q_hi = sb("q_hi", [P, 2, HG, P], F32R)
        q_lo = sb("q_lo", [P, 2, HG, P], F32R)
        keep = sb("keep", [P, NB, UW + 4])
        wgt = sb("wgt", [P, NB, UW])
        at = sb("at", [P, NA, 4 * P])
        kd = sb("kd", [P, 2, HG, 2, HD])
        qd = sb("qd", [P, 2, HG, 2, HD])
        m_hi = sb("m_hi", [P, 2, CT, P], F32R)
        m_lo = sb("m_lo", [P, 2, CT, P], F32R)
        o_raw = sb("o_raw", [P, 2, GC])
        o_sq = sb("o_sq", [P, GC])
        o_n = sb("o_n", [P, 4, GC])
        y = sb("y", [P, 3, D])
        ident = sb("ident", [P, P])
        identb = sb("identb", [P, P], mybir.dt.bfloat16)
        mask = sb("mask", [P, P], mybir.dt.bfloat16)
        gq = sb("gq", [P, 1])
        go = sb("go", [P, CT])
        st = sb("st", [P, 40])
        oms, orr, ort = st[:, 0:4], st[:, 4:8], st[:, 8:12]
        ss, rt, rstd = st[:, 12:13], st[:, 13:14], st[:, 14:15]
        mhalf = sb("mhalf", [P, 4])
        if g == 0:
            c_ld = sb("c_ld", [P, 2, CT, P])
        else:
            o_a = sb("o_a", [P, 2, GC])
            g2 = sb("g2", [P, D])
            h2 = sb("h2", [P, 2, D])
            h2t = sb("h2t", [P, KT, P])
            wr = sb("wr", [P, KT, NR])
        raw = [wgt[:, 0, :], wgt[:, 1, :], wgt[:, 2, :], keep[:, 0, 0:UW]]

        zp = ps("zp", [P, 2, UW])
        tp = ps("tp", [P, 2, 4 * P])
        op = ps("op", [P, 4 * P])
        mp = ps("mp", [P, 4 * P])

        ready, const_in, raw_in = sem("ready"), sem("const_in"), [sem(f"raw_in{i}") for i in range(CT)]
        wo_hi_done, wo_lo_done = sem("wo_hi_done"), sem("wo_lo_done")
        k_in, q_in = [sem("k_in0"), sem("k_in1")], [sem("q_in0"), sem("q_in1")]
        mp_full, mp_free = sem("mp_full"), sem("mp_free")
        k_hi_done, k_done, q_hi_done, q_done = sem("k_hi_done"), sem("k_done"), sem("q_hi_done"), sem("q_done")
        z_done, sig_done, edge_done, scan_done, a_done = (sem("z_done"), sem("sig_done"), sem("edge_done"),
                                                          sem("scan_done"), sem("a_done"))
        t_done, cp_dve, cp_act, av_done = sem("t_done"), sem("cp_dve"), sem("cp_act"), sem("av_done")
        o_out, o_sq_done, o_ms, o_step, o_done = (sem("o_out"), sem("o_sq_done"), sem("o_ms"), sem("o_step"),
                                                  sem("o_done"))
        m_in, m_hi_done, m_done, wo_done = ([sem("m_in0"), sem("m_in1")], sem("m_hi_done"), sem("m_done"),
                                            sem("wo_done"))
        y_in = [sem(f"y_in{i}") for i in range(3)]
        y_done = sem("y_done")
        st_y, st_o, st_h = [[sem(f"st_{x}{i}") for i in range(n)] for x, n in (("y", 3), ("o", 4), ("h", 2))]
        ss_done, rs_step, h2_step, h2_done = sem("ss_done"), sem("rs_step"), sem("h2_step"), sem("h2_done")
        h2t_done, rt_done, lg_done = sem("h2t_done"), sem("rt_done"), sem("lg_done")

        steps = attention_steps(g)
        units = [step[3] for step in steps if step[3]]
        n_of = {u: i for i, u in enumerate(units)}
        last_of = {u[0]: i for i, u in enumerate(units)}
        halves, base = [], []
        for i, (_, _, lo, hi, _) in enumerate(units):
            base.append(len(halves))
            halves += [(i, a, min(a + 4, hi)) for a in range(lo, hi, 4)]
        by_act = [n % 4 == 3 for n in range(len(halves))]
        end_half = {t: base[i] + sum(1 for x in halves if x[0] == i) for t, i in last_of.items()}

        order = [("k", 0), ("q", 0)] + [job for step in steps for job in step[4] + step[5]]
        use = {job: n for n, job in enumerate(order)}
        k_order = [job[1] for job in order if job[0] == "k"]
        k_at = {kt: n for n, kt in enumerate(k_order)}

        def copies_before(n, act):
            return sum(1 for x in by_act[:n] if x == act)

        def copy_halves(eng, u, act):
            for n in range(base[u], base[u + 1] if u + 1 < len(units) else len(halves)):
                if by_act[n] != act:
                    continue
                _, a, e = halves[n]
                eng.wait_ge(t_done, n + 1)
                if n >= NA:
                    eng.wait_ge(av_done, n - NA + 1)
                dst, src = at[:, n % NA, 0:(e - a) * P], tp[:, n % 2, 0:(e - a) * P]
                if act:
                    eng.activation(dst, src, ACT.Copy).then_inc(cp_act, 1)
                else:
                    eng.tensor_copy(dst, src).then_inc(cp_dve, 1)

        block = ctx.enter_context(nc.Block())
        c0 = g * GC

        @block.sync
        def _(sp):
            sp.dma_start(gq[:, :], io["q_norm_g"]).then_inc(const_in, 16)
            sp.dma_start(go[:, :], io["attn_out_g"]).then_inc(const_in, 16)
            if g == 1:
                sp.dma_start(g2[:, :], io["norm_ffn_g"].partition_broadcast(P)).then_inc(const_in, 16)
                sp.dma_start(wr[:, :, :], io["w_router"]).then_inc(const_in, 16)

            def load_k(kt):
                n = k_at[kt]
                if kt < PT:
                    ksrc, vsrc, r = io["k_out"], io["v_out"], kt
                elif kt < NKT - 1:
                    ksrc, vsrc, r = io["cache_k"], io["cache_v"], kt - PT
                else:
                    ksrc, vsrc, r = io["k_out"], io["v_out"], PT
                if n >= 2:
                    sp.wait_ge(mp_full, use[("k", k_order[n - 2])] + 1)
                for a in range(2):
                    sp.dma_start(kd[:, n % 2, :, a, :],
                                 ksrc[r * P:(r + 1) * P, c0:c0 + GC].rearrange("p (h d) -> p h d", h=HG)
                                 ).then_inc(k_in[n % 2], 16)
                sp.dma_start(v_sb[:, kt, :], vsrc[r * P:(r + 1) * P, c0:c0 + GC]).then_inc(k_in[n % 2], 16)

            def load_q(t):
                if t >= 2:
                    sp.wait_ge(mp_full, use[("q", t - 2)] + 1)
                for a in range(2):
                    sp.dma_start(qd[:, t % 2, :, a, :],
                                 scr["q"][t * P:(t + 1) * P, c0:c0 + GC].rearrange("p (h d) -> p h d", h=HG)
                                 ).then_inc(q_in[t % 2], 16)

            def load_mix(t):
                if g == 0:
                    if t >= 2:
                        sp.wait_ge(m_done, t - 1)
                    sp.dma_start(c_ld[:, t % 2, :, :], scr["c"][:, :, t * P:(t + 1) * P]).then_inc(m_in[t % 2], 16)
                else:
                    if t >= 2:
                        sp.wait_ge(mp_full, use[("mix", t - 2)] + 1)
                    sp.dma_start(o_a[:, t % 2, :], scr["o"][t * P:(t + 1) * P, :]).then_inc(m_in[t % 2], 16)

            def load_y(t):
                if t >= 3:
                    sp.wait_ge(st_y[t % 3], 16 * (t // 3))
                    if g == 1:
                        sp.wait_ge(h2_step, t - 2)
                src = io["x"] if g == 0 else scr["y"]
                sp.dma_start(y[:, t % 3, :], src[t * P:(t + 1) * P, :]).then_inc(y_in[t % 3], 16)

            def load_for(t):
                for step in steps:
                    for j in step[4] + step[5]:
                        if step[0] != t:
                            continue
                        if j[0] == "k":
                            load_k(j[1])
                        elif j[0] == "q":
                            load_q(j[1])
                        elif j[0] == "mix" or g == 0 and j[0] == "wo" and j[2] == 0:
                            load_mix(j[1])
                            load_y(j[1])

            load_k(0)
            load_q(0)
            for k in range(CT):
                sp.dma_start(raw[k], io["w_out"][(g * CT + k) * P:(g * CT + k + 1) * P, :]).then_inc(raw_in[k], 16)
            load_for(0)
            lag = 0 if g == 0 else 2
            for t in range(NT + 3):
                load_for(t + 1)
                if 0 <= t - 1 < NT and g == 0:
                    sp.wait_ge(o_done, t)
                    sp.dma_start(scr["o"][(t - 1) * P:t * P, :], o_n[:, (t - 1) % 4, :]).then_inc(st_o[(t - 1) % 4], 16)
                if 0 <= t - lag < NT:
                    sp.wait_ge(y_done, 2 * (t - lag) + 2)
                    dst = scr["y"] if g == 0 else io["y_out"]
                    sp.dma_start(dst[(t - lag) * P:(t - lag + 1) * P, :], y[:, (t - lag) % 3, :]
                                 ).then_inc(st_y[(t - lag) % 3], 16)
                    if g == 1:
                        sp.wait_ge(h2_done, t - lag + 1)
                        sp.dma_start(scr["h2"][(t - lag) * P:(t - lag + 1) * P, :],
                                     h2[:, (t - lag) % 2, :]).then_inc(st_h[(t - lag) % 2], 16)
            for slots in (st_y, st_o) if g == 0 else (st_y, st_h):
                for i, s in enumerate(slots):
                    sp.wait_ge(s, 16 * len(range(i, NT, len(slots))))

        @block.tensor
        def _(pe):
            def job(j):
                if use[j]:
                    pe.wait_ge(mp_free, use[j])
                if j[0] in "kq":
                    n = k_at[j[1]] if j[0] == "k" else j[1]
                    if j[0] == "k":
                        pe.wait_ge(k_in[n % 2], 48 * (n // 2 + 1))
                    else:
                        pe.wait_ge(q_in[n % 2], 32 * (n // 2 + 1))
                    src = kd if j[0] == "k" else qd
                    for h in range(HG):
                        last = pe.transpose(mp[:, h * P:(h + 1) * P],
                                            src[:, n % 2, h, :, :].rearrange("p a d -> p (a d)"), ident[:, :])
                elif j[0] == "mix":
                    t = j[1]
                    pe.wait_ge(m_in[t % 2], 16 * (t // 2 + 1))
                    pe.wait_ge(o_done, t + 1)
                    for k in range(CT):
                        src = o_a[:, t % 2, :] if k < 2 else o_n[:, t % 4, :]
                        last = pe.transpose(mp[:, k * P:(k + 1) * P], src[:, (k % 2) * P:(k % 2 + 1) * P], ident[:, :])
                elif j[0] == "wo":
                    t, c = j[1], j[2]
                    pe.wait_ge(m_done, t + 1)
                    pe.wait_ge(m_hi_done, t + 1)
                    pe.wait_ge(wo_lo_done, CT)
                    pe.wait_ge(wo_hi_done, CT)
                    n = 0
                    for k in range(CT):
                        for ma, wa in ((m_hi, wo_hi), (m_hi, wo_lo), (m_lo, wo_hi)):
                            last = pe.matmul(mp[:, :], ma[:, t % 2, k, :], wa[:, k, c * C:(c + 1) * C],
                                             start=(n == 0), stop=(n == 3 * CT - 1))
                            n += 1
                    last.then_inc(wo_done, 1)
                    pe.wait_ge(wo_done, 2 * t + c + 1)
                    pe.sem_inc(mp_full, 1)
                    return
                elif j[0] == "h2t":
                    t, c = j[1], j[2]
                    pe.wait_ge(h2_done, t + 1)
                    for k in range(4):
                        last = pe.transpose(mp[:, k * P:(k + 1) * P],
                                            h2[:, t % 2, (4 * c + k) * P:(4 * c + k + 1) * P], ident[:, :])
                else:
                    t = j[1]
                    pe.wait_ge(h2t_done, 2 * t + 2)
                    for k in range(KT):
                        last = pe.matmul(mp[:, 0:NR], h2t[:, k, :], wr[:, k, :], start=(k == 0), stop=(k == KT - 1))
                last.then_inc(mp_full, 1)

            def scores(u):
                t, h, lo, hi, _ = units[u]
                kb, n = key_tiles(t)
                if u >= 2:
                    pe.wait_ge(sig_done, u - 1)
                pe.wait_ge(q_done, t + 1)
                pe.wait_ge(k_done, k_at[kb + hi - 1] + 1)
                for a in range(lo, hi, 4):
                    e = min(a + 4, hi)
                    dst = zp[:, u % 2, (a - lo) * P:(e - lo) * P]
                    keys = kt_sb[:, h, (kb + a) * P:(kb + e) * P]
                    pe.matmul(dst, q_hi[:, t % 2, h, :], keys, start=True, stop=False)
                    if e == n:
                        pe.matmul(zp[:, u % 2, (n - 1 - lo) * P:(n - lo) * P], identb[:, :], mask[:, :],
                                  start=False, stop=False, skip_group_check=True)
                    last = pe.matmul(dst, q_lo[:, t % 2, h, :], keys, start=False, stop=True)
                last.then_inc(z_done, 1)

            def transpose_weights(u):
                lo = units[u][2]
                pe.wait_ge(a_done, u + 1)
                for n in range(base[u], end_of(u)):
                    _, a, e = halves[n]
                    if n >= 2:
                        pe.wait_ge(cp_act if by_act[n - 2] else cp_dve, copies_before(n - 1, by_act[n - 2]))
                    for i in range(a, e):
                        last = pe.transpose(tp[:, n % 2, (i - a) * P:(i - a + 1) * P],
                                            wgt[:, u % NB, (i - lo) * P:(i - lo + 1) * P], ident[:, :])
                    last.then_inc(t_done, 1)

            def end_of(u):
                return base[u + 1] if u + 1 < len(units) else len(halves)

            def values(u):
                t, h, lo, hi, _ = units[u]
                kb, _ = key_tiles(t)
                if h == 0 and u == first_unit(t):
                    if t:
                        pe.wait_ge(o_out, t)
                for n in range(base[u], end_of(u)):
                    _, a, e = halves[n]
                    pe.wait_ge(cp_act if by_act[n] else cp_dve, copies_before(n + 1, by_act[n]))
                    for i in range(a, e):
                        begin = u == first_unit(t) and n == base[u] and i == a
                        end = u == last_of[t] and n == end_of(u) - 1 and i == e - 1
                        last = pe.matmul(op[:, h * HD:(h + 1) * HD], at[:, n % NA, (i - a) * P:(i - a + 1) * P],
                                         v_sb[:, kb + i, h * HD:(h + 1) * HD], start=begin, stop=end,
                                         skip_group_check=True)
                    last.then_inc(av_done, 1)

            def first_unit(t):
                return last_of[t - 1] + 1 if t else 0

            pe.wait_ge(ready, 5)
            job(("k", 0))
            job(("q", 0))
            for s, (t, i, last_step, unit, jobs, late_jobs) in enumerate(steps):
                for j in jobs:
                    job(j)
                if unit:
                    scores(n_of[unit])
                if s >= 2 and steps[s - 2][3]:
                    transpose_weights(n_of[steps[s - 2][3]])
                for j in late_jobs:
                    job(j)
                if s >= 3 and steps[s - 3][3]:
                    values(n_of[steps[s - 3][3]])

        @block.scalar
        def _(act):
            act.wait_ge(const_in, 16 * (2 if g == 0 else 4))

            def job(j):
                if j[0] not in ("k", "q", "mix", "h2t"):
                    return
                act.wait_ge(mp_full, use[j] + 1)
                if j[0] == "k":
                    act.activation(kt_sb[:, :, j[1] * P:(j[1] + 1) * P],
                                   mp[:, :].rearrange("p (h t) -> p h t", h=HG), ACT.Copy).then_inc(k_hi_done, 1)
                elif j[0] == "q":
                    t = j[1]
                    if t >= 2:
                        act.wait_ge(z_done, last_of[t - 2] + 1)
                    act.activation(q_hi[:, t % 2, :, :], mp[:, :].rearrange("p (h t) -> p h t", h=HG),
                                   ACT.Copy, scale=gq[:, 0:1]).then_inc(q_hi_done, 1)
                elif j[0] == "mix":
                    t = j[1]
                    if t >= 2:
                        act.wait_ge(wo_done, 2 * t - 2)
                    act.activation(m_hi[:, t % 2, :, :], mp[:, :].rearrange("p (h t) -> p h t", h=CT),
                                   ACT.Copy).then_inc(m_hi_done, 1)
                elif j[0] == "h2t":
                    t, c = j[1], j[2]
                    if t and c == 0:
                        act.wait_ge(mp_full, use[("route", t - 1)] + 1)
                    act.activation(h2t[:, 4 * c:4 * c + 4, :], mp[:, :].rearrange("p (h t) -> p h t", h=4),
                                   ACT.Copy).then_inc(h2t_done, 1)
                    act.wait_ge(h2t_done, 2 * t + c + 1)
                    act.sem_inc(mp_free, 1)

            for k in range(CT):
                act.wait_ge(raw_in[k], 16)
                if g == 0:
                    act.activation(wo_hi[:, k, :], raw[k], ACT.Copy).then_inc(wo_hi_done, 1)
                else:
                    act.activation(wo_hi[:, k, :], raw[k], ACT.Copy, scale=go[:, k:k + 1]).then_inc(wo_hi_done, 1)
            job(("k", 0))
            job(("q", 0))
            act.wait_ge(wo_lo_done, CT)
            for s, (t, i, last_step, unit, jobs, late_jobs) in enumerate(steps):
                for j in jobs:
                    job(j)
                if unit:
                    u = n_of[unit]
                    w = (unit[3] - unit[2]) * P
                    act.wait_ge(z_done, u + 1)
                    if u >= NB:
                        act.wait_ge(t_done, base[u - NB + 1])
                        act.wait_ge(edge_done, u - NB + 2)
                        act.wait_ge(scan_done, u - NB + 2)
                    act.activation(wgt[:, u % NB, 0:w], zp[:, u % 2, 0:w], ACT.Sigmoid, scale=SCALE)
                    act.activation(keep[:, u % NB, 0:w], zp[:, u % 2, 0:w], ACT.Sigmoid,
                                   scale=-SCALE).then_inc(sig_done, 1)
                if i == 3 and 0 <= t - 1 < NT:
                    act.wait_ge(av_done, end_half[t - 1])
                    if t >= 3:
                        act.wait_ge(o_done, t - 2)
                    act.activation(o_raw[:, (t - 1) % 2, :], op[:, 0:GC], ACT.Copy).then_inc(o_out, 1)
                if s >= 2 and steps[s - 2][3]:
                    copy_halves(act, n_of[steps[s - 2][3]], True)
                for j in late_jobs:
                    job(j)
                if last_step and g == 1 and 0 <= t - 2 < NT:
                    act.wait_ge(y_done, 2 * (t - 2) + 2)
                    if t >= 3:
                        act.wait_ge(rs_step, 2 * (t - 2))
                    if t >= 4:
                        act.wait_ge(st_h[t % 2], 16 * (t // 2 - 1))
                        act.wait_ge(mp_full, use[("h2t", t - 4, 1)] + 1)
                    act.activation(h2[:, t % 2, :], y[:, (t - 2) % 3, :], ACT.Square,
                                   accum_out=ss).then_inc(ss_done, 1)

        @block.vector
        def _(dve):
            dve.wait_ge(const_in, 16 * (2 if g == 0 else 4))

            def heads(ap):
                return ap.rearrange("p (h t) -> p h t", h=HG)

            def job(j):
                if j[0] == "k":
                    dve.wait_ge(k_hi_done, k_at[j[1]] + 1)
                    low = kt_sb[64:128, :, j[1] * P:(j[1] + 1) * P]
                    dve.tensor_tensor(low, heads(mp[64:128, :]), low.bitcast(F32), ALU.subtract).then_inc(k_done, 1)
                    dve.wait_ge(k_done, k_at[j[1]] + 1)
                elif j[0] == "q":
                    t = j[1]
                    dve.wait_ge(q_hi_done, t + 1)
                    dve.scalar_tensor_tensor(q_lo[:, t % 2, :, :].rearrange("p h t -> p (h t)"), mp[:, :], gq[:, 0:1],
                                             q_hi[:, t % 2, :, :].rearrange("p h t -> p (h t)").bitcast(F32),
                                             ALU.mult, ALU.subtract).then_inc(q_done, 1)
                    dve.wait_ge(q_done, t + 1)
                elif j[0] == "mix":
                    t = j[1]
                    dve.wait_ge(m_hi_done, t + 1)
                    dve.tensor_tensor(m_lo[:, t % 2, :, :], heads(mp[:, :]), m_hi[:, t % 2, :, :].bitcast(F32),
                                      ALU.subtract).then_inc(m_done, 1)
                    dve.wait_ge(m_done, t + 1)
                elif j[0] == "wo":
                    t, c = j[1], j[2]
                    dve.wait_ge(mp_full, use[j] + 1)
                    dve.wait_ge(y_in[t % 3], 16 * (t // 3 + 1))
                    dve.tensor_tensor(y[:, t % 3, c * C:(c + 1) * C], mp[:, :], y[:, t % 3, c * C:(c + 1) * C],
                                      ALU.add).then_inc(y_done, 1)
                    dve.wait_ge(y_done, 2 * t + c + 1)
                elif j[0] == "route":
                    t = j[1]
                    dve.wait_ge(mp_full, use[j] + 1)
                    dve.tensor_copy(logits[:, t, :], mp[:, 0:NR]).then_inc(lg_done, 1)
                    dve.wait_ge(lg_done, t + 1)
                else:
                    return
                dve.sem_inc(mp_free, 1)

            for k in range(CT):
                dve.wait_ge(wo_hi_done, k + 1)
                if g == 0:
                    dve.tensor_tensor(wo_lo[:, k, :], raw[k], wo_hi[:, k, :].bitcast(F32),
                                      ALU.subtract).then_inc(wo_lo_done, 1)
                else:
                    dve.scalar_tensor_tensor(wo_lo[:, k, :], raw[k], go[:, k:k + 1],
                                             wo_hi[:, k, :].bitcast(F32), ALU.mult, ALU.subtract).then_inc(wo_lo_done, 1)
            job(("k", 0))
            job(("q", 0))
            for s, (t, i, last_step, unit, jobs, late_jobs) in enumerate(steps):
                for j in jobs:
                    job(j)
                if unit:
                    u = n_of[unit]
                    w = (unit[3] - unit[2]) * P
                    dve.wait_ge(sig_done, u + 1)
                    dve.wait_ge(edge_done, u + 1)
                    part = keep[:, u % NB, w:0:-1]
                    if unit[4]:
                        dve.wait_ge(scan_done, u)
                    dve.tensor_tensor_scan(part, part, part, keep[:, (u - 1) % NB, 1:2] if unit[4] else 1.0,
                                           ALU.mult, ALU.bypass).then_inc(scan_done, 1)
                if s >= 2 and steps[s - 2][3]:
                    copy_halves(dve, n_of[steps[s - 2][3]], False)
                if i == 3 and 0 <= t - 1 < NT:
                    dve.wait_ge(o_sq_done, t)
                    if t >= 2:
                        dve.wait_ge(o_step, 2 * (t - 1))
                    dve.tensor_reduce(oms, o_sq[:, :].rearrange("p (h d) -> p h d", h=HG), AX.X,
                                      ALU.add).then_inc(o_ms, 1)
                for j in late_jobs:
                    job(j)

        @block.gpsimd
        def _(pool):
            pool.memset(ident[:, :], 0.0).then_inc(ready, 1)
            pool.memset(mask[:, :], 0.0).then_inc(ready, 1)
            pool.memset(mhalf[:, :], -0.5)
            pool.wait_ge(ready, 2)
            pool.affine_select(out=ident[:, :], in_=ident[:, :], compare_op=ALU.not_equal, fill=1.0, base=0,
                               pattern=[[-1, P]], channel_multiplier=1).then_inc(ready, 1)
            pool.affine_select(out=mask[:, :], in_=mask[:, :], compare_op=ALU.is_gt, fill=-1e30, base=0,
                               pattern=[[-1, P]], channel_multiplier=1).then_inc(ready, 1)
            pool.wait_ge(ready, 4)
            pool.tensor_copy(identb[:, :], ident[:, :]).then_inc(ready, 1)
            pool.wait_ge(ready, 5)

            def mix(t):
                pool.wait_ge(m_in[t % 2], 16 * (t // 2 + 1))
                if t >= 2:
                    pool.wait_ge(wo_done, 2 * t - 2)
                pool.tensor_copy(m_hi[:, t % 2, :, :], c_ld[:, t % 2, :, :]).then_inc(m_hi_done, 1)
                pool.wait_ge(m_hi_done, t + 1)
                pool.tensor_tensor(m_lo[:, t % 2, :, :], c_ld[:, t % 2, :, :], m_hi[:, t % 2, :, :].bitcast(F32),
                                   ALU.subtract).then_inc(m_done, 1)

            def edge(u):
                unit = units[u]
                w = (unit[3] - unit[2]) * P
                if u >= NB:
                    pool.wait_ge(a_done, u - NB + 1)
                if unit[4]:
                    pool.wait_ge(sig_done, u)
                    pool.tensor_copy(keep[:, u % NB, w:w + 1], keep[:, (u - 1) % NB, 0:1]).then_inc(edge_done, 1)
                else:
                    pool.memset(keep[:, u % NB, w:w + 1], 1.0).then_inc(edge_done, 1)

            pool.wait_ge(wo_lo_done, CT)
            edge(0)
            for s, (t, i, last_step, unit, jobs, late_jobs) in enumerate(steps):
                if g == 0 and i == 0 and t < NT:
                    mix(t)
                n = t - 1
                if i == 3 and 0 <= n < NT:
                    pool.wait_ge(o_out, t)
                    if n:
                        pool.wait_ge(o_ms, n)
                    pool.tensor_tensor(o_sq[:, :], o_raw[:, n % 2, :], o_raw[:, n % 2, :],
                                       ALU.mult).then_inc(o_sq_done, 1)
                if unit:
                    u = n_of[unit]
                    w = (unit[3] - unit[2]) * P
                    if u + 1 < len(units):
                        edge(u + 1)
                    pool.wait_ge(scan_done, u + 1)
                    pool.tensor_tensor(wgt[:, u % NB, 0:w], wgt[:, u % NB, 0:w], keep[:, u % NB, 1:w + 1],
                                       ALU.mult).then_inc(a_done, 1)
                if (i == 4 or i == 3 and last_step) and 0 <= n < NT:
                    pool.wait_ge(o_ms, t)
                    pool.tensor_scalar(ort, oms, 1.0 / HD, EPS, ALU.mult, ALU.add).then_inc(o_step, 1)
                    pool.wait_ge(o_step, 2 * n + 1)
                    if n:
                        pool.wait_ge(o_done, n)
                    pool.tensor_tensor(orr, ort, mhalf[:, :], ALU.pow).then_inc(o_step, 1)
                    pool.wait_ge(o_step, 2 * n + 2)
                    if n >= 4:
                        if g == 0:
                            pool.wait_ge(st_o[n % 4], 16 * (n // 4))
                        else:
                            pool.wait_ge(mp_full, use[("mix", n - 4)] + 1)
                    pool.tensor_tensor(o_n[:, n % 4, :].rearrange("p (h d) -> p h d", h=HG),
                                       o_raw[:, n % 2, :].rearrange("p (h d) -> p h d", h=HG),
                                       orr.unsqueeze(2).broadcast_to([P, HG, HD]), ALU.mult).then_inc(o_done, 1)
                n = t - 3
                if i == 0 and g == 1 and 0 <= n < NT:
                    pool.wait_ge(ss_done, n + 1)
                    if n:
                        pool.wait_ge(h2_step, n)
                    pool.tensor_scalar(rt, ss, 1.0 / D, EPS, ALU.mult, ALU.add).then_inc(rs_step, 1)
                    pool.wait_ge(rs_step, 2 * n + 1)
                    pool.tensor_tensor(rstd, rt, mhalf[:, 0:1], ALU.pow).then_inc(rs_step, 1)
                    pool.wait_ge(rs_step, 2 * n + 2)
                    pool.tensor_scalar(h2[:, n % 2, :], y[:, n % 3, :], rstd, None, ALU.mult).then_inc(h2_step, 1)
                    pool.wait_ge(h2_step, n + 1)
                    pool.tensor_tensor(h2[:, n % 2, :], h2[:, n % 2, :], g2[:, :], ALU.mult).then_inc(h2_done, 1)
    return sems


NG, NE = 4, 32
EG = NE // NG
FF = 512
FT = FF // P
HF = FF // 2
PIECES = 12
RING = 16
PAD = NT * P
NBL = NE + 2 * TOK // P + 3
BIG = 1e30


def phase_moe(nc, io, scr, logits):
    with ExitStack() as ctx:
        def sb(name, shape, dt=F32):
            return ctx.enter_context(nc.sbuf_tensor("p3_" + name, shape, dt))

        def ps(name, shape):
            return ctx.enter_context(nc.psum_tensor("p3_" + name, shape, F32))

        sems = []

        def sem(name):
            sems.append(nc.alloc_semaphore("p3_" + name))
            return sems[-1]

        BF = mybir.dt.bfloat16
        iota_i, iota = sb("iota_i", [P, P], I32), sb("iota", [P, P])
        gmax, gi, se, psel = (sb(x, [P, NT]) for x in ("gmax", "gi", "se", "psel"))
        gd, geq, ohg = (sb(x, [P, NT, NG]) for x in ("gd", "geq", "ohg"))
        m = sb("m", [P, NT, NE])
        t1 = sb("t1", [P, NT, NE])
        oh = [sb("oh1", [P, NT, NE]), sb("oh2", [P, NT, NE])]
        v = [sb("v1", [P, NT]), sb("v2", [P, NT])]
        ix = [sb("i1", [P, NT]), sb("i2", [P, NT])]
        wt = [sb("w1", [P, NT]), sb("w2", [P, NT])]
        ex = sb("ex", [P, NT])
        chosen = sb("chosen", [P, NT, NE], BF)
        before, ones = sb("before", [P, P], BF), sb("ones", [P, P], BF)
        cum = sb("cum", [P, NT + 1, NE])
        full = sb("full", [P, NT, NE])
        rk, rki, hi = sb("rk", [P, NT]), sb("rki", [P, NT], I32), sb("hi", [P, NT])
        tok_i, tok = sb("tok_i", [P, NT], I32), sb("tok", [P, NT])
        pad_i, pad = sb("pad_i", [P, 1], I32), sb("pad", [P, 1])
        row, col, val = ([sb(f"{x}{k}", [P, NT]) for k in (1, 2)] for x in ("row", "col", "val"))
        slot_f = sb("slot_f", [P, NBL])
        nb, nbi = sb("nb", [P, 2, NE]), sb("nbi", [P, NE], I32)
        table = sb("table", [1, 2, NE], I32)
        sel = sb("sel", [P, NT])

        w_hi, w_lo = sb("w_hi", [P, PIECES, 2 * FF], F32R), sb("w_lo", [P, PIECES, 2 * FF], F32R)
        raw = sb("raw", [P, RING, 2 * FF])
        slots = sb("slots", [P, NBL, 2], I32)
        xg = sb("xg", [P, D])
        in_row = xg[:, 0:3 * P].rearrange("p (n r) -> p n r", n=3)
        in_col = xg[:, 3 * P:3 * P + 6 * NBL].rearrange("p (n v b) -> p n v b", n=3, v=2)
        xt_hi, xt_lo = sb("xt_hi", [P, KT, P], F32R), sb("xt_lo", [P, KT, P], F32R)
        sg, h = sb("sg", [P, FF]), sb("h", [P, FF])
        ht_hi, ht_lo = sb("ht_hi", [P, FT, P], F32R), sb("ht_lo", [P, FT, P], F32R)
        yo = sb("yo", [P, D])
        at_g, at_s = sb("at_g", [P, 1], I32), sb("at_s", [P, 1], I32)
        ident = sb("ident", [P, P])

        xtp = ps("xtp", [P, KT, P])
        dp = ps("dp", [P, 2, 512])
        gp, up = ps("gp", [P, 2, 512]), ps("up", [P, FF])
        htp = ps("htp", [P, FT, P])
        rank_ps, count_ps = xtp[:, :, :].rearrange("p (a k) q -> p a (k q)", a=2), dp
        consts, chain, exped, act_in, chosen_in, chosen_done, ranked, spread_in = (
            sem(x) for x in ("consts", "chain", "exped", "act_in", "chosen_in", "chosen_done", "ranked", "spread_in"))
        spread, zeroed = sem("spread"), sem("zeroed")
        ident_done, zero_yo, ranks_used = sem("ident_done"), sem("zero_yo"), sem("ranks_used")
        at_g_done, at_s_done = sem("at_g_done"), sem("at_s_done")
        table_done, slots_done, passed = sem("table_done"), sem("slots_done"), sem("passed")
        raw_in = [sem(f"raw_in{i}") for i in range(RING)]
        whi_done, wlo_done = sem("whi_done"), sem("wlo_done")
        gathered, added = sem("gathered"), sem("added")
        xt_ps, xh_done, xl_done = sem("xt_ps"), sem("xh_done"), sem("xl_done")
        up_done, g_done, sg_done, h_done = (sem("up_done"), [sem("g_done0"), sem("g_done1")],
                                            [sem("sg_done0"), sem("sg_done1")], [sem("h_done0"), sem("h_done1")])
        ht_ps, hh_done, hl_done = ([sem(f"{x}{i}") for i in range(2)] for x in ("ht_ps", "hh_done", "hl_done"))
        gs_mid, gs_done = [sem("gs_mid0"), sem("gs_mid1")], [sem("gs_done0"), sem("gs_done1")]
        d_done, yo_done = sem("d_done"), sem("yo_done")

        choices = [(tile, k) for k in range(2) for tile in range(NT)]

        block = ctx.enter_context(nc.Block())

        def pieces(e):
            out = [io[src][bass.ds(e * D + q * 2 * P, 2 * P), :].rearrange("(k p) f -> p k f", p=P)
                   for src in ("w_up", "w_gate") for q in range(KT // 2)]
            return out + [io["w_down"][bass.ds(e * FF + k * P, P), :] for k in range(FT)]

        @block.sync
        def _(sp):
            def load(i, a):
                for p, src in enumerate(pieces(i * 4 + a)):
                    n = a * PIECES + p
                    if not (isinstance(i, int) and n < RING):
                        sp.wait_ge(wlo_done, i * (4 * PIECES) + n - RING + 1)
                    dst = raw[:, n % RING, :]
                    sp.dma_start(dst.rearrange("p (k f) -> p k f", k=2) if p < 2 * KT // 2 else dst,
                                 src).then_inc(raw_in[n % RING], 16)

            sp.wait_ge(consts, 7)
            sp.dma_start(scr["h2"][PAD:ROWS, :], yo[:, :]).then_inc(zeroed, 16)
            sp.dma_start(io["y_out"][PAD:ROWS, :], yo[:, :]).then_inc(zeroed, 16)
            for a in range(4):
                load(0, a)
            with sp.Fori(1, NE // 4) as i:
                for a in range(4):
                    load(i, a)
            sp.wait_ge(zeroed, 32)

        def experts(eng, block_of):
            with eng.Fori(0, NE // 4 - 1) as i:
                for a in range(4):
                    blocks(eng, i, a, block_of)
            for a in range(4):
                blocks(eng, NE // 4 - 1, a, block_of)

        def blocks(eng, i, a, block_of):
            e = i * 4 + a
            start, end = (eng.value_load(table[0:1, x, bass.ds(e, 1)], min_val=1, max_val=NBL - 2) for x in range(2))
            with eng.If(end > start):
                with eng.Fori(start, end) as b:
                    block_of(b, None)
            block_of(end, None if isinstance(e, int) and e == NE - 1 else (i, a + 1))

        @block.scalar
        def _(act):
            act.wait_ge(act_in, 1)
            act.activation(gd[:, :, :], gd[:, :, :], ACT.Exp).then_inc(exped, 1)
            def lead(at, lo, hi):
                if at is None:
                    return
                i, a = at
                for p in range(lo, hi):
                    n = a * PIECES + p
                    act.wait_ge(raw_in[n % RING], (i * (4 * PIECES // RING) + n // RING + 1) * 16)
                    act.activation(w_hi[:, p, :], raw[:, n % RING, :], ACT.Copy).then_inc(whi_done, 1)

            def x_hi(b):
                act.wait_ge(xt_ps, b + 1)
                act.activation(xt_hi[:, :, :], xtp[:, :, :], ACT.Copy).then_inc(xh_done, 1)

            def sigmoid(b, k):
                act.wait_ge(g_done[k], b + 1)
                act.wait_ge(gs_done[k], b)
                act.activation(sg[:, bass.ts(k, HF)], gp[:, k, 0:HF], ACT.Sigmoid).then_inc(sg_done[k], 1)

            def h_hi(b, k):
                act.wait_ge(ht_ps[k], b + 1)
                act.wait_ge(d_done, b)
                act.activation(ht_hi[:, 2 * k:2 * k + 2, :], htp[:, 2 * k:2 * k + 2, :], ACT.Copy).then_inc(hh_done[k], 1)

            def block_of(b, at):
                if at is not None:
                    act.wait_ge(up_done, b + 1)
                lead(at, 0, 1)
                sigmoid(b, 0)
                lead(at, 1, 3)
                sigmoid(b, 1)
                h_hi(b, 0)
                x_hi(b + 1)
                h_hi(b, 1)
                lead(at, 3, 6)
                act.wait_ge(d_done, b + 1)
                act.wait_ge(added, b * 16)
                act.activation(yo[:, :], dp[:, :, :].rearrange("p c f -> p (c f)"), ACT.Copy,
                               scale=slots[:, bass.ds(b, 1), 1].bitcast(F32)).then_inc(yo_done, 1)
                lead(at, 6, PIECES)

            for done in (xh_done, *sg_done, *hh_done):
                act.sem_inc(done, 1)
            act.wait_ge(zero_yo, 1)
            act.sem_inc(yo_done, 1)
            lead((0, 0), 0, 8)
            act.wait_ge(act_in, 2)
            act.activation(ex[:, :], ex[:, :], ACT.Exp).then_inc(exped, 1)
            lead((0, 0), 8, PIECES)
            x_hi(1)
            act.wait_ge(table_done, 1)
            act.wait_ge(slots_done, 1)
            experts(act, block_of)

        @block.tensor
        def _(pe):
            pe.wait_ge(chosen_done, 1)
            for dst, lhs in ((rank_ps, before), (count_ps, ones)):
                pe.matmul(dst[:, 0, :], lhs[:, :], chosen[:, 0:PT, :].rearrange("p t e -> p (t e)"),
                          start=True, stop=True)
                last = pe.matmul(dst[:, 1, 0:NE], lhs[:, :], chosen[:, PT, :], start=True, stop=True)
            last.then_inc(ranked, 1)
            for n, (tile, k) in enumerate(choices):
                m = P if tile < PT else DEC
                pe.wait_ge(spread_in, n + 1)
                pe.matmul(up[:, 0:2 * NBL], in_row[0:m, n % 3, :], in_col[0:m, n % 3, :, :].rearrange("p v b -> p (v b)"),
                          start=(n == 0), stop=(n == len(choices) - 1)).then_inc(spread, 1)

            def transpose_x(b):
                pe.wait_ge(gathered, b * 16)
                pe.wait_ge(xl_done, b)
                for k in range(KT):
                    last = pe.transpose(xtp[:, k, :], xg[:, k * P:(k + 1) * P], ident[:, :])
                last.then_inc(xt_ps, 1)

            def transpose_h(b, k):
                pe.wait_ge(h_done[k], b + 1)
                for f in (2 * k, 2 * k + 1):
                    last = pe.transpose(htp[:, f, :], h[:, f * P:(f + 1) * P], ident[:, :])
                last.then_inc(ht_ps[k], 1)

            def weights(e, groups):
                pe.wait_ge(whi_done, e * PIECES + groups * 4)
                pe.wait_ge(wlo_done, e * PIECES + groups * 4)

            def half_down(c, k, start):
                n = 0
                for f in (2 * k, 2 * k + 1):
                    for ha, wa in ((ht_hi, w_hi), (ht_hi, w_lo), (ht_lo, w_hi)):
                        last = pe.matmul(dp[:, c, :], ha[:, f, :], wa[:, KT + f, c * 512:(c + 1) * 512],
                                         start=(start and n == 0), stop=(not start and n == 5))
                        n += 1
                return last

            def hidden(dst, group, lo, hi):
                n = 0
                for k in range(KT):
                    for xa, wa in ((xt_hi, w_hi), (xt_hi, w_lo), (xt_lo, w_hi)):
                        piece, at = group * (KT // 2) + k // 2, k % 2 * FF
                        last = pe.matmul(dst, xa[:, k, :], wa[:, piece, at + lo:at + hi],
                                         start=(n == 0), stop=(n == 3 * KT - 1))
                        n += 1
                return last

            for done in (xt_ps, up_done, *g_done, *ht_ps, d_done):
                pe.sem_inc(done, 1)
            pe.wait_ge(zero_yo, 1)
            pe.wait_ge(ranks_used, 1)
            transpose_x(1)
            pe.wait_ge(table_done, 1)
            with pe.Fori(0, NE) as e:
                start, end = (pe.value_load(table[0:1, x, bass.ds(e, 1)], min_val=1, max_val=NBL - 2) for x in range(2))
                with pe.Fori(start, end + 1) as b:
                    pe.wait_ge(xh_done, b + 1)
                    pe.wait_ge(xl_done, b + 1)
                    weights(e, 1)
                    pe.wait_ge(h_done[1], b)
                    hidden(up[:, :], 0, 0, FF).then_inc(up_done, 1)
                    weights(e, 2)
                    hidden(gp[:, 0, 0:HF], 1, 0, HF).then_inc(g_done[0], 1)
                    hidden(gp[:, 1, 0:HF], 1, HF, FF).then_inc(g_done[1], 1)
                    pe.wait_ge(hl_done[1], b)
                    transpose_h(b, 0)
                    transpose_x(b + 1)
                    weights(e, 3)
                    pe.wait_ge(hl_done[0], b + 1)
                    pe.wait_ge(yo_done, b)
                    half_down(0, 0, True)
                    transpose_h(b, 1)
                    half_down(1, 0, True)
                    pe.wait_ge(hl_done[1], b + 1)
                    half_down(0, 1, False)
                    half_down(1, 1, False).then_inc(d_done, 1)

        @block.vector
        def _(dve):
            links = [0]

            def link(ins):
                links[0] += 1
                ins.then_inc(chain, 1)
                dve.wait_ge(chain, links[0])

            def tt(out, a, b, op):
                link(dve.tensor_tensor(out, a, b, op))

            def over(ap, n):
                return ap.unsqueeze(2).broadcast_to([P, NT, n])

            def tiled(ap, n):
                return ap.unsqueeze(1).broadcast_to([P, NT, n])

            def first_max(values, n, best, index, one_hot):
                link(dve.tensor_reduce(best, values, AX.X, ALU.max))
                tt(one_hot, values, over(best, n), ALU.is_equal)
                link(dve.scalar_tensor_tensor(one_hot, one_hot, -100.0, tiled(iota[:, 0:n], n), ALU.mult, ALU.add))
                link(dve.tensor_reduce(index, one_hot, AX.X, ALU.min))
                tt(one_hot, one_hot, over(index, n), ALU.is_equal)

            lg, le = logits[:, :, 0:NG], logits[:, :, NG:NR]
            dve.wait_ge(consts, 7)
            link(dve.tensor_copy(iota[:, :], iota_i[:, :]))
            link(dve.tensor_copy(tok[:, :], tok_i[:, :]))
            link(dve.tensor_copy(pad[:, :], pad_i[:, :]))
            first_max(lg, NG, gmax[:, :], gi[:, :], ohg[:, :, :])
            tt(gd[:, :, :], lg, over(gmax[:, :], NG), ALU.subtract)
            dve.sem_inc(act_in, 1)
            dve.wait_ge(exped, 1)
            link(dve.tensor_reduce(se[:, :], gd[:, :, :], AX.X, ALU.add))
            link(dve.reciprocal(psel[:, :], se[:, :]))
            by_group = m[:, :, :].rearrange("p t (g e) -> p t g e", g=NG)
            for tile in range(NT):
                last = dve.tensor_tensor(by_group[:, tile], le[:, tile, :].rearrange("p (g e) -> p g e", g=NG),
                                         ohg[:, tile, :].unsqueeze(2).broadcast_to([P, NG, EG]), ALU.mult)
            link(last)
            link(dve.tensor_scalar(geq[:, :, :], ohg[:, :, :], BIG, -BIG, ALU.mult, ALU.add))
            for tile in range(NT):
                last = dve.tensor_tensor(by_group[:, tile], by_group[:, tile],
                                         geq[:, tile, :].unsqueeze(2).broadcast_to([P, NG, EG]), ALU.add)
            link(last)
            first_max(m[:, :, :], NE, v[0][:, :], ix[0][:, :], oh[0][:, :, :])
            link(dve.scalar_tensor_tensor(m[:, :, :], oh[0][:, :, :], -2 * BIG, m[:, :, :], ALU.mult, ALU.add))
            first_max(m[:, :, :], NE, v[1][:, :], ix[1][:, :], oh[1][:, :, :])
            tt(chosen[:, :, :], oh[0][:, :, :], oh[1][:, :, :], ALU.add)
            dve.sem_inc(chosen_in, 1)
            tt(ex[:, :], v[1][:, :], v[0][:, :], ALU.subtract)
            dve.sem_inc(act_in, 1)
            dve.wait_ge(exped, 2)
            link(dve.tensor_scalar_add(v[0][:, :], ex[:, :], 1.0))
            link(dve.reciprocal(v[1][:, :], v[0][:, :]))
            tt(wt[0][:, :], v[1][:, :], psel[:, :], ALU.mult)
            tt(wt[1][:, :], wt[0][:, :], ex[:, :], ALU.mult)
            dve.wait_ge(ranked, 1)
            link(dve.memset(cum[:, 0, :], 0.0))
            for tile in range(NT):
                tt(cum[:, tile + 1, :], cum[:, tile, :],
                   count_ps[:, tile // PT, tile % PT * NE:tile % PT * NE + NE], ALU.add)
            tt(full[:, 0:PT, :], cum[:, 0:PT, :], rank_ps[:, 0, :].rearrange("p (t e) -> p t e", e=NE), ALU.add)
            tt(full[:, PT, :], cum[:, PT, :], rank_ps[:, 1, 0:NE], ALU.add)
            dve.sem_inc(ranks_used, 1)
            link(dve.tensor_scalar(nb[:, 0, :], cum[:, NT, :], float(P - 1), None, ALU.add))
            link(dve.tensor_copy(nbi[:, :], nb[:, 0, :]))
            link(dve.tensor_scalar(nbi[:, :], nbi[:, :], 7, None, ALU.logical_shift_right))
            link(dve.tensor_scalar(nbi[:, :], nbi[:, :], 1, None, ALU.max))
            link(dve.tensor_copy(nb[:, 0, :], nbi[:, :]))
            link(dve.tensor_tensor_scan(nb[:, 1, :], nb[:, 0, :], nb[:, 0, :], 1.0, ALU.add, ALU.bypass))
            tt(nb[:, 1, :], nb[:, 1, :], nb[:, 0, :], ALU.subtract)
            link(dve.tensor_copy(table[0:1, 0, :], nb[0:1, 1, :]))
            link(dve.scalar_tensor_tensor(nb[0:1, 0, :], nb[0:1, 0, :], -1.0, nb[0:1, 1, :], ALU.add, ALU.add))
            link(dve.tensor_copy(table[0:1, 1, :], nb[0:1, 0, :]))
            dve.sem_inc(table_done, 1)
            for k in range(2):
                tt(t1[:, :, :], oh[k][:, :, :], full[:, :, :], ALU.mult)
                link(dve.tensor_reduce(rk[:, :], t1[:, :, :], AX.X, ALU.add))
                link(dve.tensor_copy(rki[:, :], rk[:, :]))
                link(dve.tensor_scalar(rki[:, :], rki[:, :], 7, None, ALU.logical_shift_right))
                link(dve.tensor_copy(hi[:, :], rki[:, :]))
                link(dve.scalar_tensor_tensor(row[k][:, :], hi[:, :], -float(P), rk[:, :], ALU.mult, ALU.add))
                tt(t1[:, :, :], oh[k][:, :, :], tiled(nb[:, 1, :], NE), ALU.mult)
                link(dve.tensor_reduce(sel[:, :], t1[:, :, :], AX.X, ALU.add))
                tt(col[k][:, :], hi[:, :], sel[:, :], ALU.add)
                tt(val[k][:, :], tok[:, :], row[k][:, :], ALU.subtract)
            for n, (tile, k) in enumerate(choices):
                if n >= 3:
                    dve.wait_ge(spread, n - 2)
                dve.tensor_scalar(in_row[:, n % 3, :], iota[:, :], row[k][:, tile:tile + 1], None, ALU.is_equal)
                for x, of in enumerate((val[k], wt[k])):
                    last = dve.tensor_scalar(in_col[:, n % 3, x, :], iota[:, 0:NBL], col[k][:, tile:tile + 1],
                                             of[:, tile:tile + 1], ALU.is_equal, ALU.mult)
                last.then_inc(spread_in, 1)
            dve.wait_ge(spread, len(choices))
            link(dve.tensor_scalar(slot_f[:, :], up[:, 0:NBL], pad[:, 0:1], None, ALU.add))
            link(dve.tensor_copy(slots[:, :, 1].bitcast(F32), up[:, NBL:2 * NBL]))
            link(dve.tensor_copy(slots[:, :, 0], slot_f[:, :]))
            dve.sem_inc(slots_done, 1)

            def rest(at, lo, hi):
                if at is None:
                    return
                i, a = at
                for p in range(lo, hi):
                    n = a * PIECES + p
                    dve.wait_ge(whi_done, i * (4 * PIECES) + n + 1)
                    dve.tensor_tensor(w_lo[:, p, :], raw[:, n % RING, :], w_hi[:, p, :].bitcast(F32),
                                      ALU.subtract).then_inc(wlo_done, 1)

            def x_rest(b):
                dve.wait_ge(xh_done, b + 1)
                dve.tensor_tensor(xt_lo[:, :, :], xtp[:, :, :], xt_hi[:, :, :].bitcast(F32),
                                  ALU.subtract).then_inc(xl_done, 1)

            def silu(b, k):
                cols = bass.ts(k, HF)
                dve.wait_ge(sg_done[k], b + 1)
                dve.tensor_tensor(sg[:, cols], gp[:, k, 0:HF], sg[:, cols], ALU.mult).then_inc(gs_mid[k], 1)
                dve.wait_ge(gs_mid[k], b + 1)
                dve.wait_ge(ht_ps[k], b)
                dve.tensor_tensor(h[:, cols], up[:, cols], sg[:, cols], ALU.mult).then_inc(h_done[k], 1)
                dve.wait_ge(h_done[k], b + 1)
                dve.sem_inc(gs_done[k], 1)

            def h_rest(b, k):
                dve.wait_ge(hh_done[k], b + 1)
                dve.tensor_tensor(ht_lo[:, 2 * k:2 * k + 2, :], htp[:, 2 * k:2 * k + 2, :],
                                  ht_hi[:, 2 * k:2 * k + 2, :].bitcast(F32), ALU.subtract).then_inc(hl_done[k], 1)

            def block_of(b, at):
                rest(at, 0, 1)
                silu(b, 0)
                rest(at, 1, 2)
                h_rest(b, 0)
                silu(b, 1)
                x_rest(b + 1)
                h_rest(b, 1)
                rest(at, 2, PIECES)

            for done in (xl_done, *gs_mid, *gs_done, *h_done, *hl_done):
                dve.sem_inc(done, 1)
            x_rest(1)
            experts(dve, block_of)

        @block.gpsimd
        def _(pool):
            pool.iota(iota_i[:, :], pattern=[[1, P]], base=0, channel_multiplier=0).then_inc(consts, 1)
            pool.iota(tok_i[:, :], pattern=[[P, NT]], base=-PAD, channel_multiplier=1).then_inc(consts, 1)
            pool.iota(pad_i[:, :], pattern=[[0, 1]], base=PAD, channel_multiplier=1).then_inc(consts, 1)
            pool.memset(yo[:, :], 0.0).then_inc(consts, 1)
            pool.memset(ones[:, :], 1.0).then_inc(consts, 1)
            pool.memset(before[:, :], 1.0).then_inc(consts, 1)
            pool.memset(ident[:, :], 0.0).then_inc(ident_done, 1)
            pool.wait_ge(ident_done, 1)
            pool.affine_select(out=ident[:, :], in_=ident[:, :], compare_op=ALU.not_equal, fill=1.0, base=0,
                               pattern=[[-1, P]], channel_multiplier=1).then_inc(ident_done, 1)
            pool.wait_ge(ident_done, 2)
            pool.wait_ge(consts, 6)
            pool.sem_inc(zero_yo, 1)
            pool.affine_select(out=before[:, :], in_=before[:, :], compare_op=ALU.is_gt, fill=0.0, base=0,
                               pattern=[[1, P]], channel_multiplier=-1).then_inc(consts, 1)
            pool.wait_ge(consts, 7)

            def rest_of_first(lo, hi):
                for p in range(lo, hi):
                    pool.wait_ge(whi_done, p + 1)
                    pool.tensor_tensor(w_lo[:, p, :], raw[:, p, :], w_hi[:, p, :].bitcast(F32),
                                       ALU.subtract).then_inc(wlo_done, 1)

            rest_of_first(0, 4)
            pool.wait_ge(chosen_in, 1)
            pool.affine_select(out=chosen[:, PT, :], in_=chosen[:, PT, :], compare_op=ALU.is_ge, fill=0.0,
                               base=DEC - 1, pattern=[[0, NE]], channel_multiplier=-1).then_inc(chosen_done, 1)
            rest_of_first(4, PIECES)
            pool.wait_ge(slots_done, 1)

            def gather(b):
                hold(pool, xt_ps, b, passed)
                pool.tensor_copy(at_g[:, :], slots[:, bass.ds(b, 1), 0]).then_inc(at_g_done, 1)
                hold(pool, at_g_done, b, passed)
                pool.indirect_dma_start(out=xg[:, :], out_offset=None, in_=scr["h2"],
                                        in_offset=bass.IndirectOffsetOnAxis(ap=at_g[:, 0:1], axis=0)
                                        ).then_inc(gathered, 16)

            def add(b):
                if not isinstance(b, int):
                    hold(pool, added, b * 16, passed)
                pool.tensor_copy(at_s[:, :], slots[:, bass.ds(b, 1), 0]).then_inc(at_s_done, 1)
                hold(pool, at_s_done, b + 1, passed)
                hold(pool, yo_done, b + 1, passed)
                pool.indirect_dma_start(out=io["y_out"], out_offset=bass.IndirectOffsetOnAxis(ap=at_s[:, 0:1], axis=0),
                                        in_=yo[:, :], in_offset=None, compute_op=ALU.add).then_inc(added, 16)

            pool.wait_ge(zeroed, 32)
            gather(1)
            pool.wait_ge(table_done, 1)
            end = pool.value_load(table[0:1, 1, NE - 1:NE], min_val=NE, max_val=NBL - 2)
            gather(2)
            add(0)
            with pool.Fori(1, end) as b:
                gather(b + 2)
                add(b)
            add(end)
            hold(pool, added, end * 16 + 16, passed)
            hold(pool, gathered, end * 16 + 16, passed)
    return sems


def build(nc, io):
    scr = {
        "q": nc.dram_tensor("scr_q", [NT * P, C], F32, kind=SCRATCH).ap(),
        "c": nc.dram_tensor("scr_c", [P, CT, NT * P], F32, kind=SCRATCH).ap(),
        "o": nc.dram_tensor("scr_o", [NT * P, GC], F32, kind=SCRATCH).ap(),
        "y": nc.dram_tensor("scr_y", [NT * P, D], F32, kind=SCRATCH).ap(),
        "h2": nc.dram_tensor("scr_h2", [ROWS, D], F32, kind=SCRATCH).ap(),
    }

    def phase_ends(sems):
        nc.clear_and_free_semaphores(sems)
        nc.all_engine_barrier()

    phase_ends(phase_project(nc, io, scr))
    with nc.sbuf_tensor("logits", [P, NT, NR], F32) as logits:
        for g in range(2):
            phase_ends(phase_attend(nc, io, scr, g, logits))
        phase_ends(phase_moe(nc, io, scr, logits))


def kernel(**inputs):
    import concourse.bacc as bacc
    import numpy as np
    from concourse.bass_utils import run_bass_kernel_spmd

    def cols(v, n):
        return np.ascontiguousarray(v.reshape(n, P).T)

    a = {k: np.asarray(v) for k, v in inputs.items()}
    x = np.zeros((ROWS, D), a["x_prompt"].dtype)
    x[:SEQ], x[SEQ:TOK] = a["x_prompt"][0], a["x_sample"][0]
    router = np.concatenate([a["w_router_group"][0], a["w_router_expert"][0]], axis=1)
    arrays = {
        "x": x,
        "norm_mix_g": cols(a["norm_mix_g"][0], KT),
        "w_in": a["w_in"][0],
        "k_norm_g": a["k_norm_g"][0],
        "q_norm_g": np.ascontiguousarray(np.concatenate([a["q_norm_g"][0]] * 2)[:, None]),
        "conv_w": np.ascontiguousarray(a["conv_w"][0].reshape(W, CT, P).transpose(2, 1, 0)),
        "conv_b": cols(a["conv_b"][0], CT),
        "conv_ln_g": cols(a["conv_ln_g"][0], CT),
        "conv_ln_b": cols(a["conv_ln_b"][0], CT),
        "cache_conv": a["cache_conv"][0, 0],
        "cache_k": a["cache_k"][0, 0].reshape(PAST, C),
        "cache_v": a["cache_v"][0, 0].reshape(PAST, C),
        "attn_out_g": cols(a["attn_out_g"][0].reshape(-1), CT),
        "norm_ffn_g": a["norm_ffn_g"][0],
        "w_out": a["w_out"][0],
        "w_router": np.ascontiguousarray(router.reshape(KT, P, NR).transpose(1, 0, 2)),
        "w_gate": a["w_exp_gate"][0].reshape(NE * D, FF),
        "w_up": a["w_exp_up"][0].reshape(NE * D, FF),
        "w_down": a["w_exp_down"][0].reshape(NE * FF, D),
    }
    arrays = {"in_" + k: np.ascontiguousarray(v) for k, v in arrays.items()}

    nc = bacc.Bacc("TRN2", target_bir_lowering=False, num_devices=1)
    io = {k[3:]: nc.dram_tensor(k, list(v.shape), F32, kind="ExternalInput").ap() for k, v in arrays.items()}
    for name in ("k_out", "v_out", "u_out"):
        io[name] = nc.dram_tensor(name, [NT * P, C], F32, kind="ExternalOutput").ap()
    io["y_out"] = nc.dram_tensor("y_out", [ROWS, D], F32, kind="ExternalOutput").ap()
    build(nc, io)
    got = run_bass_kernel_spmd(nc, [arrays], core_ids=[0]).results[0]

    y, k, v, u = (got[name] for name in ("y_out", "k_out", "v_out", "u_out"))
    k, v = k.reshape(-1, NH, HD), v.reshape(-1, NH, HD)
    return (y[None, :SEQ], y[None, SEQ:TOK], k[None, None, :SEQ], v[None, None, :SEQ],
            u[None, None, SEQ - HIST:SEQ], k[None, None, SEQ:TOK], v[None, None, SEQ:TOK],
            u[None, None, TOK - HIST:TOK])
```
